# Optimizing a Trainium2 kernel written in Bass

```python
import jax, jax.numpy as jnp
from jax import lax
import numpy as np

D_MODEL = 1024
BATCH = 1
SEQ = 2048
DEPTH = 2
DEC_BATCH = 8
DEC_SEQ = 16
PAST_LEN = 256

CHUNK = 64
WINDOW = 128
WINDOW_CHUNKS = WINDOW // CHUNK
N_A_LAYERS = DEPTH // 2
N_B_LAYERS = DEPTH - N_A_LAYERS
A_HEAD_DIM = 64
A_HEADS = D_MODEL // A_HEAD_DIM
A_DECAY_RANK = 64
A_ICLR_RANK = 64
B_HEAD_DIM = 64
B_HEADS = D_MODEL // B_HEAD_DIM
B_KV_HEADS = 4
B_GROUP = B_HEADS // B_KV_HEADS
B_WIDTH = B_HEADS * B_HEAD_DIM
PLE_DIM = 256
DEEPNORM_ALPHA = (2.0 * DEPTH) ** 0.25
DEEPNORM_BETA = (8.0 * DEPTH) ** -0.25
LN_EPS = 1e-5
GN_EPS = 64e-5
NEG_INF = -1e30

kernel_name = "yoco_rwkv7_swa_sink_stream_step"

def _layer_norm(x, g, b, eps=LN_EPS):
    xf = x.astype(jnp.float32)
    mu = jnp.mean(xf, -1, keepdims=True)
    var = jnp.mean(jnp.square(xf - mu), -1, keepdims=True)
    return ((xf - mu) * lax.rsqrt(var + eps) * g + b).astype(x.dtype)

def _rwkv7_mixer(x, shift0, wkv0, mu, w_in, w0, w_w1, w_w2, a0, w_a1, w_a2, k_k, k_a, r_k, gn_g, gn_b, w_out):
    bsz, t_len, _ = x.shape
    xprev = jnp.concatenate([shift0[:, None, :].astype(x.dtype), x[:, :-1]], axis=1)
    dx = xprev - x
    xr, xw, xk, xv, xa, xg = (x + dx * mu[j] for j in range(6))
    r = xr @ w_in[0]
    k = xk @ w_in[1]
    v = xv @ w_in[2]
    gate = jax.nn.silu(xg @ w_in[3])
    w_log = -jax.nn.softplus(-(w0 + jnp.tanh(xw @ w_w1) @ w_w2)) - 0.5
    decay = jnp.exp(-jnp.exp(w_log.astype(jnp.float32)))
    a = jax.nn.sigmoid(a0 + (xa @ w_a1) @ w_a2)

    def heads(z):
        return z.reshape(bsz, t_len, A_HEADS, A_HEAD_DIM).astype(jnp.float32)

    kk = heads(k * k_k)
    kk = kk / jnp.maximum(jnp.sqrt(jnp.sum(kk * kk, -1, keepdims=True)), 1e-12)
    k = k * (1.0 + (a - 1.0) * k_a)
    r_h, k_h, v_h, a_h, w_h = heads(r), heads(k), heads(v), heads(a), heads(decay)

    def step(S, inp):
        r_t, w_t, k_t, v_t, kk_t, a_t = inp
        sa = jnp.einsum('bhvk,bhk->bhv', S, -kk_t)
        S = (S * w_t[:, :, None, :] + sa[..., None] * (kk_t * a_t)[:, :, None, :]
             + v_t[..., None] * k_t[:, :, None, :])
        return S, jnp.einsum('bhvk,bhk->bhv', S, r_t)

    def tm(z):
        return jnp.swapaxes(z, 0, 1)

    s_fin, o = lax.scan(step, wkv0.astype(jnp.float32),
                        (tm(r_h), tm(w_h), tm(k_h), tm(v_h), tm(kk), tm(a_h)))
    o = tm(o)
    mean = jnp.mean(o, -1, keepdims=True)
    var = jnp.mean(jnp.square(o - mean), -1, keepdims=True)
    o = ((o - mean) * lax.rsqrt(var + GN_EPS)).reshape(bsz, t_len, D_MODEL) * gn_g + gn_b
    bonus = (jnp.sum(r_h * k_h * r_k, -1, keepdims=True) * v_h).reshape(bsz, t_len, D_MODEL)
    out = ((o + bonus).astype(x.dtype) * gate) @ w_out
    return out, x[:, -1], s_fin

def _alibi_bias(dist):
    slopes = 2.0 ** (-8.0 * jnp.arange(1, B_HEADS + 1, dtype=jnp.float32) / B_HEADS)
    return -slopes.reshape(B_KV_HEADS, B_GROUP)[:, :, None, None] * dist

def _sink_softmax(s, sinks):
    sk = sinks.astype(jnp.float32).reshape(B_KV_HEADS, B_GROUP)[:, :, None, None]
    m = jnp.maximum(jnp.max(s, -1, keepdims=True), sk)
    e = jnp.exp(s - m)
    return e / (jnp.sum(e, -1, keepdims=True) + jnp.exp(sk - m))

def _band_attention_prompt(q, k, v, sinks):
    bsz, s_len = q.shape[:2]
    n_chunks = s_len // CHUNK
    pad = WINDOW_CHUNKS * CHUNK
    kb_len = (WINDOW_CHUNKS + 1) * CHUNK
    qb = q.reshape(bsz, n_chunks, CHUNK, B_KV_HEADS, B_GROUP, B_HEAD_DIM).astype(jnp.float32)

    def blocks(z):
        zp = jnp.pad(z, ((0, 0), (pad, 0), (0, 0), (0, 0)))
        zp = zp.reshape(bsz, n_chunks + WINDOW_CHUNKS, CHUNK, B_KV_HEADS, B_HEAD_DIM)
        return jnp.concatenate([zp[:, j:j + n_chunks] for j in range(WINDOW_CHUNKS + 1)], axis=2)

    kb = blocks(k).astype(jnp.float32)
    vb = blocks(v)
    q_off = jnp.arange(CHUNK)
    k_off = jnp.arange(kb_len) - pad
    bias = _alibi_bias(jnp.abs(q_off[:, None] - k_off[None, :]).astype(jnp.float32))
    valid = (jnp.arange(n_chunks)[:, None] * CHUNK + k_off[None, :]) >= 0
    s = jnp.einsum('bcqkgd,bcjkd->bckgqj', qb, kb) * (B_HEAD_DIM ** -0.5) + bias
    s = jnp.where(valid[None, :, None, None, None, :], s, NEG_INF)
    p = _sink_softmax(s, sinks)
    o = jnp.einsum('bckgqj,bcjkd->bcqkgd', p.astype(vb.dtype), vb)
    return o.reshape(bsz, s_len, B_WIDTH)

def _band_attention_sample(q, k_new, v_new, k_cache, v_cache, sinks):
    bsz, t_len = q.shape[:2]
    r_len = k_cache.shape[1]
    kk = jnp.concatenate([k_cache.astype(k_new.dtype), k_new], axis=1)
    vv = jnp.concatenate([v_cache.astype(v_new.dtype), v_new], axis=1)
    qh = q.reshape(bsz, t_len, B_KV_HEADS, B_GROUP, B_HEAD_DIM).astype(jnp.float32)
    dist = jnp.abs(jnp.arange(t_len)[:, None] + r_len - jnp.arange(r_len + t_len)[None, :]).astype(jnp.float32)
    s = jnp.einsum('bqkgd,bjkd->bkgqj', qh, kk.astype(jnp.float32)) * (B_HEAD_DIM ** -0.5) + _alibi_bias(dist)
    p = _sink_softmax(s, sinks)
    o = jnp.einsum('bkgqj,bjkd->bqkgd', p.astype(vv.dtype), vv)
    return o.reshape(bsz, t_len, B_WIDTH)

def _swa_mixer(x, k, v, k_cache, v_cache, w_in, sinks, w_out):
    bsz, t_len, _ = x.shape
    qg = x @ w_in
    q = qg[..., :B_WIDTH].reshape(bsz, t_len, B_HEADS, B_HEAD_DIM)
    gate = jax.nn.silu(qg[..., B_WIDTH:])
    if k_cache is None:
        o = _band_attention_prompt(q, k, v, sinks)
    else:
        o = _band_attention_sample(q, k, v, k_cache, v_cache, sinks)
    return (o.astype(x.dtype) * gate) @ w_out

def _shared_kv(x, g, b, w_kv):
    bsz, t_len, _ = x.shape
    kv = (_layer_norm(x, g, b) @ w_kv).reshape(bsz, t_len, 2, B_KV_HEADS, B_HEAD_DIM)
    return kv[:, :, 0], kv[:, :, 1]

def _trunk(x, p, shift0, wkv0, k_cache, v_cache,
           a_mu, a_w_in, a_w0, a_w_w1, a_w_w2, a_a0, a_w_a1, a_w_a2, a_k_k, a_k_a, a_r_k,
           a_gn_g, a_gn_b, a_w_out, kv_ln_g, kv_ln_b, w_kv, b_w_in, b_sinks, b_w_out,
           ln_g, ln_b, ple_w_proj, ple_w_gate):
    new_shift, new_wkv = [], []
    k = v = None
    for i in range(DEPTH):
        if i < N_A_LAYERS:
            h, sh, st = _rwkv7_mixer(x, shift0[i], wkv0[i], a_mu[i], a_w_in[i], a_w0[i], a_w_w1[i], a_w_w2[i],
                                     a_a0[i], a_w_a1[i], a_w_a2[i], a_k_k[i], a_k_a[i], a_r_k[i],
                                     a_gn_g[i], a_gn_b[i], a_w_out[i])
            new_shift.append(sh)
            new_wkv.append(st)
        else:
            if i == N_A_LAYERS:
                k, v = _shared_kv(x, kv_ln_g, kv_ln_b, w_kv)
            j = i - N_A_LAYERS
            h = _swa_mixer(x, k, v, k_cache, v_cache, b_w_in[j], b_sinks[j], b_w_out[j])
        x = _layer_norm(DEEPNORM_ALPHA * x + h, ln_g[i], ln_b[i])
        x = x + jax.nn.sigmoid(x @ ple_w_gate[i]) * (p[i] @ ple_w_proj[i])
    return x, jnp.stack(new_shift), jnp.stack(new_wkv), k, v

def setup_inputs(seed: int = 0) -> dict:
    key = jax.random.key(seed)
    ks = iter(jax.random.split(key, 40))
    f32 = jnp.float32

    def nrm(shape, scale=1.0):
        return scale * jax.random.normal(next(ks), shape, f32)

    def uni(shape, lo, hi):
        return jax.random.uniform(next(ks), shape, f32, minval=lo, maxval=hi)

    cache_rows = min(WINDOW, PAST_LEN)
    d = D_MODEL
    return {
        "x_prompt": nrm((BATCH, SEQ, d)),
        "x_sample": nrm((DEC_BATCH, DEC_SEQ, d)),
        "p_prompt": nrm((DEPTH, BATCH, SEQ, PLE_DIM)),
        "p_sample": nrm((DEPTH, DEC_BATCH, DEC_SEQ, PLE_DIM)),
        "state_a_shift": nrm((N_A_LAYERS, DEC_BATCH, d)),
        "state_a_wkv": nrm((N_A_LAYERS, DEC_BATCH, A_HEADS, A_HEAD_DIM, A_HEAD_DIM), 0.1),
        "cache_k": nrm((DEC_BATCH, cache_rows, B_KV_HEADS, B_HEAD_DIM)),
        "cache_v": nrm((DEC_BATCH, cache_rows, B_KV_HEADS, B_HEAD_DIM)),
        "a_mu": uni((N_A_LAYERS, 6, d), 0.0, 1.0),
        "a_w_in": nrm((N_A_LAYERS, 4, d, d), d ** -0.5),
        "a_w0": uni((N_A_LAYERS, d), -6.0, -1.0),
        "a_w_w1": nrm((N_A_LAYERS, d, A_DECAY_RANK), d ** -0.5),
        "a_w_w2": nrm((N_A_LAYERS, A_DECAY_RANK, d), 0.1 * A_DECAY_RANK ** -0.5),
        "a_a0": nrm((N_A_LAYERS, d), 0.1),
        "a_w_a1": nrm((N_A_LAYERS, d, A_ICLR_RANK), d ** -0.5),
        "a_w_a2": nrm((N_A_LAYERS, A_ICLR_RANK, d), 0.1 * A_ICLR_RANK ** -0.5),
        "a_k_k": 0.85 + nrm((N_A_LAYERS, d), 0.05),
        "a_k_a": 1.0 + nrm((N_A_LAYERS, d), 0.05),
        "a_r_k": nrm((N_A_LAYERS, A_HEADS, A_HEAD_DIM), 0.1),
        "a_gn_g": 1.0 + nrm((N_A_LAYERS, d), 0.05),
        "a_gn_b": nrm((N_A_LAYERS, d), 0.01),
        "a_w_out": nrm((N_A_LAYERS, d, d), DEEPNORM_BETA * d ** -0.5),
        "kv_ln_g": 1.0 + nrm((d,), 0.05),
        "kv_ln_b": nrm((d,), 0.01),
        "w_kv": nrm((d, 2 * B_KV_HEADS * B_HEAD_DIM), d ** -0.5),
        "b_w_in": nrm((N_B_LAYERS, d, 2 * B_WIDTH), d ** -0.5),
        "b_sinks": nrm((N_B_LAYERS, B_HEADS), 0.5),
        "b_w_out": nrm((N_B_LAYERS, B_WIDTH, d), DEEPNORM_BETA * B_WIDTH ** -0.5),
        "ln_g": 1.0 + nrm((DEPTH, d), 0.05),
        "ln_b": nrm((DEPTH, d), 0.01),
        "ple_w_proj": nrm((DEPTH, PLE_DIM, d), PLE_DIM ** -0.5),
        "ple_w_gate": nrm((DEPTH, d, d), d ** -0.5),
    }

def reference(x_prompt, x_sample, p_prompt, p_sample, state_a_shift, state_a_wkv, cache_k, cache_v,
              a_mu, a_w_in, a_w0, a_w_w1, a_w_w2, a_a0, a_w_a1, a_w_a2, a_k_k, a_k_a, a_r_k,
              a_gn_g, a_gn_b, a_w_out, kv_ln_g, kv_ln_b, w_kv, b_w_in, b_sinks, b_w_out,
              ln_g, ln_b, ple_w_proj, ple_w_gate):
    weights = (a_mu, a_w_in, a_w0, a_w_w1, a_w_w2, a_a0, a_w_a1, a_w_a2, a_k_k, a_k_a, a_r_k,
               a_gn_g, a_gn_b, a_w_out, kv_ln_g, kv_ln_b, w_kv, b_w_in, b_sinks, b_w_out,
               ln_g, ln_b, ple_w_proj, ple_w_gate)
    bsz = x_prompt.shape[0]
    shift_zero = jnp.zeros((N_A_LAYERS, bsz, D_MODEL), x_prompt.dtype)
    wkv_zero = jnp.zeros((N_A_LAYERS, bsz, A_HEADS, A_HEAD_DIM, A_HEAD_DIM), jnp.float32)
    y_prompt, prompt_shift, prompt_wkv, k_p, v_p = _trunk(
        x_prompt, p_prompt, shift_zero, wkv_zero, None, None, *weights)
    keep = min(WINDOW, x_prompt.shape[1])
    prompt_k = k_p[:, -keep:]
    prompt_v = v_p[:, -keep:]
    y_sample, sample_shift, sample_wkv, sample_k, sample_v = _trunk(
        x_sample, p_sample, state_a_shift, state_a_wkv, cache_k, cache_v, *weights)
    return (y_prompt, y_sample, prompt_shift, prompt_wkv, prompt_k, prompt_v,
            sample_shift, sample_wkv, sample_k, sample_v)


_drawn_inputs = setup_inputs


def setup_inputs(seed=0):
    import zlib

    import numpy as np

    out = dict(_drawn_inputs(seed))
    spreads = {}
    factors = {'cache_k': 2.757,
     'a_w_w1': 8.0,
     'a_w_w2': 8.0,
     'a_gn_g': 7.634,
     'a_gn_b': 63.193,
     'kv_ln_b': 5.667,
     'b_sinks': 28.436,
     'ln_b': 4.48,
     'a_r_k': 2.852}
    for name, (base, spread) in spreads.items():
        noise = np.random.default_rng([zlib.crc32(name.encode()), seed]).standard_normal(out[name].shape)
        drawn = base * np.exp(spread * noise) if base else spread * noise
        out[name] = __import__('jax').numpy.asarray(drawn.astype(out[name].dtype))
    for name, factor in factors.items():
        out[name] = (out[name] * factor).astype(out[name].dtype)
    return out
```

```python
from contextlib import ExitStack

import concourse.bass as bass
from concourse import mybir

F32 = mybir.dt.float32
ALU = mybir.AluOpType
ACT = mybir.ActivationFunctionType
X = mybir.AxisListType.X

P = 128
D = 1024
NB = D // P
HALF = D // 2
HB = NB // 2
HD = 64
NH = D // HD
HH = NH // 2
RANK = 64
PLE = 256
DEC = 8
DSEQ = 16
ALPHA = (2.0 * 2) ** 0.25
LN_EPS = 1e-5
GN_EPS = 64e-5
DECAY = -(2.718281828459045 ** -0.5)


def wait(eng, sem, value):
    if isinstance(value, int) and value <= 0:
        return
    eng.wait_ge(sem, value)


def tiles(eng, prompt_tiles, step):
    pairs = prompt_tiles // 2
    step(0, 0)
    step(1, 1)
    if pairs > 2:
        with eng.Fori(1, pairs - 1) as p:
            step(p * 2, 0)
            step(p * 2 + 1, 1)
    step(prompt_tiles - 2, 0)
    step(prompt_tiles - 1, 1)
    step(prompt_tiles, 0)


def of_parity(t, par, each):
    return t // 2 * each if isinstance(t, int) else (t - par) * (each // 2)


def is_sample(t, prompt_tiles):
    return isinstance(t, int) and t == prompt_tiles


def rows(t):
    return bass.ds(t * P, P) if not isinstance(t, int) else slice(t * P, t * P + P)


def tile_of(t):
    return bass.ds(t, 1) if not isinstance(t, int) else slice(t, t + 1)


class Masks:

    NAMES = ["ident", "cum_incl", "cum_excl", "incl", "strict", "neg_lower",
             "s_cum_incl", "s_cum_excl", "s_incl", "s_strict", "s_neg_lower", "same",
             "lev1", "lev2", "lev4", "lev8", "lev16", "lev32", "lev64", "lev1T"]

    def __init__(self, nc, ctx):
        self.all = ctx.enter_context(nc.sbuf_tensor("masks", [P, len(self.NAMES), P], F32))
        self.totals = ctx.enter_context(nc.sbuf_tensor("totals", [P, 2], F32))
        self.seq_rows = ctx.enter_context(nc.sbuf_tensor("seq_rows", [P, DEC], F32))

    def __getitem__(self, name):
        return self.all[:, self.NAMES.index(name), :]


def build_masks(nc, m):
    made = ExitStack()
    with made:
        order = made.enter_context(nc.semaphore("mask_order"))
        made.callback(clear_semaphores, nc, [order])
        block = made.enter_context(nc.Block())

        @block.gpsimd
        def _(pool):
            count = [0]

            def link(ins):
                count[0] += 1
                ins.then_inc(order, 1)
                pool.wait_ge(order, count[0])

            def keep(view, op, base, row, pattern, fill=0.0):
                link(nc.gpsimd.affine_select(out=view, in_=view, compare_op=op, fill=fill, base=base,
                                             pattern=pattern, channel_multiplier=row))

            def within(view, size):
                return [[-size, view.shape[1]]] + [[0, n] for n in view.shape[2:]]

            link(nc.gpsimd.memset(m.all[:, :, :], 1.0))
            link(nc.gpsimd.memset(m.totals[:, :], 1.0))
            link(nc.gpsimd.memset(m.seq_rows[:, :], 1.0))
            line = [[1, P]]
            keep(m["ident"], ALU.is_equal, 0, -1, line)
            for name in ("same", "s_incl", "s_strict", "s_cum_incl", "s_cum_excl", "s_neg_lower"):
                v = m[name].rearrange("p (g i) -> p g i", i=DSEQ)
                keep(v, ALU.is_ge, 0, 1, within(v, DSEQ))
                keep(v, ALU.is_ge, DSEQ - 1, -1, [[DSEQ, DEC], [0, DSEQ]])
            for name in ("incl", "cum_incl", "s_incl", "s_cum_incl"):
                keep(m[name], ALU.is_ge, 0, -1, line)
            for name in ("strict", "cum_excl", "s_strict", "s_cum_excl"):
                keep(m[name], ALU.is_gt, 0, -1, line)
            for name in ("neg_lower", "s_neg_lower"):
                keep(m[name], ALU.is_gt, 0, 1, [[-1, P]])
                link(nc.gpsimd.tensor_scalar(m[name], m[name], -1.0, 0.0, ALU.mult, ALU.add))
            for name in ("cum_incl", "cum_excl"):
                link(nc.gpsimd.tensor_scalar(m[name][0:64, :], m[name][0:64, :], -1.0, 0.0, ALU.add, ALU.add))
            keep(m.totals[:, 0:1], ALU.is_ge, 63, -1, [[0, 1]])
            keep(m.totals[:, 1:2], ALU.is_ge, -64, 1, [[0, 1]])
            keep(m.seq_rows[:, :], ALU.is_ge, 0, 1, [[-DSEQ, DEC]])
            keep(m.seq_rows[:, :], ALU.is_ge, DSEQ - 1, -1, [[DSEQ, DEC]])
            for b in (1, 2, 4, 8, 16, 32, 64):
                v = m[f"lev{b}"].rearrange("p (g h i) -> p g h i", h=2, i=b)
                link(nc.gpsimd.memset(v[:, :, 0, :], 0.0))
                n = P // (2 * b)
                keep(v[:, :, 1, :], ALU.is_ge, 0, 1, [[-2 * b, n], [0, b]])
                keep(v[:, :, 1, :], ALU.is_ge, b - 1, -1, [[2 * b, n], [0, b]])
                link(nc.gpsimd.tensor_tensor(m[f"lev{b}"], m[f"lev{b}"], m["ident"], ALU.add))
            v = m["lev1T"].rearrange("p (g h) -> p g h", h=2)
            link(nc.gpsimd.memset(v[:, :, 1], 0.0))
            keep(v[:, :, 0], ALU.is_equal, -1, 1, [[-2, P // 2]])
            link(nc.gpsimd.tensor_tensor(m["lev1T"], m["lev1T"], m["ident"], ALU.add))


def clear_semaphores(nc, sems):
    block = nc.Block()
    with block:

        @block.gpsimd
        def _(pool):
            for s in sems:
                pool.sem_clear(s)


def gemm(nc, out, xT, w, cols, first_wait=None):
    n = w.shape[1]
    for j in range(n):
        last = nc.tensor.matmul(out, xT[:, j, :], w[:, j, cols], start=(j == 0), stop=(j == n - 1))
    return last


def load_previous_rows(nc, eng, t, sample, x_rows, x_sample, shift, dst, sem):
    if sample:
        eng.dma_start(dst[0:P:DSEQ, :], shift[0]).then_inc(sem, 16)
        for b in range(DEC):
            eng.dma_start(dst[b * DSEQ + 1:(b + 1) * DSEQ, :], x_sample[b, 0:DSEQ - 1, :]).then_inc(sem, 16)
    elif isinstance(t, int) and t == 0:
        eng.dma_start(dst[1:P, :], x_rows[0:P - 1, :]).then_inc(sem, 16)
    else:
        start = t * P - 1
        src = x_rows[start:start + P, :] if isinstance(t, int) else x_rows[bass.ds(start, P), :]
        eng.dma_start(dst[:, :], src).then_inc(sem, 16)


SAMPLE_LOADS = 2 + DEC


def phase_a1(nc, m, io, T):
    with ExitStack() as ctx:
        def sb(name, shape):
            return ctx.enter_context(nc.sbuf_tensor("a1_" + name, shape, F32))

        sems = []

        def sem(name):
            sems.append(ctx.enter_context(nc.semaphore("a1_" + name)))
            return sems[-1]

        wr, wk = sb("wr", [P, NB, D]), sb("wk", [P, NB, D])
        w1, a1 = sb("w1", [P, NB, RANK]), sb("a1", [P, NB, RANK])
        w2, a2 = sb("w2", [RANK + 1, D]), sb("a2", [RANK + 1, D])
        par = sb("par", [P, 3, D])
        mu_rows, mu = sb("mu_rows", [6 * NB, P]), sb("mu", [P, 6, NB])
        x, dx = sb("x", [P, D]), sb("dx", [P, D])
        xT, dT = sb("xT", [P, NB, P]), sb("dT", [P, NB, P])
        mix_w, mix_a = sb("mix_w", [P, NB, P]), sb("mix_a", [P, NB, P])
        mix_r = [sb(f"mix_r{i}", [P, NB, P]) for i in range(2)]
        mix_k = [sb(f"mix_k{i}", [P, NB, P]) for i in range(2)]
        hid_w, hid_a = sb("hid_w", [RANK + 1, P]), sb("hid_a", [RANK + 1, P])
        twice = lambda name, n=HALF: [sb(f"{name}{i}", [P, n]) for i in range(2)]
        ta, ks, ep, em, ee = (twice(n) for n in ("ta", "ks", "ep", "em", "ee"))
        at, bh, kh, rt = (twice(n) for n in ("at", "bh", "kh", "rt"))
        bonus = twice("bonus", HH)
        dec = [sb(f"dec{i}", [P, HB, DEC]) for i in range(2)]
        tw, kku, sq, kkn, am, kp, rk = (sb(n, [P, HALF]) for n in ("tw", "kku", "sq", "kkn", "am", "kp", "rk"))
        ss, rn, one = sb("ss", [P, HH]), sb("rn", [P, HH]), sb("one", [P, 1])
        stage = [sb(f"stage{i}", [P, HB, P]) for i in range(4)]

        bank = lambda name: ctx.enter_context(nc.psum_tensor("a1_" + name, [P, 512], F32))
        pzw, pza, pk, pr, pcum, plow, pin, pout = (
            bank(n) for n in ("pzw", "pza", "pk", "pr", "pcum", "plow", "pin", "pout"))

        w_loaded, small_loaded, x_loaded = sem("w_loaded"), sem("small_loaded"), sem("x_loaded")
        ready0 = sem("ready0")
        mixwa_mid = sem("mixwa_mid")
        mu_filled, mu_ready = sem("mu_filled"), sem("mu_ready")
        dx_ready = sem("dx_ready")
        in_filled, in_taken = sem("in_filled"), sem("in_taken")
        mixwa_ready, mixr_ready, mixk_ready = sem("mixwa_ready"), sem("mixr_ready"), sem("mixk_ready")
        low_filled, low_taken = sem("low_filled"), sem("low_taken")
        zw_filled, za_filled, k_filled, r_filled = (sem(n + "_filled") for n in ("zw", "za", "k", "r"))
        tw_ready, sg_ready, ta_ready, ks_ready = (sem(n + "_ready") for n in ("tw", "sg", "ta", "ks"))
        li_filled, le_filled = sem("li_filled"), sem("le_filled")
        em_ready, ee_ready = sem("em_ready"), sem("ee_ready")
        kku_ready, sq_ready, ss_ready, norm_ready = (sem(n + "_ready") for n in ("kku", "sq", "ss", "norm"))
        am_ready, x1_ready, kp_ready = (sem(n + "_ready") for n in ("am", "x1", "kp"))
        clip_ready, rn_ready, kkn_ready, bb_ready = (sem(n + "_ready") for n in ("clip", "rn", "kkn", "bb"))
        bh_ready, kh_ready, rt_ready, rk_ready = (sem(n + "_ready") for n in ("bh", "kh", "rt", "rk"))
        rkr_ready, bonus_ready, at_ready = sem("rkr_ready"), sem("bonus_ready"), sem("at_ready")
        out_filled, out_staged = sem("out_filled"), sem("out_staged")
        stage_stored = [sem(f"stage_stored{i}") for i in range(4)]
        tok_stored = [sem(f"tok_stored{i}") for i in range(2)]
        shift_stored = sem("shift_stored")
        last_tile = T

        def low_uses(kind, t):
            if kind == "lora":
                return 0 if isinstance(t, int) and t == 0 else t * 3 - 1
            last = isinstance(t, int) and t == last_tile
            return t * 3 + 1 if kind == "tot0" else t * 3 + (2 if last else 3)

        def loads_of(t):
            return t * 32 + (16 * SAMPLE_LOADS if is_sample(t, T) else 32)

        ctx.callback(clear_semaphores, nc, sems)
        block = ctx.enter_context(nc.Block())

        @block.sync
        def _(sp):
            sp.dma_start(mu_rows[:, :], io["a_mu"][0].rearrange("m (j p) -> (m j) p", p=P)).then_inc(small_loaded, 16)
            sp.dma_start(w1[:, :, :], io["a_w_w1"][0].rearrange("(j p) r -> p j r", p=P)).then_inc(small_loaded, 16)
            sp.dma_start(a1[:, :, :], io["a_w_a1"][0].rearrange("(j p) r -> p j r", p=P)).then_inc(small_loaded, 16)
            sp.dma_start(w2[0:RANK, :], io["a_w_w2"][0]).then_inc(small_loaded, 16)
            sp.dma_start(w2[RANK:RANK + 1, :], io["a_w0"]).then_inc(small_loaded, 16)
            sp.dma_start(a2[0:RANK, :], io["a_w_a2"][0]).then_inc(small_loaded, 16)
            sp.dma_start(a2[RANK:RANK + 1, :], io["a_a0"]).then_inc(small_loaded, 16)

            def load_x(t):
                wait(sp, in_filled, t * 4)
                src = io["x_sample"].rearrange("b i d -> (b i) d") if is_sample(t, T) else io["x_prompt"][0][rows(t), :]
                sp.dma_start(x[:, :], src).then_inc(x_loaded, 16)
                if isinstance(t, int) and t == 0:
                    sp.wait_ge(ready0, 1)
                load_previous_rows(nc, sp, t, is_sample(t, T), io["x_prompt"][0], io["x_sample"],
                                   io["state_a_shift"], dx, x_loaded)

            load_x(0)
            wk_v = io["a_w_in"][0, 1].rearrange("(j p) n -> p j n", p=P)
            wr_v = io["a_w_in"][0, 0].rearrange("(j p) n -> p j n", p=P)
            for src, dst in ((wk_v, wk), (wr_v, wr)):
                for h in range(2):
                    sp.dma_start(dst[:, :, h * HALF:(h + 1) * HALF], src[:, :, h * HALF:(h + 1) * HALF]).then_inc(w_loaded, 16)
            for i, name in enumerate(("a_k_k", "a_k_a")):
                sp.dma_start(par[:, i, :], io[name].to_broadcast([P, D])).then_inc(w_loaded, 16)
            sp.dma_start(par[:, 2, :], io["a_r_k"][0].rearrange("(o h) n -> o (h n)", o=1).to_broadcast([P, D])).then_inc(w_loaded, 16)

            def store_unit(t, h):
                u = t * 2 + h
                cols = slice(h * HALF, (h + 1) * HALF)
                sp.wait_ge(bh_ready, u + 1)
                sp.dma_start(io["tok_b"][rows(t), cols], bh[h][:, :]).then_inc(tok_stored[h], 16)
                sp.wait_ge(kh_ready, u + 1)
                sp.dma_start(io["tok_k"][rows(t), cols], kh[h][:, :]).then_inc(tok_stored[h], 16)
                sp.wait_ge(bonus_ready, u + 1)
                sp.dma_start(io["bonus"][rows(t), h * HH:(h + 1) * HH], bonus[h][:, :]).then_inc(tok_stored[h], 16)
                sp.wait_ge(low_taken, low_uses(f"tot{h}", t) + 1)
                sp.dma_start(io["dec"][rows(t), h * HB:(h + 1) * HB, :], dec[h][:, :, :]).then_inc(tok_stored[h], 16)
                for g in range(4):
                    sp.wait_ge(out_staged, u * 4 + (g + 1))
                    sp.dma_start(io["factors"][rows(t), g, h * HB:(h + 1) * HB, :], stage[g][:, :, :]).then_inc(stage_stored[g], 16)

            def step(t, par_):
                if not is_sample(t, T):
                    load_x(t + 1)
                if not (isinstance(t, int) and t == 0):
                    store_unit(t - 1, 1)
                store_unit(t, 0)

            sp.dma_start(io["prompt_shift"][0], io["x_prompt"][0][T * P - 1:T * P, :]).then_inc(shift_stored, 16)
            sp.dma_start(io["sample_shift"][0], io["x_sample"][:, DSEQ - 1, :]).then_inc(shift_stored, 16)
            tiles(sp, T, step)
            store_unit(T, 1)
            sp.wait_ge(shift_stored, 32)
            for h in range(2):
                sp.wait_ge(tok_stored[h], 64 * (T + 1))
            for g in range(4):
                sp.wait_ge(stage_stored[g], 32 * (T + 1))

        @block.tensor
        def _(pe):
            pe.wait_ge(small_loaded, 16 * 7)
            nc.tensor.transpose(plow[:, 0:6 * NB], mu_rows[:, :], m["ident"][0:6 * NB, 0:6 * NB]).then_inc(mu_filled, 1)

            def turn_in(t, g):
                if g == 0:
                    pe.wait_ge(x_loaded, loads_of(t))
                if g == 1:
                    pe.wait_ge(dx_ready, t + 1)
                wait(pe, in_taken, t * 4 + g)
                src = x if g % 2 == 0 else dx
                for i in range(HB):
                    j = (g // 2) * HB + i
                    last = nc.tensor.transpose(pin[:, i * P:(i + 1) * P], src[:, j * P:(j + 1) * P], m["ident"])
                last.then_inc(in_filled, 1)

            def lora(t):
                pe.wait_ge(mixwa_ready, t * 2 + 2)
                if isinstance(t, int) and t == 0:
                    pe.wait_ge(mu_ready, 1)
                wait(pe, low_taken, low_uses("lora", t))
                for i, (w, mix) in enumerate(((w1, mix_w), (a1, mix_a))):
                    for j in range(NB):
                        last = nc.tensor.matmul(plow[0:RANK, i * P:(i + 1) * P], w[:, j, :], mix[:, j, :],
                                                start=(j == 0), stop=(j == NB - 1))
                last.then_inc(low_filled, 1)

            def turn_out(t, h, g):
                u = t * 2 + h
                src, ready = ((kh, kh_ready), (rt, rt_ready), (bh, bh_ready), (at, at_ready))[g]
                pe.wait_ge(ready, u + 1)
                wait(pe, out_staged, u * 4 + g)
                for i in range(HB):
                    last = nc.tensor.transpose(pout[:, i * P:(i + 1) * P], src[h][:, i * P:(i + 1) * P], m["ident"])
                last.then_inc(out_filled, 1)

            def unit(t, par_, h):
                u = t * 2 + h
                first = isinstance(t, int) and t == 0 and h == 0
                cols = slice(h * HALF, (h + 1) * HALF)
                prev = (t - 1, 1) if h == 0 else (t, 0)
                sample = is_sample(t, T)
                pe.wait_ge(low_taken, low_uses("lora", t) + 1)
                wait(pe, tw_ready, u)
                nc.tensor.matmul(pzw[:, :], hid_w[:, :], w2[:, cols], start=True, stop=True).then_inc(zw_filled, 1)
                if not first:
                    turn_out(*prev, 0)
                if h == 0 and not sample:
                    turn_in(t + 1, 0)
                wait(pe, ta_ready, u)
                nc.tensor.matmul(pza[:, :], hid_a[:, :], a2[:, cols], start=True, stop=True).then_inc(za_filled, 1)
                if not first:
                    turn_out(*prev, 1)
                if h == 0 and not sample:
                    turn_in(t + 1, 1)
                if first:
                    pe.wait_ge(w_loaded, 16 * 7)
                pe.wait_ge(mixk_ready, t + 1)
                wait(pe, ks_ready, u)
                gemm(nc, pk[:, :], mix_k[par_], wk, cols).then_inc(k_filled, 1)
                if not first:
                    turn_out(*prev, 2)
                if h == 0 and not sample:
                    turn_in(t + 1, 2)
                pe.wait_ge(sg_ready, u + 1)
                wait(pe, ee_ready, u)
                nc.tensor.matmul(pcum[:, :], m["s_cum_incl" if sample else "cum_incl"], tw[:, :],
                                 start=True, stop=True).then_inc(li_filled, 1)
                pe.wait_ge(mixr_ready, t + 1)
                wait(pe, rt_ready, u)
                wait(pe, rk_ready, u)
                gemm(nc, pr[:, :], mix_r[par_], wr, cols).then_inc(r_filled, 1)
                if not first:
                    turn_out(*prev, 3)
                if h == 0 and not sample:
                    turn_in(t + 1, 3)
                pe.wait_ge(em_ready, u + 1)
                nc.tensor.matmul(pcum[:, :], m["s_cum_excl" if sample else "cum_excl"], tw[:, :],
                                 start=True, stop=True).then_inc(le_filled, 1)
                if h == 1 and not sample:
                    lora(t + 1)
                wait(pe, low_taken, low_uses("tot0" if h == 0 else "tot1", t))
                n = DEC if sample else 2
                for i in range(HB):
                    last = nc.tensor.matmul(plow[:, 256 + i * n:256 + (i + 1) * n], tw[:, i * P:(i + 1) * P],
                                            m.seq_rows[:, :] if sample else m.totals[:, :], start=True, stop=True)
                last.then_inc(low_filled, 1)

            for g in range(4):
                turn_in(0, g)
            lora(0)
            tiles(pe, T, lambda t, par_: (unit(t, par_, 0), unit(t, par_, 1)))
            for g in range(4):
                turn_out(T, 1, g)

        @block.scalar
        def _(act):
            act.wait_ge(mu_filled, 1)
            nc.scalar.copy(mu[:, :, :].rearrange("p m j -> p (m j)"), plow[:, 0:6 * NB]).then_inc(mu_ready, 1)

            def take_in(t, g):
                act.wait_ge(in_filled, t * 4 + (g + 1))
                if g == 0:
                    wait(act, mixwa_ready, t * 2)
                    wait(act, mixr_ready, t)
                dst = xT if g % 2 == 0 else dT
                half = slice((g // 2) * HB, (g // 2 + 1) * HB)
                nc.scalar.copy(dst[:, half, :].rearrange("p j t -> p (j t)"), pin[:, :]).then_inc(in_taken, 1)

            def take_hidden(t):
                act.wait_ge(low_filled, low_uses("lora", t) + 1)
                if isinstance(t, int) and t == 0:
                    act.wait_ge(ready0, 6)
                nc.scalar.activation(hid_w[0:RANK, :], plow[0:RANK, 0:P], ACT.Tanh)
                nc.scalar.copy(hid_a[0:RANK, :], plow[0:RANK, P:2 * P]).then_inc(low_taken, 1)

            def take_out(t, h, g):
                u = t * 2 + h
                act.wait_ge(out_filled, u * 4 + (g + 1))
                wait(act, stage_stored[g], u * 16)
                nc.scalar.copy(stage[g][:, :, :].rearrange("p j t -> p (j t)"), pout[:, :]).then_inc(out_staged, 1)

            def unit(t, h):
                u = t * 2 + h
                first = isinstance(t, int) and t == 0 and h == 0
                prev = (t - 1, 1) if h == 0 else (t, 0)
                sample = is_sample(t, T)
                act.wait_ge(zw_filled, u + 1)
                nc.scalar.activation(tw[:, :], pzw[:, :], ACT.Tanh, scale=0.5).then_inc(tw_ready, 1)
                if not first:
                    take_out(*prev, 0)
                if h == 0 and not sample:
                    take_in(t + 1, 0)
                act.wait_ge(za_filled, u + 1)
                wait(act, bb_ready, u - 1)
                nc.scalar.activation(ta[h][:, :], pza[:, :], ACT.Tanh, scale=0.5).then_inc(ta_ready, 1)
                if not first:
                    take_out(*prev, 1)
                if h == 0 and not sample:
                    take_in(t + 1, 1)
                act.wait_ge(k_filled, u + 1)
                wait(act, kp_ready, u - 1)
                nc.scalar.copy(ks[h][:, :], pk[:, :]).then_inc(ks_ready, 1)
                if not first:
                    take_out(*prev, 2)
                if h == 0 and not sample:
                    take_in(t + 1, 2)
                act.wait_ge(li_filled, u + 1)
                wait(act, rt_ready, u - 1)
                nc.scalar.activation(ep[h][:, :], pcum[:, :], ACT.Exp, scale=DECAY / 2)
                wait(act, kh_ready, u - 1)
                nc.scalar.activation(em[h][:, :], pcum[:, :], ACT.Exp, scale=-DECAY / 2).then_inc(em_ready, 1)
                if not first:
                    take_out(*prev, 3)
                if h == 0 and not sample:
                    take_in(t + 1, 3)
                act.wait_ge(le_filled, u + 1)
                wait(act, at_ready, u - 1)
                nc.scalar.activation(ee[h][:, :], pcum[:, :], ACT.Exp, scale=DECAY / 2).then_inc(ee_ready, 1)
                if h == 1 and not sample:
                    take_hidden(t + 1)
                n = DEC if sample else 2
                act.wait_ge(low_filled, low_uses("tot0" if h == 0 else "tot1", t) + 1)
                wait(act, tok_stored[h], t * 64)
                nc.scalar.activation(dec[h][:, :, 0:n], plow[:, 256:256 + HB * n].rearrange("p (j n) -> p j n", n=n),
                                     ACT.Exp, scale=DECAY / 2).then_inc(low_taken, 1)
                act.wait_ge(ss_ready, u + 1)
                nc.scalar.activation(ss[:, :], ss[:, :], ACT.Sqrt).then_inc(norm_ready, 1)

            for g in range(4):
                take_in(0, g)
            take_hidden(0)
            tiles(act, T, lambda t, par_: (unit(t, 0), unit(t, 1)))
            for g in range(4):
                take_out(T, 1, g)

        @block.gpsimd
        def _(pool):
            def mix_wa(t):
                pool.wait_ge(in_taken, t * 4 + 4)
                wait(pool, low_filled, low_uses("lora", t - 1) + 1 if not isinstance(t, int) or t > 0 else 0)
                for i, (dst, row) in enumerate(((mix_w, 1), (mix_a, 4))):
                    s = mu[:, row, :].unsqueeze(2).to_broadcast([P, NB, P])
                    nc.gpsimd.tensor_tensor(dst[:, :, :], dT[:, :, :], s, ALU.mult).then_inc(mixwa_mid, 1)
                    pool.wait_ge(mixwa_mid, t * 2 + (i + 1))
                    nc.gpsimd.tensor_tensor(dst[:, :, :], dst[:, :, :], xT[:, :, :], ALU.add).then_inc(mixwa_ready, 1)

            def unit(t, h):
                u = t * 2 + h
                pool.wait_ge(tw_ready, u + 1)
                nc.gpsimd.tensor_tensor(tw[:, :], tw[:, :], one[:, :].to_broadcast([P, HALF]), ALU.add).then_inc(sg_ready, 1)
                if h == 1 and not is_sample(t, T):
                    mix_wa(t + 1)
                pool.wait_ge(x1_ready, u + 1)
                wait(pool, rk_ready, u)
                wait(pool, kh_ready, u)
                nc.gpsimd.tensor_tensor(kp[:, :], sq[:, :], ks[h][:, :], ALU.add).then_inc(kp_ready, 1)
                pool.wait_ge(rk_ready, u + 1)
                nc.gpsimd.tensor_tensor(rk[:, :], rk[:, :], par[:, 2, h * HALF:(h + 1) * HALF], ALU.mult).then_inc(rkr_ready, 1)

            pool.wait_ge(mu_ready, 1)
            mix_wa(0)
            pool.wait_ge(ready0, 6)
            pool.wait_ge(w_loaded, 16 * 7)
            tiles(pool, T, lambda t, par_: (unit(t, 0), unit(t, 1)))

        @block.vector
        def _(dve):
            def make_dx(t):
                dve.wait_ge(x_loaded, loads_of(t))
                nc.vector.tensor_tensor(dx[:, :], dx[:, :], x[:, :], ALU.subtract).then_inc(dx_ready, 1)

            def mix_rk(t, par_):
                dve.wait_ge(in_taken, t * 4 + 4)
                wait(dve, r_filled, t * 2 - 2)
                for dst, row, ready in ((mix_k[par_], 2, mixk_ready), (mix_r[par_], 0, mixr_ready)):
                    for j in range(NB):
                        last = nc.vector.scalar_tensor_tensor(out=dst[:, j, :], in0=dT[:, j, :], scalar=mu[:, row, j:j + 1],
                                                              in1=xT[:, j, :], op0=ALU.mult, op1=ALU.add)
                    last.then_inc(ready, 1)

            def heads(ap):
                return ap.rearrange("p (h n) -> p h n", n=HD)

            def unit(t, par_, h):
                u = t * 2 + h
                cols = slice(h * HALF, (h + 1) * HALF)
                sample = is_sample(t, T)
                if h == 0 and not sample:
                    make_dx(t + 1)
                dve.wait_ge(ks_ready, u + 1)
                wait(dve, bb_ready, u)
                nc.vector.tensor_tensor(kku[:, :], ks[h][:, :], par[:, 0, cols], ALU.mult).then_inc(kku_ready, 1)
                wait(dve, kp_ready, u)
                dve.wait_ge(kku_ready, u + 1)
                nc.vector.tensor_tensor(sq[:, :], kku[:, :], kku[:, :], ALU.mult).then_inc(sq_ready, 1)
                dve.wait_ge(sq_ready, u + 1)
                wait(dve, clip_ready, u)
                nc.vector.tensor_reduce(ss[:, :], heads(sq[:, :]), X, ALU.add).then_inc(ss_ready, 1)
                if h == 1 and not sample:
                    mix_rk(t + 1, 1 - par_)
                dve.wait_ge(ta_ready, u + 1)
                wait(dve, x1_ready, u)
                nc.vector.scalar_tensor_tensor(out=am[:, :], in0=ta[h][:, :], scalar=1.0, in1=par[:, 1, cols],
                                               op0=ALU.subtract, op1=ALU.mult).then_inc(am_ready, 1)
                dve.wait_ge(am_ready, u + 1)
                dve.wait_ge(ss_ready, u + 1)
                nc.vector.scalar_tensor_tensor(out=sq[:, :], in0=am[:, :], scalar=0.5, in1=ks[h][:, :],
                                               op0=ALU.mult, op1=ALU.mult).then_inc(x1_ready, 1)
                dve.wait_ge(norm_ready, u + 1)
                wait(dve, kkn_ready, u)
                nc.vector.tensor_scalar(rn[:, :], ss[:, :], 1e-12, None, ALU.max).then_inc(clip_ready, 1)
                dve.wait_ge(clip_ready, u + 1)
                nc.vector.reciprocal(rn[:, :], rn[:, :]).then_inc(rn_ready, 1)
                dve.wait_ge(rn_ready, u + 1)
                wait(dve, at_ready, u)
                nc.vector.tensor_tensor(heads(kkn[:, :]), heads(kku[:, :]),
                                        rn[:, :].unsqueeze(2).to_broadcast([P, HH, HD]), ALU.mult).then_inc(kkn_ready, 1)
                dve.wait_ge(kkn_ready, u + 1)
                nc.vector.scalar_tensor_tensor(out=kku[:, :], in0=ta[h][:, :], scalar=1.0, in1=kkn[:, :],
                                               op0=ALU.add, op1=ALU.mult).then_inc(bb_ready, 1)
                dve.wait_ge(bb_ready, u + 1)
                dve.wait_ge(em_ready, u + 1)
                wait(dve, out_filled, (u - 1) * 4)
                wait(dve, tok_stored[h], t * 64)
                nc.vector.scalar_tensor_tensor(out=bh[h][:, :], in0=kku[:, :], scalar=0.5, in1=em[h][:, :],
                                               op0=ALU.mult, op1=ALU.mult).then_inc(bh_ready, 1)
                dve.wait_ge(kp_ready, u + 1)
                nc.vector.tensor_tensor(kh[h][:, :], kp[:, :], em[h][:, :], ALU.mult).then_inc(kh_ready, 1)
                dve.wait_ge(r_filled, u + 1)
                nc.vector.tensor_tensor(rt[h][:, :], pr[:, :], ep[h][:, :], ALU.mult).then_inc(rt_ready, 1)
                wait(dve, bonus_ready, u)
                nc.vector.tensor_tensor(rk[:, :], pr[:, :], kp[:, :], ALU.mult).then_inc(rk_ready, 1)
                dve.wait_ge(ee_ready, u + 1)
                nc.vector.tensor_tensor(at[h][:, :], kkn[:, :], ee[h][:, :], ALU.mult).then_inc(at_ready, 1)
                dve.wait_ge(rkr_ready, u + 1)
                nc.vector.tensor_reduce(bonus[h][:, :], heads(rk[:, :]), X, ALU.add).then_inc(bonus_ready, 1)

            nc.vector.memset(dx[0:1, :], 0.0).then_inc(ready0, 1)
            nc.vector.memset(one[:, :], 1.0).then_inc(ready0, 1)
            nc.vector.memset(hid_w[RANK:RANK + 1, :], 1.0).then_inc(ready0, 1)
            nc.vector.memset(hid_a[RANK:RANK + 1, :], 1.0).then_inc(ready0, 1)
            for h in range(2):
                nc.vector.memset(dec[h][:, :, :], 1.0).then_inc(ready0, 1)

            make_dx(0)
            dve.wait_ge(mu_ready, 1)
            mix_rk(0, 0)
            dve.wait_ge(w_loaded, 16 * 7)
            tiles(dve, T, lambda t, par_: (unit(t, par_, 0), unit(t, par_, 1)))


def phase_a2(nc, m, io, T):
    with ExitStack() as ctx:
        def sb(name, shape):
            return ctx.enter_context(nc.sbuf_tensor("a2_" + name, shape, F32))

        sems = []

        def sem(name):
            sems.append(ctx.enter_context(nc.semaphore("a2_" + name)))
            return sems[-1]

        wv, wg = sb("wv", [P, NB, D]), sb("wg", [P, NB, D])
        par = sb("par", [P, 2, D])
        mu_rows, mu = sb("mu_rows", [6 * NB, P]), sb("mu", [P, 6, NB])
        x = [sb(f"x{i}", [P, D]) for i in range(2)]
        dx = [sb(f"dx{i}", [P, D]) for i in range(2)]
        xT, dT = sb("xT", [P, NB, P]), sb("dT", [P, NB, P])
        mix_v = [sb(f"mix_v{i}", [P, NB, P]) for i in range(2)]
        mix_g = [sb(f"mix_g{i}", [P, NB, P]) for i in range(2)]
        bonus = [sb(f"bonus{i}", [P, NH]) for i in range(2)]
        v, g, gmul, gadd = (sb(n, [P, D]) for n in ("v", "g", "gmul", "gadd"))

        bank = lambda name: ctx.enter_context(nc.psum_tensor("a2_" + name, [P, 512], F32))
        pv, pg, pin = [bank("pv0"), bank("pv1")], [bank("pg0"), bank("pg1")], bank("pin")

        w_loaded, mu_loaded, par_loaded = sem("w_loaded"), sem("mu_loaded"), sem("par_loaded")
        x_loaded = [sem(f"x_loaded{i}") for i in range(2)]
        bonus_loaded = [sem(f"bonus_loaded{i}") for i in range(2)]
        zero_row = sem("zero_row")
        mu_filled, mu_ready, dx_ready = sem("mu_filled"), sem("mu_ready"), sem("dx_ready")
        in_filled, in_taken = sem("in_filled"), sem("in_taken")
        mixv_ready, mixg_ready = sem("mixv_ready"), sem("mixg_ready")
        v_filled, g_filled = sem("v_filled"), sem("g_filled")
        v_ready, g_ready = sem("v_ready"), sem("g_ready")
        gmul_ready, gadd_ready, bv_ready, sum_ready = (sem(n) for n in ("gmul_ready", "gadd_ready", "bv_ready", "sum_ready"))
        v_stored, gmul_stored, gadd_stored = sem("v_stored"), sem("gmul_stored"), sem("gadd_stored")

        ctx.callback(clear_semaphores, nc, sems)
        block = ctx.enter_context(nc.Block())

        def loads_of(t, par_):
            return of_parity(t, par_, 32) + (16 * SAMPLE_LOADS if is_sample(t, T) else 32)

        @block.sync
        def _(sp):
            sp.dma_start(mu_rows[:, :], io["a_mu"][0].rearrange("m (j p) -> (m j) p", p=P)).then_inc(mu_loaded, 16)

            def load_x(t, par_):
                wait(sp, in_filled, (t - 1) * 4)
                src = io["x_sample"].rearrange("b i d -> (b i) d") if is_sample(t, T) else io["x_prompt"][0][rows(t), :]
                sp.dma_start(x[par_][:, :], src).then_inc(x_loaded[par_], 16)
                if isinstance(t, int) and t == 0:
                    sp.wait_ge(zero_row, 1)
                load_previous_rows(nc, sp, t, is_sample(t, T), io["x_prompt"][0], io["x_sample"],
                                   io["state_a_shift"], dx[par_], x_loaded[par_])
                wait(sp, gadd_ready, (t - 1) * 2)
                sp.dma_start(bonus[par_][:, :], io["bonus"][rows(t), :]).then_inc(bonus_loaded[par_], 16)

            load_x(0, 0)
            for src, dst in ((io["a_w_in"][0, 2], wv), (io["a_w_in"][0, 3], wg)):
                for h in range(2):
                    cols = slice(h * HALF, (h + 1) * HALF)
                    sp.dma_start(dst[:, :, cols], src.rearrange("(j p) n -> p j n", p=P)[:, :, cols]).then_inc(w_loaded, 16)
            load_x(1, 1)
            for i, name in enumerate(("a_gn_g", "a_gn_b")):
                sp.dma_start(par[:, i, :], io[name].to_broadcast([P, D])).then_inc(par_loaded, 16)

            def step(t, par_):
                if not is_sample(t, T) and not (isinstance(t, int) and t == T - 1):
                    load_x(t + 2, par_)
                for h in range(2):
                    cols = slice(h * HALF, (h + 1) * HALF)
                    sp.wait_ge(v_ready, t * 2 + (h + 1))
                    sp.dma_start(io["tok_v"][rows(t), cols], v[:, cols]).then_inc(v_stored, 16)
                    sp.wait_ge(gmul_ready, t * 2 + (h + 1))
                    sp.dma_start(io["gate_mul"][rows(t), cols], gmul[:, cols]).then_inc(gmul_stored, 16)
                    sp.wait_ge(gadd_ready, t * 2 + (h + 1))
                    sp.dma_start(io["gate_add"][rows(t), cols], gadd[:, cols]).then_inc(gadd_stored, 16)

            tiles(sp, T, step)
            for stored in (v_stored, gmul_stored, gadd_stored):
                sp.wait_ge(stored, 32 * (T + 1))

        @block.tensor
        def _(pe):
            pe.wait_ge(mu_loaded, 16)
            nc.tensor.transpose(pin[:, 0:6 * NB], mu_rows[:, :], m["ident"][0:6 * NB, 0:6 * NB]).then_inc(mu_filled, 1)
            pe.wait_ge(mu_ready, 1)

            def turn_in(t, par_, grp):
                if grp == 0:
                    pe.wait_ge(x_loaded[par_], loads_of(t, par_))
                if grp == 1:
                    pe.wait_ge(dx_ready, t + 1)
                wait(pe, in_taken, t * 4 + grp)
                src = x[par_] if grp % 2 == 0 else dx[par_]
                for i in range(HB):
                    j = (grp // 2) * HB + i
                    last = nc.tensor.transpose(pin[:, i * P:(i + 1) * P], src[:, j * P:(j + 1) * P], m["ident"])
                last.then_inc(in_filled, 1)

            def step(t, par_):
                for h in range(2):
                    cols = slice(h * HALF, (h + 1) * HALF)
                    if isinstance(t, int) and t == 0:
                        pe.wait_ge(w_loaded, 16 * 4)
                    pe.wait_ge(mixv_ready, t + 1)
                    wait(pe, v_ready, t * 2 - (1 - h))
                    gemm(nc, pv[h][:, :], mix_v[par_], wv, cols).then_inc(v_filled, 1)
                    if not is_sample(t, T):
                        turn_in(t + 1, 1 - par_, h * 2)
                    pe.wait_ge(mixg_ready, t + 1)
                    wait(pe, g_ready, t * 2 - (1 - h))
                    gemm(nc, pg[h][:, :], mix_g[par_], wg, cols).then_inc(g_filled, 1)
                    if not is_sample(t, T):
                        turn_in(t + 1, 1 - par_, h * 2 + 1)

            for grp in range(4):
                turn_in(0, 0, grp)
            tiles(pe, T, step)

        @block.scalar
        def _(act):
            act.wait_ge(mu_filled, 1)
            nc.scalar.copy(mu[:, :, :].rearrange("p m j -> p (m j)"), pin[:, 0:6 * NB]).then_inc(mu_ready, 1)

            def take_in(t, grp):
                act.wait_ge(in_filled, t * 4 + (grp + 1))
                if grp == 0:
                    wait(act, mixg_ready, t)
                dst = xT if grp % 2 == 0 else dT
                half = slice((grp // 2) * HB, (grp // 2 + 1) * HB)
                nc.scalar.copy(dst[:, half, :].rearrange("p j t -> p (j t)"), pin[:, :]).then_inc(in_taken, 1)

            def step(t, par_):
                for h in range(2):
                    cols = slice(h * HALF, (h + 1) * HALF)
                    act.wait_ge(v_filled, t * 2 + (h + 1))
                    wait(act, v_stored, t * 32)
                    wait(act, bv_ready, t * 2)
                    nc.scalar.copy(v[:, cols], pv[h][:, :]).then_inc(v_ready, 1)
                    if not is_sample(t, T):
                        take_in(t + 1, h * 2)
                    act.wait_ge(g_filled, t * 2 + (h + 1))
                    wait(act, gadd_ready, t * 2)
                    nc.scalar.activation(g[:, cols], pg[h][:, :], ACT.Silu).then_inc(g_ready, 1)
                    if not is_sample(t, T):
                        take_in(t + 1, h * 2 + 1)

            for grp in range(4):
                take_in(0, grp)
            tiles(act, T, step)

        @block.vector
        def _(dve):
            nc.vector.memset(dx[0][0:1, :], 0.0).then_inc(zero_row, 1)

            def make_dx(t, par_):
                dve.wait_ge(x_loaded[par_], loads_of(t, par_))
                nc.vector.tensor_tensor(dx[par_][:, :], dx[par_][:, :], x[par_][:, :], ALU.subtract).then_inc(dx_ready, 1)

            def mixes(t, par_):
                dve.wait_ge(in_taken, t * 4 + 4)
                wait(dve, g_filled, t * 2 - 2)
                for dst, row, ready in ((mix_v[par_], 3, mixv_ready), (mix_g[par_], 5, mixg_ready)):
                    for j in range(NB):
                        last = nc.vector.scalar_tensor_tensor(out=dst[:, j, :], in0=dT[:, j, :], scalar=mu[:, row, j:j + 1],
                                                              in1=xT[:, j, :], op0=ALU.mult, op1=ALU.add)
                    last.then_inc(ready, 1)

            def step(t, par_):
                if not is_sample(t, T):
                    make_dx(t + 1, 1 - par_)
                for h in range(2):
                    n = t * 2 + (h + 1)
                    cols = slice(h * HALF, (h + 1) * HALF)
                    dve.wait_ge(v_ready, n)
                    dve.wait_ge(bonus_loaded[par_], of_parity(t, par_, 16) + 16)
                    wait(dve, gadd_stored, t * 32)
                    b = bonus[par_][:, h * HH:(h + 1) * HH].unsqueeze(2).to_broadcast([P, HH, HD])
                    nc.vector.tensor_tensor(gadd[:, cols].rearrange("p (h n) -> p h n", n=HD),
                                            v[:, cols].rearrange("p (h n) -> p h n", n=HD), b, ALU.mult).then_inc(bv_ready, 1)
                    dve.wait_ge(bv_ready, n)
                    nc.vector.tensor_tensor(gadd[:, cols], gadd[:, cols], par[:, 1, cols], ALU.add).then_inc(sum_ready, 1)
                    dve.wait_ge(g_ready, n)
                    wait(dve, gmul_stored, t * 32)
                    nc.vector.tensor_tensor(gmul[:, cols], g[:, cols], par[:, 0, cols], ALU.mult).then_inc(gmul_ready, 1)
                    dve.wait_ge(sum_ready, n)
                    nc.vector.tensor_tensor(gadd[:, cols], gadd[:, cols], g[:, cols], ALU.mult).then_inc(gadd_ready, 1)
                if not is_sample(t, T):
                    mixes(t + 1, 1 - par_)

            make_dx(0, 0)
            dve.wait_ge(mu_ready, 1)
            mixes(0, 0)
            dve.wait_ge(par_loaded, 32)
            tiles(dve, T, step)


LEVELS = (2, 4, 8, 16, 32, 64)
SCORE_USES = NH + 4
M_USES = 4 * len(LEVELS)
TU_USES = 8 * (len(LEVELS) - 1) + 4


def phase_a3(nc, m, io, T, sample=False):
    with ExitStack() as ctx:
        pre = "s3_" if sample else "a3_"
        bufs = 1 if sample else 2

        def sb(name, shape):
            return ctx.enter_context(nc.sbuf_tensor(pre + name, shape, F32))

        sems = []

        def sem(name):
            sems.append(ctx.enter_context(nc.semaphore(pre + name)))
            return sems[-1]

        K_, R_, B_, A_ = range(4)
        fac = [sb(f"fac{i}", [P, 4, NB, P]) for i in range(bufs)]
        dec = [sb(f"dec{i}", [P, NB, DEC]) for i in range(bufs)]
        sc = [sb(f"sc{i}", [P, NH, 4, P]) for i in range(bufs)]
        quad = sb("quad", [P, 4, P])
        tu = sb("tu", [P, NH, 2, P])
        mp = sb("mp", [P, NH, P])
        ufin = sb("ufin", [P, NH, P])
        tok = sb("tok", [P, 3, D])
        gates = sb("gates", [P, 2, D])
        xs, sa, o, tmp = (sb(n, [P, D]) for n in ("xs", "sa", "o", "tmp"))
        f, s1, s2 = sb("f", [P, NB]), sb("s1", [P, NH]), sb("s2", [P, NH])
        if sample:
            st = sb("st", [P, NB, DEC, P])
            seq_cols = sb("seq_cols", [P, DEC, P])
            raw = sb("raw", [P, DEC, HD])
            raw_bd = sb("raw_bd", [P, DEC, P])
            wide = sb("wide", [P, 2, DEC, P])
        else:
            st = sb("st", [P, NB, P])
            raw = sb("raw", [P, NB, HD])

        bank = lambda name: ctx.enter_context(nc.psum_tensor(pre + name, [P, 512], F32))
        psc, pm, ptu, pch = ([bank(f"{n}{i}") for i in range(2)] for n in ("psc", "pm", "ptu", "pch"))

        fac_loaded = [sem(f"fac_loaded{i}") for i in range(bufs)]
        tok_loaded, gates_loaded = sem("tok_loaded"), sem("gates_loaded")
        setup = sem("setup")
        sc_filled, sc_taken = sem("sc_filled"), sem("sc_taken")
        aprime_ready, t1_ready = sem("aprime_ready"), sem("t1_ready")
        m_filled, m_ready = sem("m_filled"), sem("m_ready")
        tu_filled, tu_taken = sem("tu_filled"), sem("tu_taken")
        x_filled, x_ready = sem("x_filled"), sem("x_ready")
        sa_filled, sa_ready = sem("sa_filled"), sem("sa_ready")
        o_filled, o_ready = sem("o_filled"), sem("o_ready")
        p_filled, state_sum, state_ready, f_ready = sem("p_filled"), sem("state_sum"), sem("state_ready"), sem("f_ready")
        sum_ready, mean_ready, d_ready, sq_ready = (sem(n + "_ready") for n in ("sum", "mean", "d", "sq"))
        sqsum_ready, var_ready, std_ready, rstd_ready = (sem(n + "_ready") for n in ("sqsum", "var", "std", "rstd"))
        dn_ready, ymul_ready, y_ready, y_stored = sem("dn_ready"), sem("ymul_ready"), sem("y_ready"), sem("y_stored")
        out_filled, out_ready, state_stored = sem("out_filled"), sem("out_ready"), sem("state_stored")
        if sample:
            raw_loaded, bd_ready, bd_filled, bd_taken = (sem(n) for n in ("raw_loaded", "bd_ready", "bd_filled", "bd_taken"))
            wide_ready, wide_used = sem("wide_ready"), sem("wide_used")

        tile0 = T if sample else 0
        steps = 1 if sample else T

        ctx.callback(clear_semaphores, nc, sems)
        block = ctx.enter_context(nc.Block())

        def over(eng, step):
            if sample:
                step(0, 0)
                step(1, 0)
            else:
                tiles(eng, T, step)

        def has_tile(t):
            return not (isinstance(t, int) and t == steps)

        def has_chain(t):
            return not (isinstance(t, int) and t == 0)

        def fac_loads(t, par_):
            return of_parity(t, par_, 32) + 32

        @block.sync
        def _(sp):
            def load_factors(t, par_):
                sp.dma_start(fac[par_][:, :, :, :], io["factors"][rows(t + tile0), :, :, :]).then_inc(fac_loaded[par_], 16)
                sp.dma_start(dec[par_][:, :, :], io["dec"][rows(t + tile0), :, :]).then_inc(fac_loaded[par_], 16)

            def load_tok(t):
                for i, name in enumerate(("tok_b", "tok_k", "tok_v")):
                    sp.dma_start(tok[:, i, :], io[name][rows(t + tile0), :]).then_inc(tok_loaded, 16)

            def load_gates(t):
                for i, name in enumerate(("gate_mul", "gate_add")):
                    sp.dma_start(gates[:, i, :], io[name][rows(t + tile0), :]).then_inc(gates_loaded, 16)

            load_factors(0, 0)
            load_tok(0)
            load_gates(0)
            if sample:
                for j in range(NB):
                    wait(sp, bd_ready, j)
                    for b in range(DEC):
                        src = io["state_a_wkv"][0, b, 2 * j:2 * j + 2, :, :].rearrange("e v k -> (e v) k")
                        sp.dma_start(raw[:, b, :], src).then_inc(raw_loaded, 16)
            else:
                load_factors(1, 1)

            def step(t, par_):
                if has_chain(t):
                    if has_tile(t) and not (isinstance(t, int) and t == steps - 1):
                        sp.wait_ge(o_filled, t)
                        sp.wait_ge(f_ready, t)
                        load_factors(t + 1, 1 - par_)
                    if has_tile(t):
                        sp.wait_ge(p_filled, t)
                        load_tok(t)
                    sp.wait_ge(y_ready, t)
                    sp.dma_start(io["mixed"][rows(t + (tile0 - 1)), :], tmp[:, :]).then_inc(y_stored, 16)
                    if has_tile(t):
                        load_gates(t)

            over(sp, step)
            if sample:
                for j in range(NB):
                    sp.wait_ge(out_ready, 2 * j + 2)
                    for b in range(DEC):
                        dst = io["sample_wkv"][0, b, 2 * j:2 * j + 2, :, :].rearrange("e v k -> (e v) k")
                        sp.dma_start(dst, raw[:, b, :]).then_inc(state_stored, 16)
                sp.wait_ge(state_stored, 16 * DEC * NB)
            else:
                sp.wait_ge(out_ready, 4)
                dst = io["prompt_wkv"][0, 0].rearrange("(j e) v k -> (e v) j k", e=2)
                sp.dma_start(dst, raw[:, :, :]).then_inc(state_stored, 16)
                sp.wait_ge(state_stored, 16)
            sp.wait_ge(y_stored, 16 * steps)

        @block.tensor
        def _(pe):
            def head(ap, h):
                return ap[64 * (h % 2):64 * (h % 2) + 64, h // 2, :]

            def scores(t, par_):
                fb = fac[par_]
                pe.wait_ge(fac_loaded[par_], fac_loads(t, par_))
                for h in range(NH):
                    wait(pe, sc_taken, t * SCORE_USES + (h - 1))
                    out = psc[h % 2]
                    a, r, b, k = (head(fb[:, i, :, :], h) for i in (A_, R_, B_, K_))
                    nc.tensor.matmul(out[:, 0:P], a, b, start=True, stop=True)
                    nc.tensor.matmul(out[:, P:2 * P], b, r, start=True, stop=True)
                    nc.tensor.matmul(out[:, 2 * P:3 * P], k, a, start=True, stop=True)
                    nc.tensor.matmul(out[:, 3 * P:4 * P], k, r, start=True, stop=True).then_inc(sc_filled, 1)

            def turn(t, par_):
                for b in range(4):
                    pe.wait_ge(aprime_ready, t * 4 + (b + 1))
                    pe.wait_ge(sc_taken, t * SCORE_USES + (NH + b - 1))
                    for i in range(4):
                        last = nc.tensor.transpose(psc[b % 2][:, i * P:(i + 1) * P], sc[par_][:, 4 * b + i, 0, :], m["ident"])
                    last.then_inc(sc_filled, 1)

            def level(t, par_, l):
                final = l == len(LEVELS) - 1
                for b in range(4):
                    if l == 0:
                        pe.wait_ge(t1_ready, t * 4 + (b + 1))
                        pe.wait_ge(sc_taken, t * SCORE_USES + (NH + b + 1))
                    else:
                        pe.wait_ge(tu_taken, t * TU_USES + (8 * (l - 1) + 2 * b + 2))
                    wait(pe, m_ready, t * M_USES + (4 * l + b - 1))
                    for i in range(4):
                        h = 4 * b + i
                        last = nc.tensor.matmul(pm[b % 2][:, i * P:(i + 1) * P], sc[par_][:, h, 0, :], tu[:, h, 1, :],
                                                start=True, stop=True)
                    last.then_inc(m_filled, 1)
                for q in range(4 if final else 8):
                    pe.wait_ge(m_ready, t * M_USES + (4 * l + (q if final else q // 2) + 1))
                    wait(pe, tu_taken, t * TU_USES + (8 * l + q - 1))
                    out = ptu[q % 2]
                    if final:
                        for i in range(4):
                            h = 4 * q + i
                            last = nc.tensor.matmul(out[:, i * P:(i + 1) * P], tu[:, h, 0, :], mp[:, h, :],
                                                    start=True, stop=True)
                    else:
                        for i in range(2):
                            h = 2 * q + i
                            nc.tensor.matmul(out[:, 2 * i * P:(2 * i + 1) * P], mp[:, h, :], tu[:, h, 0, :],
                                             start=True, stop=True)
                            last = nc.tensor.matmul(out[:, (2 * i + 1) * P:(2 * i + 2) * P], tu[:, h, 0, :], mp[:, h, :],
                                                    start=True, stop=True)
                    last.then_inc(tu_filled, 1)

            def pair_cols(j):
                return slice((j % 4) * P, (j % 4 + 1) * P)

            def from_state(c, c_par, which, j, slot):
                out = pch[j // 4][:, pair_cols(j)]
                if not sample:
                    nc.tensor.matmul(out, fac[c_par][:, which, j, :], st[:, j, :], start=True, stop=False)
                    return
                pe.wait_ge(wide_ready, slot + 1)
                for b in range(DEC):
                    nc.tensor.matmul(out, wide[:, slot % 2, b, :], st[:, j, b, :], start=(b == 0), stop=False)

            def add_heads(j, parts, stop=True):
                n = [(h, *p) for h in (2 * j, 2 * j + 1) for p in parts]
                for i, (h, lhsT, rhs) in enumerate(n):
                    cols = slice((h % 8) * HD, (h % 8 + 1) * HD)
                    last = nc.tensor.matmul(pch[j // 4][:, cols], lhsT(h), rhs[:, h * HD:(h + 1) * HD],
                                            start=False, stop=(i == len(n) - 1))
                return last

            def chain(t, par_, part):
                c_par = 0 if sample else 1 - par_
                if part == "x":
                    pe.wait_ge(tok_loaded, t * 48)
                    if sample:
                        pe.wait_ge(bd_taken, 2 * NB)
                    else:
                        wait(pe, state_ready, t - 1)
                    for j in range(NB):
                        from_state(t - 1, c_par, A_, j, j)
                        last = add_heads(j, [(lambda h: sc[c_par][:, h, 2, :], tok[:, 2, :])])
                        last.then_inc(x_filled, 1)
                if part == "sa":
                    pe.wait_ge(x_ready, t * 2)
                    pe.wait_ge(tu_taken, t * TU_USES)
                    for h in range(NH):
                        last = nc.tensor.matmul(pch[h // 8][:, (h % 8) * HD:(h % 8 + 1) * HD], ufin[:, h, :],
                                                xs[:, h * HD:(h + 1) * HD], start=True, stop=True)
                    last.then_inc(sa_filled, 1)
                if part == "o":
                    pe.wait_ge(sa_ready, t * 2)
                    for j in range(NB):
                        from_state(t - 1, c_par, R_, j, NB + j)
                        last = add_heads(j, [(lambda h: sc[c_par][:, h, 1, :], sa), (lambda h: sc[c_par][:, h, 3, :], tok[:, 2, :])])
                        if sample:
                            last.then_inc(wide_used, 1)
                        elif j == NB - 1:
                            last.then_inc(o_filled, 1)
                if part == "p":
                    pe.wait_ge(o_ready, t * 2)
                    if not sample:
                        for j in range(NB):
                            cols = slice(j * P, (j + 1) * P)
                            out = pch[j // 4][:, pair_cols(j)]
                            nc.tensor.matmul(out, tok[:, 0, cols], sa[:, cols], start=True, stop=False)
                            last = nc.tensor.matmul(out, tok[:, 1, cols], tok[:, 2, cols], start=False, stop=True)
                        last.then_inc(p_filled, 1)
                        return
                    for j in range(NB):
                        cols = slice(j * P, (j + 1) * P)
                        pe.wait_ge(wide_ready, 2 * NB + 2 * j + 2)
                        wait(pe, out_ready, 2 * j)
                        for q in range(2):
                            for i in range(2):
                                last = nc.tensor.matmul(pch[q][:, :], tok[:, i, cols], wide[:, i, 4 * q:4 * q + 4, :],
                                                        start=(i == 0), stop=(i == 1))
                        last.then_inc(p_filled, 1)
                        pe.wait_ge(state_ready, j + 1)
                        for b in range(DEC):
                            last = nc.tensor.transpose(psc[b // 4][:, (b % 4) * P:(b % 4 + 1) * P], st[:, j, b, :], m["ident"])
                        last.then_inc(out_filled, 1)

            def step(t, par_):
                if has_tile(t):
                    scores(t, par_)
                    turn(t, par_)
                parts = ["x", "sa", "o", "p"] if has_chain(t) else []
                if parts:
                    chain(t, par_, "x")
                for l in range(len(LEVELS)):
                    if has_tile(t):
                        level(t, par_, l)
                    if parts and l < 3:
                        chain(t, par_, parts[l + 1])

            pe.wait_ge(setup, 4 if sample else 5)
            if sample:
                for j in range(NB):
                    pe.wait_ge(bd_ready, j + 1)
                    wait(pe, bd_taken, 2 * j)
                    for b in range(DEC):
                        last = nc.tensor.transpose(pch[b // 4][:, (b % 4) * P:(b % 4 + 1) * P], raw_bd[:, b, :], m["ident"])
                    last.then_inc(bd_filled, 1)
            over(pe, step)
            if not sample:
                pe.wait_ge(state_ready, T)
                pe.wait_ge(sc_taken, T * SCORE_USES)
                for j in range(NB):
                    last = nc.tensor.transpose(psc[j // 4][:, pair_cols(j)], st[:, j, :], m["ident"])
                last.then_inc(out_filled, 1)

        @block.scalar
        def _(act):
            def take_tu(t, l):
                final = l == len(LEVELS) - 1
                for q in range(4 if final else 8):
                    act.wait_ge(tu_filled, t * TU_USES + (8 * l + q + 1))
                    if final:
                        dst = ufin[:, 4 * q:4 * q + 4, :].rearrange("p h c -> p (h c)")
                    else:
                        dst = tu[:, 2 * q:2 * q + 2, :, :].rearrange("p h i c -> p (h i c)")
                    nc.scalar.copy(dst, ptu[q % 2][:, :]).then_inc(tu_taken, 1)

            def take(dst, ready, scale=1.0):
                for i in range(2):
                    nc.scalar.mul(dst[:, i * HALF:(i + 1) * HALF], pch[i][:, :], scale).then_inc(ready, 1)

            def chain(t, part):
                if part == "x":
                    act.wait_ge(x_filled, t * NB)
                    wait(act, sqsum_ready, t - 1)
                    take(xs, x_ready)
                if part == "sa":
                    act.wait_ge(sa_filled, t)
                    take(sa, sa_ready, -1.0)
                if part == "o":
                    if sample:
                        act.wait_ge(wide_used, NB)
                    else:
                        act.wait_ge(o_filled, t)
                    wait(act, d_ready, t - 1)
                    take(o, o_ready)
                if part == "square":
                    act.wait_ge(d_ready, t)
                    nc.scalar.square(xs[:, :], tmp[:, :]).then_inc(sq_ready, 1)
                if part == "root":
                    act.wait_ge(var_ready, t)
                    nc.scalar.activation(s2[:, :], s2[:, :], ACT.Sqrt).then_inc(std_ready, 1)

            def step(t, par_):
                parts = ["sa", "o", None, "square", "root", None] if has_chain(t) else [None] * 6
                if has_chain(t):
                    chain(t, "x")
                for l in range(len(LEVELS)):
                    if has_tile(t):
                        take_tu(t, l)
                    if parts[l]:
                        chain(t, parts[l])

            if sample:
                for j in range(NB):
                    act.wait_ge(bd_filled, j + 1)
                    for q in range(2):
                        nc.scalar.copy(st[:, j, 4 * q:4 * q + 4, :].rearrange("p b c -> p (b c)"), pch[q][:, :]).then_inc(bd_taken, 1)
            over(act, step)

        @block.gpsimd
        def _(pool):
            signs = ["s_neg_lower", "s_incl", "s_strict", "s_incl"] if sample else ["neg_lower", "incl", "strict", "incl"]
            for i, name in enumerate(signs):
                nc.gpsimd.tensor_copy(quad[:, i, :], m[name]).then_inc(setup, 1)
                pool.wait_ge(setup, i + 1)
            if sample:
                nc.gpsimd.memset(seq_cols[:, :, :], 1.0).then_inc(setup, 1)
                pool.wait_ge(setup, 5)
                nc.gpsimd.affine_select(out=seq_cols[:, :, :], in_=seq_cols[:, :, :], compare_op=ALU.is_ge, fill=0.0, base=0,
                                        pattern=[[-DSEQ, DEC], [1, P]], channel_multiplier=0).then_inc(setup, 1)
                pool.wait_ge(setup, 6)
                nc.gpsimd.affine_select(out=seq_cols[:, :, :], in_=seq_cols[:, :, :], compare_op=ALU.is_ge, fill=0.0, base=DSEQ - 1,
                                        pattern=[[DSEQ, DEC], [-1, P]], channel_multiplier=0).then_inc(setup, 1)
                pool.wait_ge(setup, 7)
                nc.gpsimd.memset(raw_bd[:, :, :], 0.0).then_inc(setup, 1)
                pool.wait_ge(setup, 8)
                for j in range(NB):
                    pool.wait_ge(raw_loaded, 16 * DEC * (j + 1))
                    wait(pool, bd_filled, j)
                    nc.gpsimd.tensor_copy(raw_bd[0:64, :, 0:64], raw[0:64, :, :]).then_inc(setup, 1)
                    pool.wait_ge(setup, 9 + j)
                    nc.gpsimd.tensor_copy(raw_bd[64:P, :, 64:P], raw[64:P, :, :]).then_inc(bd_ready, 1)
                pool.wait_ge(bd_ready, NB)

            def a_prime(t, par_):
                for b in range(4):
                    heads = slice(4 * b, 4 * b + 4)
                    pool.wait_ge(sc_taken, t * SCORE_USES + (4 * b + 4))
                    a = sc[par_][:, heads, 0, :]
                    nc.gpsimd.tensor_tensor(a, a, m["ident"].unsqueeze(1).to_broadcast([P, 4, P]), ALU.add).then_inc(aprime_ready, 1)
                    pool.wait_ge(aprime_ready, t * 4 + (b + 1))
                    nc.gpsimd.tensor_tensor(tu[:, heads, 0, :], a, m["lev1T"].unsqueeze(1).to_broadcast([P, 4, P]),
                                            ALU.mult).then_inc(t1_ready, 1)

            def per_head(col):
                return col.unsqueeze(2).to_broadcast([P, NH, HD])

            def by_head(ap):
                return ap.rearrange("p (h n) -> p h n", n=HD)

            def step(t, par_):
                if has_tile(t):
                    a_prime(t, par_)
                if not has_chain(t):
                    return
                if sample:
                    pool.wait_ge(fac_loaded[0], 32)
                    for j in range(NB):
                        spread_after_x(j)
                    for j in range(NB):
                        spread_after_o(j)
                pool.wait_ge(mean_ready, t)
                wait(pool, y_stored, (t - 1) * 16)
                nc.gpsimd.tensor_tensor(by_head(tmp[:, :]), by_head(o[:, :]), per_head(s1[:, :]), ALU.subtract).then_inc(d_ready, 1)
                pool.wait_ge(rstd_ready, t)
                nc.gpsimd.tensor_tensor(by_head(tmp[:, :]), by_head(tmp[:, :]), per_head(s2[:, :]), ALU.mult).then_inc(dn_ready, 1)
                if sample:
                    for j in range(NB):
                        cols = slice(j * P, (j + 1) * P)
                        for i, src in enumerate((sa[:, cols], tok[:, 2, cols])):
                            wait(pool, p_filled, j)
                            nc.gpsimd.tensor_tensor(wide[:, i, :, :], src.unsqueeze(1).to_broadcast([P, DEC, P]),
                                                    m.seq_rows[:, :].unsqueeze(2).to_broadcast([P, DEC, P]), ALU.mult).then_inc(wide_ready, 1)
                            pool.wait_ge(wide_ready, 2 * NB + 2 * j + i + 1)

            def spread_after_x(j):
                if j >= 2:
                    pool.wait_ge(x_filled, j - 1)
                nc.gpsimd.tensor_tensor(wide[:, j % 2, :, :], fac[0][:, A_, j, :].unsqueeze(1).to_broadcast([P, DEC, P]),
                                        seq_cols[:, :, :], ALU.mult).then_inc(wide_ready, 1)

            def spread_after_o(j):
                pool.wait_ge(wide_ready, NB + j)
                if j < 2:
                    pool.wait_ge(x_filled, NB - 1 + j)
                else:
                    pool.wait_ge(wide_used, j - 1)
                nc.gpsimd.tensor_tensor(wide[:, j % 2, :, :], fac[0][:, R_, j, :].unsqueeze(1).to_broadcast([P, DEC, P]),
                                        seq_cols[:, :, :], ALU.mult).then_inc(wide_ready, 1)

            over(pool, step)

        @block.vector
        def _(dve):
            def take_scores(t, par_):
                for h in range(NH):
                    dve.wait_ge(sc_filled, t * SCORE_USES + (h + 1))
                    nc.vector.tensor_tensor(sc[par_][:, h, :, :], psc[h % 2][:, :].rearrange("p (i c) -> p i c", i=4),
                                            quad[:, :, :], ALU.mult).then_inc(sc_taken, 1)

            def take_turned(t):
                for b in range(4):
                    dve.wait_ge(sc_filled, t * SCORE_USES + (NH + b + 1))
                    nc.vector.tensor_tensor(tu[:, 4 * b:4 * b + 4, 1, :], psc[b % 2][:, :].rearrange("p (i c) -> p i c", i=4),
                                            m["lev1"].unsqueeze(1).to_broadcast([P, 4, P]), ALU.mult).then_inc(sc_taken, 1)

            def take_m(t, l):
                for b in range(4):
                    dve.wait_ge(m_filled, t * M_USES + (4 * l + b + 1))
                    nc.vector.tensor_tensor(mp[:, 4 * b:4 * b + 4, :], pm[b % 2][:, :].rearrange("p (i c) -> p i c", i=4),
                                            m[f"lev{LEVELS[l]}"].unsqueeze(1).to_broadcast([P, 4, P]), ALU.mult).then_inc(m_ready, 1)

            def chain(t, par_, part):
                c_par = 0 if sample else 1 - par_
                if part == "mean":
                    dve.wait_ge(o_ready, t * 2)
                    wait(dve, d_ready, t - 1)
                    nc.vector.tensor_reduce(s1[:, :], o[:, :].rearrange("p (h n) -> p h n", n=HD), X, ALU.add).then_inc(sum_ready, 1)
                    dve.wait_ge(sum_ready, t)
                    nc.vector.tensor_scalar(s1[:, :], s1[:, :], 1.0 / HD, None, ALU.mult).then_inc(mean_ready, 1)
                if part == "state" and not sample:
                    dve.wait_ge(p_filled, t)
                    for q in range(2):
                        for e in range(2):
                            s = st[64 * e:64 * e + 64, 4 * q:4 * q + 4, 64 * e:64 * e + 64]
                            d = pch[q][64 * e:64 * e + 64, :].rearrange("p (j c) -> p j c", j=4)[:, :, 64 * e:64 * e + 64]
                            nc.vector.tensor_tensor(s, d, s, ALU.add).then_inc(state_sum, 1)
                    dve.wait_ge(state_sum, t * 4)
                    dve.wait_ge(f_ready, t)
                    for e in range(2):
                        s = st[64 * e:64 * e + 64, :, 64 * e:64 * e + 64]
                        last = nc.vector.tensor_tensor(s, s, f[64 * e:64 * e + 64, :].unsqueeze(2).to_broadcast([64, NB, 64]), ALU.mult)
                    last.then_inc(state_ready, 1)
                if part == "var":
                    dve.wait_ge(sq_ready, t)
                    wait(dve, dn_ready, t - 1)
                    nc.vector.tensor_reduce(s2[:, :], xs[:, :].rearrange("p (h n) -> p h n", n=HD), X, ALU.add).then_inc(sqsum_ready, 1)
                    dve.wait_ge(sqsum_ready, t)
                    nc.vector.tensor_scalar(s2[:, :], s2[:, :], 1.0 / HD, GN_EPS, ALU.mult, ALU.add).then_inc(var_ready, 1)
                if part == "rstd":
                    dve.wait_ge(std_ready, t)
                    nc.vector.reciprocal(s2[:, :], s2[:, :]).then_inc(rstd_ready, 1)
                if part == "y":
                    dve.wait_ge(dn_ready, t)
                    dve.wait_ge(gates_loaded, t * 32)
                    nc.vector.tensor_tensor(tmp[:, :], tmp[:, :], gates[:, 0, :], ALU.mult).then_inc(ymul_ready, 1)
                    dve.wait_ge(ymul_ready, t)
                    nc.vector.tensor_tensor(tmp[:, :], tmp[:, :], gates[:, 1, :], ALU.add).then_inc(y_ready, 1)

            def decay_factor(t, par_):
                if has_tile(t):
                    dve.wait_ge(fac_loaded[par_], fac_loads(t, par_))
                    nc.vector.tensor_tensor(f[:, :], dec[1 - par_][:, :, 1], dec[par_][:, :, 0], ALU.mult).then_inc(f_ready, 1)
                else:
                    nc.vector.tensor_copy(f[:, :], dec[1 - par_][:, :, 1]).then_inc(f_ready, 1)

            def step(t, par_):
                if has_tile(t):
                    take_scores(t, par_)
                    take_turned(t)
                if has_chain(t) and not sample:
                    decay_factor(t, par_)
                parts = [None, None, "mean", "state", "var", "rstd"] if has_chain(t) else [None] * 6
                for l in range(len(LEVELS)):
                    if has_tile(t):
                        take_m(t, l)
                    if parts[l]:
                        chain(t, par_, parts[l])
                if has_chain(t):
                    chain(t, par_, "y")

            dve.wait_ge(setup, 4)
            if sample:
                dve.wait_ge(bd_taken, 2 * NB)
            else:
                nc.vector.memset(st[:, :, :], 0.0).then_inc(setup, 1)
                dve.wait_ge(setup, 5)
            over(dve, step)
            if sample:
                for j in range(NB):
                    dve.wait_ge(p_filled, j + 1)
                    for q in range(2):
                        for e in range(2):
                            s = st[64 * e:64 * e + 64, j, 4 * q:4 * q + 4, 64 * e:64 * e + 64]
                            d = pch[q][64 * e:64 * e + 64, :].rearrange("p (b c) -> p b c", b=4)[:, :, 64 * e:64 * e + 64]
                            nc.vector.tensor_tensor(s, d, s, ALU.add).then_inc(state_sum, 1)
                    dve.wait_ge(state_sum, 4 * (j + 1))
                    for e in range(2):
                        s = st[64 * e:64 * e + 64, j, :, 64 * e:64 * e + 64]
                        last = nc.vector.tensor_tensor(s, s, dec[0][64 * e:64 * e + 64, j, :].unsqueeze(2).to_broadcast([64, DEC, 64]), ALU.mult)
                    last.then_inc(state_ready, 1)
                    dve.wait_ge(out_filled, j + 1)
                    wait(dve, state_stored, 16 * DEC * j)
                    for e in range(2):
                        for q in range(2):
                            d = psc[q][64 * e:64 * e + 64, :].rearrange("p (b c) -> p b c", b=4)[:, :, 64 * e:64 * e + 64]
                            last = nc.vector.tensor_copy(raw[64 * e:64 * e + 64, 4 * q:4 * q + 4, :], d)
                        last.then_inc(out_ready, 1)
            else:
                dve.wait_ge(out_filled, 1)
                for q in range(2):
                    for e in range(2):
                        d = psc[q][64 * e:64 * e + 64, :].rearrange("p (j c) -> p j c", j=4)[:, :, 64 * e:64 * e + 64]
                        nc.vector.tensor_copy(raw[64 * e:64 * e + 64, 4 * q:4 * q + 4, :], d).then_inc(out_ready, 1)


def phase_a3_sample(nc, m, io, T):
    phase_a3(nc, m, io, T, sample=True)


class Uses:

    def __init__(self, order, full=2):
        self.order, self.full = order, full
        self.n = len(order(full))
        assert self.n % 2 == 0

    def before(self, t, what):
        if isinstance(t, int):
            return sum(len(self.order(i)) for i in range(t)) + self.order(t).index(what)
        start = sum(len(self.order(i)) for i in range(self.full))
        return t * self.n + (start - self.full * self.n + self.order(self.full).index(what))

    def bank(self, t, what):
        i = t if isinstance(t, int) else self.full
        return self.before(i, what) % 2


def iterations(eng, T, step):
    tiles(eng, T, step)
    step(T + 1, 1)
    step(T + 2, 0)


class Norm:

    def __init__(self, nc, sb, sem, name, gain, bias):
        self.nc, self.gain, self.bias = nc, gain, bias
        self.stats, self.mv, self.rstd = sb(name + "_stats", [P, 2, 6]), sb(name + "_mv", [P, 2]), sb(name + "_rstd", [P, 1])
        self.pause = sb(name + "_pause", [P, 1])
        self.stats_ready, self.mv_ready, self.var_ready = sem(name + "_stats"), sem(name + "_mv"), sem(name + "_var")
        self.std_ready, self.rstd_ready = sem(name + "_std"), sem(name + "_rstd")
        self.scaled_ready, self.gained_ready, self.done_ready = sem(name + "_scaled"), sem(name + "_gained"), sem(name + "_done")

    def statistics(self, dve, buf, n):
        nc = self.nc
        for h in range(2):
            nc.vector.bn_stats(self.stats[:, h, :], buf[:, h * HALF:(h + 1) * HALF]).then_inc(self.stats_ready, 1)
        dve.wait_ge(self.stats_ready, n * 2 + 2)
        nc.vector.memset(self.pause[:, :], 0.0)
        nc.vector.bn_aggr(self.mv[:, :], self.stats[:, :, :]).then_inc(self.mv_ready, 1)
        dve.wait_ge(self.mv_ready, n + 1)
        nc.vector.tensor_scalar(self.rstd[:, :], self.mv[:, 1:2], LN_EPS, None, ALU.add).then_inc(self.var_ready, 1)

    def root(self, act, n):
        act.wait_ge(self.var_ready, n + 1)
        self.nc.scalar.activation(self.rstd[:, :], self.rstd[:, :], ACT.Sqrt).then_inc(self.std_ready, 1)

    def scale(self, dve, dst, src, n):
        nc = self.nc
        dve.wait_ge(self.std_ready, n + 1)
        nc.vector.reciprocal(self.rstd[:, :], self.rstd[:, :]).then_inc(self.rstd_ready, 1)
        dve.wait_ge(self.rstd_ready, n + 1)
        nc.vector.tensor_scalar(dst, src, self.mv[:, 0:1], self.rstd[:, 0:1], ALU.subtract, ALU.mult).then_inc(self.scaled_ready, 1)

    def apply(self, pool, buf, n):
        nc = self.nc
        pool.wait_ge(self.scaled_ready, n + 1)
        nc.gpsimd.tensor_tensor(buf, buf, self.gain, ALU.mult).then_inc(self.gained_ready, 1)
        pool.wait_ge(self.gained_ready, n + 1)
        nc.gpsimd.tensor_tensor(buf, buf, self.bias, ALU.add).then_inc(self.done_ready, 1)


def phase_out(nc, m, io, T, layer):
    shared = layer == 0
    source = io["mixed" if shared else "gated"]
    w_out_src = io["a_w_out" if shared else "b_w_out"][0]
    with ExitStack() as ctx:
        def sb(name, shape):
            return ctx.enter_context(nc.sbuf_tensor(f"out{layer}_" + name, shape, F32))

        sems = []

        def sem(name):
            sems.append(ctx.enter_context(nc.semaphore(f"out{layer}_" + name)))
            return sems[-1]

        w_out, w_gate, w_kv = sb("w_out", [P, NB, D]), sb("w_gate", [P, NB, D]), sb("w_kv", [P, NB, HALF])
        w_proj = sb("w_proj", [P, PLE // P, D])
        par = sb("par", [P, 4, D])
        y = sb("y", [P, D])
        x, z = ([sb(f"{n}{i}", [P, D]) for i in range(2)] for n in ("x", "z"))
        p = [sb(f"p{i}", [P, PLE]) for i in range(2)]
        yT, zT, cT, pT = sb("yT", [P, NB, P]), sb("zT", [P, NB, P]), sb("cT", [P, NB, P]), sb("pT", [P, PLE // P, P])
        sig, c, kv = sb("sig", [P, D]), sb("c", [P, D]), sb("kv", [P, HALF])

        bank = lambda name: ctx.enter_context(nc.psum_tensor(f"out{layer}_" + name, [P, 512], F32))
        pout, pgate, pturn = ([bank(f"{n}{i}") for i in range(2)] for n in ("pout", "pgate", "pturn"))
        pproj, pkv = bank("pproj"), bank("pkv")

        w_loaded, y_loaded = sem("w_loaded"), sem("y_loaded")
        xp_loaded = [sem(f"xp_loaded{i}") for i in range(2)]
        turn_filled, turn_taken = sem("turn_filled"), sem("turn_taken")
        out_filled, z_ready = sem("out_filled"), sem("z_ready")
        gate_filled, sig_ready, proj_filled, u_ready, x1_ready = (
            sem(n) for n in ("gate_filled", "sig_ready", "proj_filled", "u_ready", "x1_ready"))
        kv_filled, kv_ready, kv_stored = sem("kv_filled"), sem("kv_ready"), sem("kv_stored")
        x1_stored = [sem(f"x1_stored{i}") for i in range(2)]
        norm = Norm(nc, sb, sem, "ln", par[:, 0, :], par[:, 1, :])
        kv_norm = Norm(nc, sb, sem, "kvln", par[:, 2, :], par[:, 3, :])

        def has(t):
            return not isinstance(t, int) or 0 <= t <= T

        def has_kv(t):
            return shared and has(t)

        def order(t):
            return ((["c0", "c1"] if has_kv(t - 2) else []) + (["z0", "z1", "p0", "p1"] if has(t - 1) else [])
                    + (["y0", "y1"] if has(t + 1) else []))

        turns = Uses(order)
        FIRST = 2

        def turned(t, what):
            return turns.before(t, what) + (FIRST + 1)

        ctx.callback(clear_semaphores, nc, sems)
        block = ctx.enter_context(nc.Block())

        @block.sync
        def _(sp):
            def load_y(t):
                sp.dma_start(y[:, :], source[rows(t), :]).then_inc(y_loaded, 16)

            def load_xp(t, par_):
                sample = is_sample(t, T)
                src = (io["x1"][rows(t), :] if not shared else io["x_sample"].rearrange("b i d -> (b i) d") if sample
                       else io["x_prompt"][0][rows(t), :])
                sp.dma_start(x[par_][:, :], src).then_inc(xp_loaded[par_], 16)
                src = io["p_sample"][layer].rearrange("b i d -> (b i) d") if sample else io["p_prompt"][layer, 0][rows(t), :]
                sp.dma_start(p[par_][:, :], src).then_inc(xp_loaded[par_], 16)

            load_y(0)
            blocks = lambda w: w.rearrange("(j p) n -> p j n", p=P)
            for h in range(2):
                cols = slice(h * HALF, (h + 1) * HALF)
                sp.dma_start(w_out[:, :, cols], blocks(w_out_src)[:, :, cols]).then_inc(w_loaded, 16)
            load_xp(0, 0)
            load_xp(1, 1)
            for i, v in enumerate((io["ln_g"][layer:layer + 1, :], io["ln_b"][layer:layer + 1, :], io["kv_ln_g"].unsqueeze(0), io["kv_ln_b"].unsqueeze(0))):
                sp.dma_start(par[:, i, :], v.to_broadcast([P, D])).then_inc(w_loaded, 16)
            sp.dma_start(w_gate[:, :, :], blocks(io["ple_w_gate"][layer])).then_inc(w_loaded, 16)
            sp.dma_start(w_proj[:, :, :], blocks(io["ple_w_proj"][layer])).then_inc(w_loaded, 16)
            sp.dma_start(w_kv[:, :, :], blocks(io["w_kv"])).then_inc(w_loaded, 16)

            def step(t, par_):
                if has(t + 1):
                    wait(sp, turn_filled, FIRST if isinstance(t, int) and t == 0 else turned(t - 1, "y1"))
                    load_y(t + 1)
                if has(t - 1) and not (isinstance(t, int) and t == 0):
                    if has(t + 1):
                        sp.wait_ge(turn_filled, turned(t, "p1"))
                        load_xp(t + 1, 1 - par_)
                    sp.wait_ge(x1_ready, t)
                    dst = (io["x1"][rows(t - 1), :] if shared else io["y_sample"].rearrange("b i d -> (b i) d")
                           if is_sample(t - 1, T) else io["y_prompt"][0][rows(t - 1), :])
                    sp.dma_start(dst, z[1 - par_][:, :]).then_inc(x1_stored[1 - par_], 16)
                if has_kv(t - 2):
                    sp.wait_ge(kv_ready, t - 1)
                    sp.dma_start(io["kv"][rows(t - 2), :], kv[:, :]).then_inc(kv_stored, 16)
                    if isinstance(t, int) and t in (T + 1, T + 2):
                        for i, name in enumerate(("prompt_k", "prompt_v") if t == T + 1 else ("sample_k", "sample_v")):
                            dst = io[name].rearrange("a b h d -> (a b) (h d)")
                            sp.dma_start(dst, kv[:, i * 256:(i + 1) * 256]).then_inc(kv_stored, 16)

            iterations(sp, T, step)
            if shared:
                sp.wait_ge(kv_stored, 16 * (T + 1) + 64)
            sp.wait_ge(x1_stored[0], 16 * (T // 2 + 1))
            sp.wait_ge(x1_stored[1], 16 * (T // 2))

        @block.tensor
        def _(pe):
            def turn(src, n, i, value):
                wait(pe, turn_taken, value - 2)
                for k in range(n):
                    j = i * n + k
                    last = nc.tensor.transpose(pturn[i][:, k * P:(k + 1) * P], src[:, j * P:(j + 1) * P], m["ident"])
                last.then_inc(turn_filled, 1)

            def step(t, par_):
                for h in range(2):
                    if has(t):
                        if h == 0:
                            pe.wait_ge(turn_taken, FIRST if isinstance(t, int) and t == 0 else turned(t - 1, "y1"))
                        if isinstance(t, int) and t == 0:
                            pe.wait_ge(w_loaded, 16 * 9)
                        wait(pe, z_ready, t * 2 - (1 - h))
                        gemm(nc, pout[h][:, :], yT, w_out, slice(h * HALF, (h + 1) * HALF)).then_inc(out_filled, 1)
                    if h == 0 and has_kv(t - 2):
                        pe.wait_ge(kv_norm.done_ready, t - 1)
                        for i in range(2):
                            turn(c, HB, i, turned(t, f"c{i}"))
                if has(t - 1):
                    pe.wait_ge(norm.done_ready, t)
                    for i in range(2):
                        turn(z[1 - par_], HB, i, turned(t, f"z{i}"))
                if has_kv(t - 2):
                    pe.wait_ge(turn_taken, turned(t, "c1"))
                    wait(pe, kv_ready, t - 2)
                    gemm(nc, pkv[:, :], cT, w_kv, slice(0, HALF)).then_inc(kv_filled, 1)
                if has(t - 1):
                    pe.wait_ge(xp_loaded[1 - par_], of_parity(t - 1, 1 - par_, 32) + 32)
                    for i in range(2):
                        turn(p[1 - par_], 1, i, turned(t, f"p{i}"))
                for h in range(2):
                    cols = slice(h * HALF, (h + 1) * HALF)
                    if has(t - 1):
                        pe.wait_ge(turn_taken, turned(t, "z1"))
                        wait(pe, sig_ready, t * 2 - (3 - h))
                        gemm(nc, pgate[h][:, :], zT, w_gate, cols).then_inc(gate_filled, 1)
                        pe.wait_ge(turn_taken, turned(t, "p1"))
                        wait(pe, u_ready, t * 2 - (2 - h))
                        gemm(nc, pproj[:, :], pT, w_proj, cols).then_inc(proj_filled, 1)
                    if has(t + 1):
                        if h == 0:
                            pe.wait_ge(y_loaded, t * 16 + 32)
                        turn(y, HB, h, turned(t, f"y{h}"))

            pe.wait_ge(y_loaded, 16)
            for i in range(2):
                turn(y, HB, i, i + 1)
            iterations(pe, T, step)

        @block.scalar
        def _(act):
            def take(dst, i, n, value):
                act.wait_ge(turn_filled, value)
                nc.scalar.copy(dst[:, i * n:(i + 1) * n, :].rearrange("p j t -> p (j t)"), pturn[i][:, 0:n * P]).then_inc(turn_taken, 1)

            def step(t, par_):
                for name, dst, n, here in (("c", cT, HB, has_kv(t - 2)), ("z", zT, HB, has(t - 1))):
                    if here:
                        for i in range(2):
                            take(dst, i, n, turned(t, f"{name}{i}"))
                if has_kv(t - 2):
                    act.wait_ge(kv_filled, t - 1)
                    wait(act, kv_stored, t * 16 - 32 + (32 if is_sample(t - 2, T) else 0))
                    nc.scalar.copy(kv[:, :], pkv[:, :]).then_inc(kv_ready, 1)
                if has(t - 1):
                    for i in range(2):
                        take(pT, i, 1, turned(t, f"p{i}"))
                if has(t):
                    norm.root(act, t)
                for h in range(2):
                    if has(t - 1):
                        act.wait_ge(gate_filled, t * 2 - (1 - h))
                        wait(act, x1_ready, t - 1)
                        nc.scalar.activation(sig[:, h * HALF:(h + 1) * HALF], pgate[h][:, :], ACT.Sigmoid).then_inc(sig_ready, 1)
                    if has(t + 1):
                        take(yT, h, HB, turned(t, f"y{h}"))
                if has_kv(t - 1):
                    kv_norm.root(act, t - 1)

            for i in range(2):
                take(yT, i, HB, i + 1)
            iterations(act, T, step)

        @block.gpsimd
        def _(pool):
            pool.wait_ge(w_loaded, 16 * 9)

            def step(t, par_):
                if has(t):
                    norm.apply(pool, z[par_][:, :], t)
                if has_kv(t - 1):
                    kv_norm.apply(pool, c[:, :], t - 1)

            iterations(pool, T, step)

        @block.vector
        def _(dve):
            def step(t, par_):
                if has(t):
                    dve.wait_ge(xp_loaded[par_], of_parity(t, par_, 32) + 32)
                    wait(dve, x1_stored[par_], of_parity(t, par_, 16))
                    if shared:
                        wait(dve, kv_norm.scaled_ready, t - 1)
                    for h in range(2):
                        cols = slice(h * HALF, (h + 1) * HALF)
                        dve.wait_ge(out_filled, t * 2 + (h + 1))
                        nc.vector.scalar_tensor_tensor(out=z[par_][:, cols], in0=x[par_][:, cols], scalar=ALPHA,
                                                       in1=pout[h][:, :], op0=ALU.mult, op1=ALU.add).then_inc(z_ready, 1)
                    dve.wait_ge(z_ready, t * 2 + 2)
                    norm.statistics(dve, z[par_], t)
                    norm.scale(dve, z[par_][:, :], z[par_][:, :], t)
                if has(t - 1):
                    for h in range(2):
                        cols = slice(h * HALF, (h + 1) * HALF)
                        dve.wait_ge(proj_filled, t * 2 - (1 - h))
                        dve.wait_ge(sig_ready, t * 2 - (1 - h))
                        nc.vector.tensor_tensor(sig[:, cols], sig[:, cols], pproj[:, :], ALU.mult).then_inc(u_ready, 1)
                    dve.wait_ge(u_ready, t * 2)
                    zb = z[1 - par_]
                    nc.vector.tensor_tensor(zb[:, :], zb[:, :], sig[:, :], ALU.add).then_inc(x1_ready, 1)
                if has_kv(t - 1):
                    dve.wait_ge(x1_ready, t)
                    kv_norm.statistics(dve, zb, t - 1)
                    wait(dve, turn_filled, turned(t, "c1") if has_kv(t - 2) else 0)
                    kv_norm.scale(dve, c[:, :], zb[:, :], t - 1)

            iterations(dve, T, step)


def phase_out_a(nc, m, io, T):
    phase_out(nc, m, io, T, 0)


def phase_out_b(nc, m, io, T):
    phase_out(nc, m, io, T, 1)


PAIRS = NH // 2
KEYS = P + DSEQ



def head_of(i, c):
    return i // 2 * 4 + c * 2 + i % 2


SLOPES = [2.0 ** (-8.0 * (h + 1) / NH) for h in range(NH)]


def attention_constants():
    import numpy as np
    q, k = np.arange(P)[:, None], np.arange(2 * P)[None, :] - P
    age = q // 64 - k // 64
    near = np.where((age >= 0) & (age <= 2), -np.abs(q - k), -1e30).astype(np.float32)
    row = np.arange(P)
    head = (row // DSEQ * 2)[:, None, None] + np.arange(2)[None, :, None]
    dist = np.abs((row % DSEQ)[:, None, None] + P - np.arange(KEYS)[None, None, :])
    bias = (-np.array(SLOPES)[head] * dist).astype(np.float32)
    return {"near": near, "sample_bias": np.ascontiguousarray(bias)}


def phase_b(nc, m, io, T):
    with ExitStack() as ctx:
        def sb(name, shape):
            return ctx.enter_context(nc.sbuf_tensor("b_" + name, shape, F32))

        sems = []

        def sem(name):
            sems.append(ctx.enter_context(nc.semaphore("b_" + name)))
            return sems[-1]

        twice = lambda name, shape: [sb(f"{name}{i}", shape) for i in range(2)]
        w = sb("w", [P, NB, 2 * D])
        near, sample_bias = sb("near", [P, 2 * P]), sb("sample_bias", [P, 2, KEYS])
        sink, neg_sink = twice("sink", [P, 4, 2, 2]), twice("neg_sink", [P, 4, 2, 2])
        x, xT = sb("x", [P, D]), sb("xT", [P, NB, P])
        kd = sb("kd", [P, 4, 2, HD])
        kT, v = twice("kT", [P, 4, P]), twice("v", [P, 4 * HD])
        qT, gate, y = twice("qT", [P, NB, P]), twice("gate", [P, D]), twice("y", [P, D])
        th = sb("th", [P, HALF])
        s, pT = twice("s", [P, 2, 2 * P]), twice("pT", [P, 4, P])
        mx, nm, den = sb("mx", [P, 2]), sb("nm", [P, 4, 2, 2]), sb("den", [P, 4, 2, 2])
        sunk, rden = sb("sunk", [P, 4, 2, 2]), sb("rden", [P, 4, 2, 2])
        each = lambda name, shape: [sb(f"{name}{i}", shape) for i in range(DEC)]
        kd_c, kd_n = each("kd_c", [P, 4, 2, HD]), each("kd_n", [DSEQ, 4, 2, HD])
        v_c, v_n, kT_s = each("v_c", [P, 4 * HD]), each("v_n", [DSEQ, 4 * HD]), each("kT_s", [P, 4, KEYS])

        bank = lambda name: ctx.enter_context(nc.psum_tensor("b_" + name, [P, 512], F32))
        ps, pturn, po = ([bank(f"{n}{i}") for i in range(2)] for n in ("ps", "pturn", "po"))
        pq, pg = bank("pq"), bank("pg")

        w_loaded, const_loaded, x_loaded, k_loaded, v_loaded = (
            sem(n + "_loaded") for n in ("w", "const", "x", "k", "v"))
        request_loaded = [sem(f"request_loaded{i}") for i in range(DEC)]
        neg_ready = sem("neg_ready")
        turn_filled, turn_taken = sem("turn_filled"), sem("turn_taken")
        q_filled, q_ready, gate_filled, th_ready, gate_ready = (
            sem(n) for n in ("q_filled", "q_ready", "gate_filled", "th_ready", "gate_ready"))
        s_filled, s_ready, mx_ready, nm_ready, e_ready, pv_filled = (
            sem(n) for n in ("s_filled", "s_ready", "mx_ready", "nm_ready", "e_ready", "pv_filled"))
        sum_ready, sunk_ready, den_ready, rden_ready, o_ready, y_ready = (
            sem(n) for n in ("sum_ready", "sunk_ready", "den_ready", "rden_ready", "o_ready", "y_ready"))
        attended_stored, attended_loaded = sem("attended_stored"), sem("attended_loaded")
        y_stored = [sem(f"y_stored{i}") for i in range(2)]

        def prompt(t):
            return not isinstance(t, int) or 0 <= t < T

        def order(t):
            if not isinstance(t, int) or t < T:
                return ([f"p{i}" for i in range(PAIRS)] + (["k0", "k1"] if prompt(t + 1) else [])
                        + (["x0", "x1"] if prompt(t + 1) else []))
            names = []
            for i in range(DEC + 3):
                names += [f"kc{i}", f"kn{i}"] if i < DEC else []
                names += [f"pc{i - 3}", f"pn{i - 3}"] if i >= 3 else []
            return names

        def flat(a):
            return a[:, :, :, :].rearrange("p g c h -> p (g c h)")

        def lined(q):
            return q[:, :, :].rearrange("p j t -> p (j t)")

        turns = Uses(order)
        FIRST = 6

        def turned(t, what):
            if isinstance(t, int) and t < 0:
                return {"x1": FIRST, "k1": 4}[what]
            return turns.before(t, what) + (FIRST + 1)

        ctx.callback(clear_semaphores, nc, sems)
        block = ctx.enter_context(nc.Block())

        @block.sync
        def _(sp):
            def load_x(t):
                sp.dma_start(x[:, :], io["x1"][rows(t), :]).then_inc(x_loaded, 16)

            def load_keys(dst, src, loaded):
                for c in range(2):
                    sp.dma_start(dst[:, :, c, :], src.rearrange("n (g d) -> n g d", d=HD)).then_inc(loaded, 16)

            def load_v(t, par_):
                sp.dma_start(v[par_][:, :], io["kv"][rows(t), 4 * HD:8 * HD]).then_inc(v_loaded, 16)

            load_x(0)
            wv = io["b_w_in"][0].rearrange("(j p) n -> p j n", p=P)
            for i in range(2):
                cols = slice(i * HALF, (i + 1) * HALF)
                sp.dma_start(w[:, :, cols], wv[:, :, cols]).then_inc(w_loaded, 16)
            load_keys(kd, io["kv"][rows(0), 0:4 * HD], k_loaded)
            load_v(0, 0)
            sp.dma_start(w[:, :, D:2 * D], wv[:, :, D:2 * D]).then_inc(w_loaded, 16)
            sp.dma_start(near[:, :], io["near"]).then_inc(const_loaded, 16)
            sp.dma_start(sample_bias[:, :, :], io["sample_bias"]).then_inc(const_loaded, 16)
            sp.dma_start(flat(sink[0]), io["b_sinks"].to_broadcast([P, NH])).then_inc(const_loaded, 16)
            for r in range(PAIRS):
                sp.dma_start(flat(sink[1])[r * DSEQ:(r + 1) * DSEQ, :].rearrange("t (b c) -> t b c", c=2),
                             io["b_sinks"][:, 2 * r:2 * r + 2].unsqueeze(1).to_broadcast([DSEQ, DEC, 2])).then_inc(const_loaded, 16)
            sp.wait_ge(turn_filled, 2)
            load_x(1)

            def load_request(b):
                new = slice(T * P + b * DSEQ, T * P + (b + 1) * DSEQ)
                load_keys(kd_c[b], io["cache_k"][b].rearrange("n g d -> n (g d)"), request_loaded[b])
                load_keys(kd_n[b], io["kv"][new, 0:4 * HD], request_loaded[b])
                sp.dma_start(v_c[b][:, :], io["cache_v"][b].rearrange("n g d -> n (g d)")).then_inc(request_loaded[b], 16)
                sp.dma_start(v_n[b][:, :], io["kv"][new, 4 * HD:8 * HD]).then_inc(request_loaded[b], 16)

            for b in range(DEC):
                load_request(b)

            def step(t, par_):
                if is_sample(t, T):
                    sp.wait_ge(o_ready, t * 2 + 2)
                    att = io["attended"].rearrange("(b t) (r c) -> r t b c", t=DSEQ, c=P)
                    for r in range(PAIRS):
                        sp.dma_start(att[r], y[par_][r * DSEQ:(r + 1) * DSEQ, :].rearrange("t (b c) -> t b c", c=P)).then_inc(attended_stored, 16)
                    sp.wait_ge(attended_stored, 16 * PAIRS)
                    sp.dma_start(x[:, :], io["attended"]).then_inc(attended_loaded, 16)
                else:
                    if prompt(t + 1):
                        wait(sp, turn_filled, turned(t - 1, "k1"))
                        load_keys(kd, io["kv"][rows(t + 1), 0:4 * HD], k_loaded)
                        wait(sp, turn_filled, turned(t - 1, "x1"))
                        load_x(t + 2)
                        sp.wait_ge(pv_filled, t * PAIRS + PAIRS)
                        load_v(t + 1, 1 - par_)
                sp.wait_ge(y_ready, t * 2 + 2)
                sp.dma_start(io["gated"][rows(t), :], y[par_][:, :]).then_inc(y_stored[par_], 16)

            tiles(sp, T, step)
            sp.wait_ge(y_stored[0], 16 * (T // 2 + 1))
            sp.wait_ge(y_stored[1], 16 * (T // 2))

        @block.tensor
        def _(pe):
            def turn(i, pieces, value):
                wait(pe, turn_taken, value - 2)
                for src, n, col in pieces:
                    last = nc.tensor.transpose(pturn[i][0:src.shape[1], col:col + n], src, m["ident"][0:n, 0:n])
                last.then_inc(turn_filled, 1)

            def turn_x(t, value):
                pe.wait_ge(x_loaded, t * 16 + 16)
                for i in range(2):
                    turn(i, [(x[:, (i * HB + j) * P:(i * HB + j + 1) * P], P, j * P) for j in range(HB)], value + (i - 1))

            def keys(kd_, g):
                return kd_[:, g, :, :].rearrange("n c d -> n (c d)")

            def turn_k(t, value):
                pe.wait_ge(k_loaded, t * 32 + 32)
                for i in range(2):
                    turn(i, [(keys(kd, 2 * i + g), P, g * P) for g in range(2)], value + (i - 1))

            def q_block(t, i):
                if i % HB == 0:
                    wait(pe, q_ready, t * 2 + i // HB)
                out = pq[:, i % HB * P:(i % HB + 1) * P]
                for j in range(NB):
                    last = nc.tensor.matmul(out, w[:, j, i * P:(i + 1) * P], xT[:, j, :], start=(j == 0), stop=(j == NB - 1))
                if i % HB == HB - 1:
                    last.then_inc(q_filled, 1)

            def gate_piece(t, i):
                h, first = i // HB, i % HB * 2
                if first == 0:
                    wait(pe, gate_ready, t * 2 + h)
                for j in (first, first + 1):
                    last = nc.tensor.matmul(pg[:, :], xT[:, j, :], w[:, j, D + h * HALF:D + (h + 1) * HALF],
                                            start=(j == 0), stop=(j == NB - 1))
                if j == NB - 1:
                    last.then_inc(gate_filled, 1)

            def scores(t, par_, i):
                wait(pe, s_ready, t * 2 * PAIRS + (i * 2 - 2))
                if i == 0:
                    pe.wait_ge(q_ready, t * 2 + 2)
                    pe.wait_ge(turn_taken, turned(t - 1, "k1"))
                half = slice(i % 2 * HD, (i % 2 + 1) * HD)
                for c in range(2):
                    for ring, at in ((1 - par_, 0), (par_, P)):
                        if at == 0 and isinstance(t, int) and t == 0:
                            continue
                        last = nc.tensor.matmul(ps[i % 2][:, c * 2 * P + at:c * 2 * P + at + P], qT[par_][half, i // 2 * 2 + c, :],
                                                kT[ring][half, i // 2, :], start=True, stop=True)
                last.then_inc(s_filled, 1)

            def weighted(t, par_, i):
                if i == 0:
                    pe.wait_ge(v_loaded, t * 16 + 16)
                if i % HB == 0:
                    wait(pe, o_ready, t * 2 + (i // HB - 1))
                pe.wait_ge(turn_taken, turned(t, f"p{i}"))
                first = isinstance(t, int) and t == 0
                for c in range(2):
                    col = head_of(i, c) % HH * HD
                    for k, ring in enumerate((1 - par_, par_)):
                        if k == 0 and first:
                            continue
                        last = nc.tensor.matmul(po[i // HB][:, col:col + HD], pT[i % 2][:, c * 2 + k, :],
                                                v[ring][:, i // 2 * HD:(i // 2 + 1) * HD], start=(k == 0 or first), stop=(k == 1))
                last.then_inc(pv_filled, 1)

            def prompt_step(t, par_):
                for i in range(PAIRS + 2):
                    if i < PAIRS:
                        scores(t, par_, i)
                    if 1 <= i <= PAIRS:
                        n = i - 1
                        pe.wait_ge(e_ready, t * 2 * PAIRS + (n * 2 + 2))
                        first = isinstance(t, int) and t == 0
                        turn(turns.bank(t, f"p{n}"), [(s[n % 2][:, c, k * P:(k + 1) * P], P, (c * 2 + k) * P)
                                                     for c in range(2) for k in range(1 if first else 0, 2)], turned(t, f"p{n}"))
                    if i < PAIRS:
                        if i == 0:
                            pe.wait_ge(turn_taken, turned(t - 1, "x1"))
                        q_block(t + 1, i)
                    if 2 <= i < PAIRS + 1:
                        weighted(t, par_, i - 2)
                    if i < PAIRS:
                        gate_piece(t + 1, i)
                    if prompt(t + 1):
                        if i == PAIRS:
                            turn_k(t + 1, turned(t, "k1"))
                        if i == PAIRS + 1:
                            turn_x(t + 2, turned(t, "x1"))
                weighted(t, par_, PAIRS - 1)

            def sample_step(t, par_):
                for i in range(DEC + 4):
                    if i < DEC:
                        pe.wait_ge(request_loaded[i], 96)
                        turn(turns.bank(t, f"kc{i}"), [(keys(kd_c[i], g), P, g * P) for g in range(4)], turned(t, f"kc{i}"))
                        turn(turns.bank(t, f"kn{i}"), [(keys(kd_n[i], g), DSEQ, g * DSEQ) for g in range(4)], turned(t, f"kn{i}"))
                    u = i - 2
                    if 0 <= u < PAIRS:
                        half, requests = slice(u % 2 * HD, (u % 2 + 1) * HD), (u // 2 * 2, u // 2 * 2 + 1)
                        pe.wait_ge(s_ready, t * 2 * PAIRS + u * 2 - 2)
                        if u == 0:
                            pe.wait_ge(q_ready, t * 2 + 2)
                        pe.wait_ge(turn_taken, turned(t, f"kn{requests[1]}"))
                        for c, b in enumerate(requests):
                            for g in range(4):
                                last = nc.tensor.matmul(ps[u % 2][g * 32:(g + 1) * 32, c * KEYS:(c + 1) * KEYS],
                                                        lined(qT[par_])[half, (4 * b + g) * 32:(4 * b + g + 1) * 32],
                                                        kT_s[b][half, g, :], start=True, stop=True)
                        last.then_inc(s_filled, 1)
                    u = i - 3
                    if 0 <= u < PAIRS:
                        pe.wait_ge(e_ready, t * 2 * PAIRS + u * 2 + 2)
                        e = lined(s[u % 2])
                        turn(turns.bank(t, f"pc{u}"), [(e[:, c * KEYS:c * KEYS + P], P, c * P) for c in range(2)], turned(t, f"pc{u}"))
                        turn(turns.bank(t, f"pn{u}"), [(e[:, c * KEYS + P:(c + 1) * KEYS], P, c * P) for c in range(2)], turned(t, f"pn{u}"))
                    u = i - 4
                    if 0 <= u < PAIRS:
                        if u % HB == 0:
                            pe.wait_ge(o_ready, t * 2 + u // HB - 1)
                        pe.wait_ge(turn_taken, turned(t, f"pn{u}"))
                        for c in range(2):
                            b, col = u // 2 * 2 + c, head_of(u, c) % HH * HD
                            for g in range(4):
                                mine, of_g = slice(g * 32, (g + 1) * 32), slice(g * HD, (g + 1) * HD)
                                out = po[u // HB][mine, col:col + HD]
                                nc.tensor.matmul(out, pT[u % 2][:, c, mine], v_c[b][:, of_g], start=True, stop=False)
                                last = nc.tensor.matmul(out, pT[u % 2][0:DSEQ, 2 + c, mine], v_n[b][:, of_g], start=False, stop=True)
                        last.then_inc(pv_filled, 1)

            turn_x(0, 2)
            turn_k(0, 4)
            pe.wait_ge(turn_taken, 2)
            pe.wait_ge(w_loaded, 16 * 2)
            for i in range(NB):
                q_block(0, i)
            pe.wait_ge(w_loaded, 16 * 3)
            for i in range(NB):
                gate_piece(0, i)
            turn_x(1, FIRST)
            tiles(pe, T, lambda t, par_: sample_step(t, par_) if is_sample(t, T) else prompt_step(t, par_))

        @block.scalar
        def _(act):
            def take(i, pieces, value):
                act.wait_ge(turn_filled, value)
                for dst, src in pieces:
                    last = nc.scalar.copy(dst, src)
                last.then_inc(turn_taken, 1)

            def take_x(value):
                for i in range(2):
                    take(i, [(xT[:, i * HB:(i + 1) * HB, :].rearrange("p j t -> p (j t)"), pturn[i][:, :])], value + (i - 1))

            def take_k(par_, value):
                for i in range(2):
                    take(i, [(kT[par_][:, 2 * i:2 * i + 2, :].rearrange("p g t -> p (g t)"), pturn[i][:, 0:2 * P])], value + (i - 1))

            def take_q(t, par_, h):
                act.wait_ge(q_filled, t * 2 + (h + 1))
                dst, src = qT[par_][:, h * HB:(h + 1) * HB, :], pq[:, :].rearrange("p (j t) -> p j t", t=P)
                if is_sample(t, T):
                    dst = lined(qT[par_]).rearrange("p (b j t) -> p j b t", b=DEC, t=DSEQ)[:, h * HB:(h + 1) * HB]
                    src = src.rearrange("p j (b t) -> p j b t", t=DSEQ)
                nc.scalar.activation(dst, src, ACT.Copy,
                                     scale=HD ** -0.5).then_inc(q_ready, 1)

            def gate_tanh(t, h):
                act.wait_ge(gate_filled, t * 2 + (h + 1))
                wait(act, gate_ready, t * 2 + h)
                nc.scalar.activation(th[:, :], pg[:, :], ACT.Tanh, scale=0.5).then_inc(th_ready, 1)

            def exps(t, i, keys):
                act.wait_ge(nm_ready, t * PAIRS + (i + 1))
                for c in range(2):
                    nc.scalar.activation(keys[c], keys[c], ACT.Exp, bias=flat(nm)[:, head_of(i, c):head_of(i, c) + 1],
                                         accum_out=flat(den)[:, head_of(i, c):head_of(i, c) + 1]).then_inc(e_ready, 1)

            def exp_sinks(t):
                act.wait_ge(sum_ready, t + 1)
                nc.scalar.activation(flat(sunk), flat(sunk), ACT.Exp).then_inc(sunk_ready, 1)

            def prompt_step(t, par_):
                first = isinstance(t, int) and t == 0
                for i in range(PAIRS + 1):
                    if i in (HB, PAIRS):
                        gate_tanh(t + 1, i // HB - 1)
                    if i >= 1:
                        n = i - 1
                        if n >= 2:
                            act.wait_ge(pv_filled, t * PAIRS + (n - 1))
                        else:
                            wait(act, pv_filled, t * PAIRS + (n - 1) if not first else 0)
                        b = turns.bank(t, f"p{n}")
                        pieces = ([(pT[n % 2][:, c * 2 + 1, :], pturn[b][:, (c * 2 + 1) * P:(c * 2 + 2) * P]) for c in range(2)] if first
                                  else [(pT[n % 2][:, :, :].rearrange("p k t -> p (k t)"), pturn[b][:, :])])
                        take(b, pieces, turned(t, f"p{n}"))
                    if i < PAIRS:
                        exps(t, i, [s[i % 2][:, c, P if first else 0:] for c in range(2)])
                    if i in (HB - 1, PAIRS - 1):
                        take_q(t + 1, 1 - par_, i // HB)
                exp_sinks(t)
                if prompt(t + 1):
                    take_k(1 - par_, turned(t, "k1"))
                    take_x(turned(t, "x1"))

            def sample_step(t, par_):
                for i in range(DEC + 3):
                    if i < DEC:
                        b, k = turns.bank(t, f"kc{i}"), kT_s[i]
                        take(b, [(k[:, :, 0:P], pturn[b][:, :].rearrange("p (g n) -> p g n", n=P))], turned(t, f"kc{i}"))
                        b = turns.bank(t, f"kn{i}")
                        take(b, [(k[:, :, P:KEYS], pturn[b][:, 0:4 * DSEQ].rearrange("p (g n) -> p g n", n=DSEQ))], turned(t, f"kn{i}"))
                    n = i - 3
                    if n >= 0:
                        b = turns.bank(t, f"pc{n}")
                        act.wait_ge(pv_filled, t * PAIRS + n - 1)
                        take(b, [(pT[n % 2][:, 0:2, :].rearrange("p c t -> p (c t)"), pturn[b][:, 0:2 * P])], turned(t, f"pc{n}"))
                        b = turns.bank(t, f"pn{n}")
                        take(b, [(pT[n % 2][0:DSEQ, 2:4, :].rearrange("p c t -> p (c t)"), pturn[b][0:DSEQ, 0:2 * P])], turned(t, f"pn{n}"))
                    n = i - 2
                    if 0 <= n < PAIRS:
                        exps(t, n, [lined(s[n % 2])[:, c * KEYS:(c + 1) * KEYS] for c in range(2)])
                exp_sinks(t)

            take_x(2)
            take_k(0, 4)
            for h in range(2):
                take_q(0, 0, h)
            for h in range(2):
                gate_tanh(0, h)
            take_x(FIRST)
            tiles(act, T, lambda t, par_: sample_step(t, par_) if is_sample(t, T) else prompt_step(t, par_))

        @block.vector
        def _(dve):
            def make_gate(t, par_, h):
                dve.wait_ge(th_ready, t * 2 + (h + 1))
                wait(dve, y_ready, t * 2 - 2 if not isinstance(t, int) or t > 1 else 0)
                nc.vector.scalar_tensor_tensor(out=gate[par_][:, h * HALF:(h + 1) * HALF], in0=th[:, :], scalar=1.0,
                                               in1=pg[:, :], op0=ALU.add, op1=ALU.mult).then_inc(gate_ready, 1)

            def maximum(t, i, keys, kind):
                dve.wait_ge(s_ready, t * 2 * PAIRS + (i * 2 + 2))
                wait(dve, nm_ready, t * PAIRS + i)
                nc.vector.tensor_reduce(mx[:, :], keys, X, ALU.max).then_inc(mx_ready, 1)
                dve.wait_ge(mx_ready, t * PAIRS + (i + 1))
                nc.vector.scalar_tensor_tensor(out=nm[:, i // 2, :, i % 2], in0=mx[:, :], scalar=-1.0, in1=neg_sink[kind][:, i // 2, :, i % 2],
                                               op0=ALU.mult, op1=ALU.min).then_inc(nm_ready, 1)

            def finish(t, par_, kind):
                dve.wait_ge(e_ready, t * 2 * PAIRS + 2 * PAIRS)
                nc.vector.tensor_tensor(flat(sunk), flat(nm), flat(sink[kind]), ALU.add).then_inc(sum_ready, 1)
                dve.wait_ge(sunk_ready, t + 1)
                nc.vector.tensor_tensor(flat(den), flat(den), flat(sunk), ALU.add).then_inc(den_ready, 1)
                dve.wait_ge(den_ready, t + 1)
                nc.vector.reciprocal(flat(rden), flat(den)).then_inc(rden_ready, 1)
                dve.wait_ge(rden_ready, t + 1)
                wait(dve, y_stored[par_], of_parity(t, par_, 16))
                for h in range(2):
                    dve.wait_ge(pv_filled, t * PAIRS + (h + 1) * HB)
                    scale = flat(rden)[:, h * HH:(h + 1) * HH].unsqueeze(2).to_broadcast([P, HH, HD])
                    nc.vector.tensor_tensor(y[par_][:, h * HALF:(h + 1) * HALF].rearrange("p (i d) -> p i d", d=HD),
                                            po[h][:, :].rearrange("p (i d) -> p i d", d=HD), scale, ALU.mult).then_inc(o_ready, 1)
                if kind == 1:
                    dve.wait_ge(attended_loaded, 16)
                for h in range(2):
                    cols = slice(h * HALF, (h + 1) * HALF)
                    dve.wait_ge(o_ready, t * 2 + (h + 1))
                    nc.vector.scalar_tensor_tensor(out=y[par_][:, cols], in0=(x if kind == 1 else y[par_])[:, cols], scalar=0.5,
                                                   in1=gate[par_][:, cols], op0=ALU.mult, op1=ALU.mult).then_inc(y_ready, 1)

            def prompt_step(t, par_):
                first = isinstance(t, int) and t == 0
                lo = P if first else 0
                for i in range(PAIRS):
                    n_turned = turned(t, f"p{i - 2}") if i >= 2 else (0 if first else turned(t - 1, f"p{PAIRS - 2 + i}"))
                    dve.wait_ge(s_filled, t * PAIRS + (i + 1))
                    wait(dve, turn_filled, n_turned)
                    for c in range(2):
                        nc.vector.scalar_tensor_tensor(out=s[i % 2][:, c, lo:], in0=near[:, lo:], scalar=SLOPES[head_of(i, c)],
                                                       in1=ps[i % 2][:, c * 2 * P + lo:(c + 1) * 2 * P], op0=ALU.mult,
                                                       op1=ALU.add).then_inc(s_ready, 1)
                    maximum(t, i, s[i % 2][:, :, lo:], 0)
                    if i == HB:
                        make_gate(t + 1, 1 - par_, 0)
                make_gate(t + 1, 1 - par_, 1)
                finish(t, par_, 0)

            def sample_step(t, par_):
                for b in range(DEC):
                    dve.wait_ge(s_filled, t * PAIRS + b + 1)
                    dve.wait_ge(turn_filled, turned(t, f"pn{b - 2}") if b >= 2 else turned(t - 1, f"p{PAIRS - 2 + b}"))
                    both = lambda a: a[:, 0:2 * KEYS].rearrange("p (c k) -> p c k", k=KEYS)
                    nc.vector.tensor_tensor(both(lined(s[b % 2])), both(ps[b % 2]),
                                            sample_bias[:, b % 2, :].unsqueeze(1).to_broadcast([P, 2, KEYS]), ALU.add).then_inc(s_ready, 2)
                    maximum(t, b, both(lined(s[b % 2])), 1)
                finish(t, par_, 1)

            dve.wait_ge(const_loaded, 16 * (3 + PAIRS))
            for kind in range(2):
                nc.vector.tensor_scalar(flat(neg_sink[kind]), flat(sink[kind]), -1.0, 0.0, ALU.mult, ALU.add).then_inc(neg_ready, 1)
            dve.wait_ge(neg_ready, 2)
            for h in range(2):
                make_gate(0, 0, h)
            tiles(dve, T, lambda t, par_: sample_step(t, par_) if is_sample(t, T) else prompt_step(t, par_))


INS = ["x_prompt", "x_sample", "p_prompt", "p_sample", "state_a_shift", "state_a_wkv", "cache_k", "cache_v",
       "a_mu", "a_w_in", "a_w0", "a_w_w1", "a_w_w2", "a_a0", "a_w_a1", "a_w_a2", "a_k_k", "a_k_a", "a_r_k",
       "a_gn_g", "a_gn_b", "a_w_out", "kv_ln_g", "kv_ln_b", "w_kv", "b_w_in", "b_sinks", "b_w_out",
       "ln_g", "ln_b", "ple_w_proj", "ple_w_gate"]


def outputs_of(seq):
    return [("y_prompt", (1, seq, D)), ("y_sample", (DEC, DSEQ, D)), ("prompt_shift", (1, 1, D)),
            ("prompt_wkv", (1, 1, NH, HD, HD)), ("prompt_k", (1, P, 4, HD)), ("prompt_v", (1, P, 4, HD)),
            ("sample_shift", (1, DEC, D)), ("sample_wkv", (1, DEC, NH, HD, HD)),
            ("sample_k", (DEC, DSEQ, 4, HD)), ("sample_v", (DEC, DSEQ, 4, HD))]


def scratch_of(n_rows):
    return [("factors", (n_rows, 4, NB, P)),
            ("tok_b", (n_rows, D)), ("tok_k", (n_rows, D)), ("tok_v", (n_rows, D)),
            ("gate_mul", (n_rows, D)), ("gate_add", (n_rows, D)), ("bonus", (n_rows, NH)),
            ("dec", (n_rows, NB, DEC)), ("mixed", (n_rows, D)), ("x1", (n_rows, D)),
            ("kv", (n_rows, 2 * 4 * HD)), ("attended", (P, D)), ("gated", (n_rows, D))]


def build(nc, io, seq, phases):
    T = seq // P
    with ExitStack() as ctx:
        m = Masks(nc, ctx)
        build_masks(nc, m)
        for phase in phases:
            phase(nc, m, io, T)


PHASES = [phase_a1, phase_a2, phase_a3, phase_a3_sample, phase_out_a, phase_b, phase_out_b]


def kernel(**inputs):
    import numpy as _np
    import concourse.bacc as _bacc
    from concourse.bass_utils import run_bass_kernel_spmd as _run

    nc = _bacc.Bacc("TRN2", target_bir_lowering=False, num_devices=1)
    arrays, io = {}, {}
    for name in INS:
        a = _np.ascontiguousarray(inputs[name])
        arrays["in_" + name] = a
        io[name] = nc.dram_tensor("in_" + name, a.shape, mybir.dt.from_np(a.dtype), kind="ExternalInput").ap()
    for name, a in attention_constants().items():
        arrays["in_" + name] = a
        io[name] = nc.dram_tensor("in_" + name, a.shape, F32, kind="ExternalInput").ap()
    seq = inputs["x_prompt"].shape[1]
    outs = outputs_of(seq)
    for name, shape in outs:
        io[name] = nc.dram_tensor("out_" + name, shape, F32, kind="ExternalOutput").ap()
    for name, shape in scratch_of(seq + P):
        io[name] = nc.dram_tensor(name, shape, F32).ap()
    build(nc, io, seq, PHASES)
    r = _run(nc, [arrays], core_ids=[0])
    return tuple(r.results[0]["out_" + name] for name, _ in outs)
```

```python
from contextlib import ExitStack

import concourse.bass as bass
from concourse import mybir

F32 = mybir.dt.float32
F16 = mybir.dt.float16
ALU = mybir.AluOpType
ACT = mybir.ActivationFunctionType
X = mybir.AxisListType.X

P = 128
D = 1024
NB = D // P
HALF = D // 2
HB = NB // 2
HD = 64
NH = D // HD
HH = NH // 2
RANK = 64
PLE = 256
DEC = 8
DSEQ = 16
ALPHA = (2.0 * 2) ** 0.25
LN_EPS = 1e-5
GN_EPS = 64e-5
DECAY = -(2.718281828459045 ** -0.5)


def wait(eng, sem, value):
    if isinstance(value, int) and value <= 0:
        return
    eng.wait_ge(sem, value)


def tiles(eng, prompt_tiles, step):
    pairs = prompt_tiles // 2
    step(0, 0)
    step(1, 1)
    if pairs > 2:
        with eng.Fori(1, pairs - 1) as p:
            step(p * 2, 0)
            step(p * 2 + 1, 1)
    step(prompt_tiles - 2, 0)
    step(prompt_tiles - 1, 1)
    step(prompt_tiles, 0)


def of_parity(t, par, each):
    return t // 2 * each if isinstance(t, int) else (t - par) * (each // 2)


def is_sample(t, prompt_tiles):
    return isinstance(t, int) and t == prompt_tiles


def rows(t):
    return bass.ds(t * P, P) if not isinstance(t, int) else slice(t * P, t * P + P)


def tile_of(t):
    return bass.ds(t, 1) if not isinstance(t, int) else slice(t, t + 1)


class Masks:

    NAMES = ["ident", "cum_incl", "cum_excl", "incl", "strict", "neg_lower",
             "s_cum_incl", "s_cum_excl", "s_incl", "s_strict", "s_neg_lower", "same",
             "lev1", "lev2", "lev4", "lev8", "lev16", "lev32", "lev64", "lev1T"]

    def __init__(self, nc, ctx):
        self.all = ctx.enter_context(nc.sbuf_tensor("masks", [P, len(self.NAMES), P], F32))
        self.totals = ctx.enter_context(nc.sbuf_tensor("totals", [P, 2], F32))
        self.seq_rows = ctx.enter_context(nc.sbuf_tensor("seq_rows", [P, DEC], F32))

    def __getitem__(self, name):
        return self.all[:, self.NAMES.index(name), :]


class MaskTools:

    def __init__(self, nc, pool, order):
        self.nc, self.pool, self.order, self.count = nc, pool, order, 0

    def link(self, ins):
        self.count += 1
        ins.then_inc(self.order, 1)
        self.pool.wait_ge(self.order, self.count)

    def keep(self, view, op, base, row, pattern, fill=0.0):
        self.link(self.nc.gpsimd.affine_select(out=view, in_=view, compare_op=op, fill=fill, base=base,
                                               pattern=pattern, channel_multiplier=row))


def build_masks(nc, m, pool, order):
    tools = MaskTools(nc, pool, order)
    link, keep = tools.link, tools.keep

    def within(view, size):
        return [[-size, view.shape[1]]] + [[0, n] for n in view.shape[2:]]

    link(nc.gpsimd.memset(m.all[:, :, :], 1.0))
    link(nc.gpsimd.memset(m.totals[:, :], 1.0))
    link(nc.gpsimd.memset(m.seq_rows[:, :], 1.0))
    line = [[1, P]]
    keep(m["ident"], ALU.is_equal, 0, -1, line)
    for name in ("same", "s_incl", "s_strict", "s_cum_incl", "s_cum_excl", "s_neg_lower"):
        v = m[name].rearrange("p (g i) -> p g i", i=DSEQ)
        keep(v, ALU.is_ge, 0, 1, within(v, DSEQ))
        keep(v, ALU.is_ge, DSEQ - 1, -1, [[DSEQ, DEC], [0, DSEQ]])
    for name in ("incl", "cum_incl", "s_incl", "s_cum_incl"):
        keep(m[name], ALU.is_ge, 0, -1, line)
    for name in ("strict", "cum_excl", "s_strict", "s_cum_excl"):
        keep(m[name], ALU.is_gt, 0, -1, line)
    for name in ("neg_lower", "s_neg_lower"):
        keep(m[name], ALU.is_gt, 0, 1, [[-1, P]])
        link(nc.gpsimd.tensor_scalar(m[name], m[name], -1.0, 0.0, ALU.mult, ALU.add))
    for name in ("cum_incl", "cum_excl"):
        link(nc.gpsimd.tensor_scalar(m[name][0:64, :], m[name][0:64, :], -1.0, 0.0, ALU.add, ALU.add))
    keep(m.totals[:, 0:1], ALU.is_ge, 63, -1, [[0, 1]])
    keep(m.totals[:, 1:2], ALU.is_ge, -64, 1, [[0, 1]])
    keep(m.seq_rows[:, :], ALU.is_ge, 0, 1, [[-DSEQ, DEC]])
    keep(m.seq_rows[:, :], ALU.is_ge, DSEQ - 1, -1, [[DSEQ, DEC]])


def build_level_masks(nc, m, pool, order):
    tools = MaskTools(nc, pool, order)
    link, keep = tools.link, tools.keep
    for b in (1, 2, 4, 8, 16, 32, 64):
        v = m[f"lev{b}"].rearrange("p (g h i) -> p g h i", h=2, i=b)
        link(nc.gpsimd.memset(v[:, :, 0, :], 0.0))
        n = P // (2 * b)
        keep(v[:, :, 1, :], ALU.is_ge, 0, 1, [[-2 * b, n], [0, b]])
        keep(v[:, :, 1, :], ALU.is_ge, b - 1, -1, [[2 * b, n], [0, b]])
        link(nc.gpsimd.tensor_tensor(m[f"lev{b}"], m[f"lev{b}"], m["ident"], ALU.subtract))
    v = m["lev1T"].rearrange("p (g h) -> p g h", h=2)
    link(nc.gpsimd.memset(v[:, :, 1], 0.0))
    keep(v[:, :, 0], ALU.is_equal, -1, 1, [[-2, P // 2]])
    link(nc.gpsimd.tensor_tensor(m["lev1T"], m["lev1T"], m["ident"], ALU.subtract))


def clear_semaphores(nc, sems):
    block = nc.Block()
    with block:

        @block.gpsimd
        def _(pool):
            for s in sems:
                pool.sem_clear(s)


def gemm(nc, out, xT, w, cols, first_wait=None):
    n = w.shape[1]
    for j in range(n):
        last = nc.tensor.matmul(out, xT[:, j, :], w[:, j, cols], start=(j == 0), stop=(j == n - 1))
    return last


def load_previous_rows(nc, eng, t, sample, x_rows, x_sample, shift, dst, sem):
    if sample:
        eng.dma_start(dst[0:P:DSEQ, :], shift[0]).then_inc(sem, 16)
        for b in range(DEC):
            eng.dma_start(dst[b * DSEQ + 1:(b + 1) * DSEQ, :], x_sample[b, 0:DSEQ - 1, :]).then_inc(sem, 16)
    elif isinstance(t, int) and t == 0:
        eng.dma_start(dst[1:P, :], x_rows[0:P - 1, :]).then_inc(sem, 16)
    else:
        start = t * P - 1
        src = x_rows[start:start + P, :] if isinstance(t, int) else x_rows[bass.ds(start, P), :]
        eng.dma_start(dst[:, :], src).then_inc(sem, 16)


SAMPLE_LOADS = 2 + DEC


def phase_a1(nc, m, io, T):
    with ExitStack() as ctx:
        def sb(name, shape):
            return ctx.enter_context(nc.sbuf_tensor("a1_" + name, shape, F32))

        sems = []

        def sem(name):
            sems.append(ctx.enter_context(nc.semaphore("a1_" + name)))
            return sems[-1]

        wr, wk = sb("wr", [P, NB, D]), sb("wk", [P, NB, D])
        w1, a1 = sb("w1", [P, NB, RANK]), sb("a1", [P, NB, RANK])
        w2, a2 = sb("w2", [RANK + 1, D]), sb("a2", [RANK + 1, D])
        par = sb("par", [P, 3, D])
        mu_rows, mu = sb("mu_rows", [6 * NB, P]), sb("mu", [P, 6, NB])
        x, dx = sb("x", [P, D]), sb("dx", [P, D])
        xT, dT = sb("xT", [P, NB, P]), sb("dT", [P, NB, P])
        mix_w, mix_a = sb("mix_w", [P, NB, P]), sb("mix_a", [P, NB, P])
        mix_r = [sb(f"mix_r{i}", [P, NB, P]) for i in range(2)]
        mix_k = [sb(f"mix_k{i}", [P, NB, P]) for i in range(2)]
        hid_w, hid_a = sb("hid_w", [RANK + 1, P]), sb("hid_a", [RANK + 1, P])
        twice = lambda name, n=HALF: [sb(f"{name}{i}", [P, n]) for i in range(2)]
        ta, ks, ep, em, ee = (twice(n) for n in ("ta", "ks", "ep", "em", "ee"))
        at, bh, kh, rt = (twice(n) for n in ("at", "bh", "kh", "rt"))
        bonus = twice("bonus", HH)
        dec = [sb(f"dec{i}", [P, HB, DEC]) for i in range(2)]
        tw, kku, sq, kkn, am, kp, rk = (sb(n, [P, HALF]) for n in ("tw", "kku", "sq", "kkn", "am", "kp", "rk"))
        ss, rn, one = sb("ss", [P, HH]), sb("rn", [P, HH]), sb("one", [P, 1])
        stage = [sb(f"stage{i}", [P, HB, P]) for i in range(4)]

        bank = lambda name: ctx.enter_context(nc.psum_tensor("a1_" + name, [P, 512], F32))
        pzw, pza, pk, pr, pcum, plow, pin, pout = (
            bank(n) for n in ("pzw", "pza", "pk", "pr", "pcum", "plow", "pin", "pout"))

        w_loaded, small_loaded, x_loaded = sem("w_loaded"), sem("small_loaded"), sem("x_loaded")
        ready0 = sem("ready0")
        mixwa_mid = sem("mixwa_mid")
        mu_filled, mu_ready = sem("mu_filled"), sem("mu_ready")
        dx_ready = sem("dx_ready")
        in_filled, in_taken = sem("in_filled"), sem("in_taken")
        mixwa_ready, mixr_ready, mixk_ready = sem("mixwa_ready"), sem("mixr_ready"), sem("mixk_ready")
        low_filled, low_taken = sem("low_filled"), sem("low_taken")
        zw_filled, za_filled, k_filled, r_filled = (sem(n + "_filled") for n in ("zw", "za", "k", "r"))
        tw_ready, sg_ready, ta_ready, ks_ready = (sem(n + "_ready") for n in ("tw", "sg", "ta", "ks"))
        li_filled, le_filled = sem("li_filled"), sem("le_filled")
        em_ready, ee_ready = sem("em_ready"), sem("ee_ready")
        kku_ready, sq_ready, ss_ready, norm_ready = (sem(n + "_ready") for n in ("kku", "sq", "ss", "norm"))
        am_ready, x1_ready, kp_ready = (sem(n + "_ready") for n in ("am", "x1", "kp"))
        clip_ready, rn_ready, kkn_ready, bb_ready = (sem(n + "_ready") for n in ("clip", "rn", "kkn", "bb"))
        bh_ready, kh_ready, rt_ready, rk_ready = (sem(n + "_ready") for n in ("bh", "kh", "rt", "rk"))
        rkr_ready, bonus_ready, at_ready = sem("rkr_ready"), sem("bonus_ready"), sem("at_ready")
        out_filled, out_staged = sem("out_filled"), sem("out_staged")
        stage_stored = [sem(f"stage_stored{i}") for i in range(4)]
        tok_stored = [sem(f"tok_stored{i}") for i in range(2)]
        shift_stored = sem("shift_stored")
        mask_mark = sb("mask_mark", [1, 1])
        mask_order, masks_ready = sem("mask_order"), sem("masks_ready")
        last_tile = T

        def low_uses(kind, t):
            if kind == "lora":
                return 0 if isinstance(t, int) and t == 0 else t * 3 - 1
            last = isinstance(t, int) and t == last_tile
            return t * 3 + 1 if kind == "tot0" else t * 3 + (2 if last else 3)

        def loads_of(t):
            return t * 32 + (16 * SAMPLE_LOADS if is_sample(t, T) else 32)

        ctx.callback(clear_semaphores, nc, sems)
        block = ctx.enter_context(nc.Block())

        @block.sync
        def _(sp):
            sp.dma_start(mu_rows[:, :], io["a_mu"][0].rearrange("m (j p) -> (m j) p", p=P)).then_inc(small_loaded, 16)
            sp.dma_start(w1[:, :, :], io["a_w_w1"][0].rearrange("(j p) r -> p j r", p=P)).then_inc(small_loaded, 16)
            sp.dma_start(a1[:, :, :], io["a_w_a1"][0].rearrange("(j p) r -> p j r", p=P)).then_inc(small_loaded, 16)
            sp.dma_start(w2[0:RANK, :], io["a_w_w2"][0]).then_inc(small_loaded, 16)
            sp.dma_start(w2[RANK:RANK + 1, :], io["a_w0"]).then_inc(small_loaded, 16)
            sp.dma_start(a2[0:RANK, :], io["a_w_a2"][0]).then_inc(small_loaded, 16)
            sp.dma_start(a2[RANK:RANK + 1, :], io["a_a0"]).then_inc(small_loaded, 16)

            def load_x(t):
                wait(sp, in_filled, t * 4)
                src = io["x_sample"].rearrange("b i d -> (b i) d") if is_sample(t, T) else io["x_prompt"][0][rows(t), :]
                sp.dma_start(x[:, :], src).then_inc(x_loaded, 16)
                if isinstance(t, int) and t == 0:
                    sp.wait_ge(ready0, 1)
                load_previous_rows(nc, sp, t, is_sample(t, T), io["x_prompt"][0], io["x_sample"],
                                   io["state_a_shift"], dx, x_loaded)

            load_x(0)
            wk_v = io["a_w_in"][0, 1].rearrange("(j p) n -> p j n", p=P)
            wr_v = io["a_w_in"][0, 0].rearrange("(j p) n -> p j n", p=P)
            for src, dst in ((wk_v, wk), (wr_v, wr)):
                for h in range(2):
                    sp.dma_start(dst[:, :, h * HALF:(h + 1) * HALF], src[:, :, h * HALF:(h + 1) * HALF]).then_inc(w_loaded, 16)
            for i, name in enumerate(("a_k_k", "a_k_a")):
                sp.dma_start(par[:, i, :], io[name].to_broadcast([P, D])).then_inc(w_loaded, 16)
            sp.dma_start(par[:, 2, :], io["a_r_k"][0].rearrange("(o h) n -> o (h n)", o=1).to_broadcast([P, D])).then_inc(w_loaded, 16)

            def store_unit(t, h):
                u = t * 2 + h
                cols = slice(h * HALF, (h + 1) * HALF)
                sp.wait_ge(bh_ready, u + 1)
                sp.dma_start(io["tok_b"][rows(t), cols], bh[h][:, :]).then_inc(tok_stored[h], 16)
                sp.wait_ge(kh_ready, u + 1)
                sp.dma_start(io["tok_k"][rows(t), cols], kh[h][:, :]).then_inc(tok_stored[h], 16)
                sp.wait_ge(bonus_ready, u + 1)
                sp.dma_start(io["bonus"][rows(t), h * HH:(h + 1) * HH], bonus[h][:, :]).then_inc(tok_stored[h], 16)
                sp.wait_ge(low_taken, low_uses(f"tot{h}", t) + 1)
                sp.dma_start(io["dec"][rows(t), h * HB:(h + 1) * HB, :], dec[h][:, :, :]).then_inc(tok_stored[h], 16)
                for g in range(4):
                    sp.wait_ge(out_staged, u * 4 + (g + 1))
                    sp.dma_start(io["factors"][rows(t), g, h * HB:(h + 1) * HB, :], stage[g][:, :, :]).then_inc(stage_stored[g], 16)

            def step(t, par_):
                if not is_sample(t, T):
                    load_x(t + 1)
                if not (isinstance(t, int) and t == 0):
                    store_unit(t - 1, 1)
                store_unit(t, 0)

            sp.dma_start(io["prompt_shift"][0], io["x_prompt"][0][T * P - 1:T * P, :]).then_inc(shift_stored, 16)
            sp.dma_start(io["sample_shift"][0], io["x_sample"][:, DSEQ - 1, :]).then_inc(shift_stored, 16)
            tiles(sp, T, step)
            store_unit(T, 1)
            sp.wait_ge(shift_stored, 32)
            for h in range(2):
                sp.wait_ge(tok_stored[h], 64 * (T + 1))
            for g in range(4):
                sp.wait_ge(stage_stored[g], 32 * (T + 1))

        @block.tensor
        def _(pe):
            pe.wait_ge(masks_ready, 1)
            pe.wait_ge(small_loaded, 16 * 7)
            nc.tensor.transpose(plow[:, 0:6 * NB], mu_rows[:, :], m["ident"][0:6 * NB, 0:6 * NB]).then_inc(mu_filled, 1)

            def turn_in(t, g):
                if g == 0:
                    pe.wait_ge(x_loaded, loads_of(t))
                if g == 1:
                    pe.wait_ge(dx_ready, t + 1)
                wait(pe, in_taken, t * 4 + g)
                src = x if g % 2 == 0 else dx
                for i in range(HB):
                    j = (g // 2) * HB + i
                    last = nc.tensor.transpose(pin[:, i * P:(i + 1) * P], src[:, j * P:(j + 1) * P], m["ident"])
                last.then_inc(in_filled, 1)

            def lora(t):
                pe.wait_ge(mixwa_ready, t * 2 + 2)
                if isinstance(t, int) and t == 0:
                    pe.wait_ge(mu_ready, 1)
                wait(pe, low_taken, low_uses("lora", t))
                for i, (w, mix) in enumerate(((w1, mix_w), (a1, mix_a))):
                    for j in range(NB):
                        last = nc.tensor.matmul(plow[0:RANK, i * P:(i + 1) * P], w[:, j, :], mix[:, j, :],
                                                start=(j == 0), stop=(j == NB - 1))
                last.then_inc(low_filled, 1)

            def turn_out(t, h, g):
                u = t * 2 + h
                src, ready = ((kh, kh_ready), (rt, rt_ready), (bh, bh_ready), (at, at_ready))[g]
                pe.wait_ge(ready, u + 1)
                wait(pe, out_staged, u * 4 + g)
                for i in range(HB):
                    last = nc.tensor.transpose(pout[:, i * P:(i + 1) * P], src[h][:, i * P:(i + 1) * P], m["ident"])
                last.then_inc(out_filled, 1)

            def unit(t, par_, h):
                u = t * 2 + h
                first = isinstance(t, int) and t == 0 and h == 0
                cols = slice(h * HALF, (h + 1) * HALF)
                prev = (t - 1, 1) if h == 0 else (t, 0)
                sample = is_sample(t, T)
                pe.wait_ge(low_taken, low_uses("lora", t) + 1)
                wait(pe, tw_ready, u)
                nc.tensor.matmul(pzw[:, :], hid_w[:, :], w2[:, cols], start=True, stop=True).then_inc(zw_filled, 1)
                if h == 0 and not sample:
                    turn_in(t + 1, 0)
                wait(pe, ta_ready, u)
                nc.tensor.matmul(pza[:, :], hid_a[:, :], a2[:, cols], start=True, stop=True).then_inc(za_filled, 1)
                if first:
                    pe.wait_ge(w_loaded, 16 * 7)
                pe.wait_ge(mixk_ready, t + 1)
                wait(pe, ks_ready, u)
                gemm(nc, pk[:, :], mix_k[par_], wk, cols).then_inc(k_filled, 1)
                if not first:
                    turn_out(*prev, 0)
                if h == 0 and not sample:
                    turn_in(t + 1, 1)
                pe.wait_ge(sg_ready, u + 1)
                wait(pe, ee_ready, u)
                nc.tensor.matmul(pcum[:, :], m["s_cum_incl" if sample else "cum_incl"], tw[:, :],
                                 start=True, stop=True).then_inc(li_filled, 1)
                if not first:
                    turn_out(*prev, 1)
                if h == 0 and not sample:
                    turn_in(t + 1, 2)
                pe.wait_ge(mixr_ready, t + 1)
                wait(pe, rt_ready, u)
                wait(pe, rk_ready, u)
                gemm(nc, pr[:, :], mix_r[par_], wr, cols).then_inc(r_filled, 1)
                if not first:
                    turn_out(*prev, 2)
                if h == 0 and not sample:
                    turn_in(t + 1, 3)
                pe.wait_ge(em_ready, u + 1)
                nc.tensor.matmul(pcum[:, :], m["s_cum_excl" if sample else "cum_excl"], tw[:, :],
                                 start=True, stop=True).then_inc(le_filled, 1)
                if not first:
                    turn_out(*prev, 3)
                if h == 1 and not sample:
                    lora(t + 1)
                wait(pe, low_taken, low_uses("tot0" if h == 0 else "tot1", t))
                n = DEC if sample else 2
                for i in range(HB):
                    last = nc.tensor.matmul(plow[:, 256 + i * n:256 + (i + 1) * n], tw[:, i * P:(i + 1) * P],
                                            m.seq_rows[:, :] if sample else m.totals[:, :], start=True, stop=True)
                last.then_inc(low_filled, 1)

            for g in range(4):
                turn_in(0, g)
            lora(0)
            tiles(pe, T, lambda t, par_: (unit(t, par_, 0), unit(t, par_, 1)))
            for g in range(4):
                turn_out(T, 1, g)

        @block.scalar
        def _(act):
            act.wait_ge(mu_filled, 1)
            nc.scalar.copy(mu[:, :, :].rearrange("p m j -> p (m j)"), plow[:, 0:6 * NB]).then_inc(mu_ready, 1)

            def take_in(t, g):
                act.wait_ge(in_filled, t * 4 + (g + 1))
                if g == 0:
                    wait(act, mixwa_ready, t * 2)
                    wait(act, mixr_ready, t)
                dst = xT if g % 2 == 0 else dT
                half = slice((g // 2) * HB, (g // 2 + 1) * HB)
                nc.scalar.copy(dst[:, half, :].rearrange("p j t -> p (j t)"), pin[:, :]).then_inc(in_taken, 1)

            def take_hidden(t):
                act.wait_ge(low_filled, low_uses("lora", t) + 1)
                if isinstance(t, int) and t == 0:
                    act.wait_ge(ready0, 6)
                nc.scalar.activation(hid_w[0:RANK, :], plow[0:RANK, 0:P], ACT.Tanh)
                nc.scalar.copy(hid_a[0:RANK, :], plow[0:RANK, P:2 * P]).then_inc(low_taken, 1)

            def take_out(t, h, g):
                u = t * 2 + h
                act.wait_ge(out_filled, u * 4 + (g + 1))
                wait(act, stage_stored[g], u * 16)
                nc.scalar.copy(stage[g][:, :, :].rearrange("p j t -> p (j t)"), pout[:, :]).then_inc(out_staged, 1)

            def unit(t, h):
                u = t * 2 + h
                first = isinstance(t, int) and t == 0 and h == 0
                prev = (t - 1, 1) if h == 0 else (t, 0)
                sample = is_sample(t, T)
                act.wait_ge(zw_filled, u + 1)
                nc.scalar.activation(tw[:, :], pzw[:, :], ACT.Tanh, scale=0.5).then_inc(tw_ready, 1)
                if h == 0 and not sample:
                    take_in(t + 1, 0)
                act.wait_ge(za_filled, u + 1)
                wait(act, bb_ready, u - 1)
                nc.scalar.activation(ta[h][:, :], pza[:, :], ACT.Tanh, scale=0.5).then_inc(ta_ready, 1)
                act.wait_ge(k_filled, u + 1)
                wait(act, kp_ready, u - 1)
                nc.scalar.copy(ks[h][:, :], pk[:, :]).then_inc(ks_ready, 1)
                if not first:
                    take_out(*prev, 0)
                if h == 0 and not sample:
                    take_in(t + 1, 1)
                act.wait_ge(ss_ready, u + 1)
                nc.scalar.activation(ss[:, :], ss[:, :], ACT.Sqrt).then_inc(norm_ready, 1)
                act.wait_ge(li_filled, u + 1)
                wait(act, rt_ready, u - 1)
                nc.scalar.activation(ep[h][:, :], pcum[:, :], ACT.Exp, scale=DECAY / 2)
                wait(act, kh_ready, u - 1)
                nc.scalar.activation(em[h][:, :], pcum[:, :], ACT.Exp, scale=-DECAY / 2).then_inc(em_ready, 1)
                if not first:
                    take_out(*prev, 1)
                if h == 0 and not sample:
                    take_in(t + 1, 2)
                if not first:
                    take_out(*prev, 2)
                if h == 0 and not sample:
                    take_in(t + 1, 3)
                act.wait_ge(le_filled, u + 1)
                wait(act, at_ready, u - 1)
                nc.scalar.activation(ee[h][:, :], pcum[:, :], ACT.Exp, scale=DECAY / 2).then_inc(ee_ready, 1)
                if not first:
                    take_out(*prev, 3)
                if h == 1 and not sample:
                    take_hidden(t + 1)
                n = DEC if sample else 2
                act.wait_ge(low_filled, low_uses("tot0" if h == 0 else "tot1", t) + 1)
                wait(act, tok_stored[h], t * 64)
                nc.scalar.activation(dec[h][:, :, 0:n], plow[:, 256:256 + HB * n].rearrange("p (j n) -> p j n", n=n),
                                     ACT.Exp, scale=DECAY / 2).then_inc(low_taken, 1)

            for g in range(4):
                take_in(0, g)
            take_hidden(0)
            tiles(act, T, lambda t, par_: (unit(t, 0), unit(t, 1)))
            for g in range(4):
                take_out(T, 1, g)

        @block.gpsimd
        def _(pool):
            def mix_wa(t):
                pool.wait_ge(in_taken, t * 4 + 4)
                wait(pool, low_filled, low_uses("lora", t - 1) + 1 if not isinstance(t, int) or t > 0 else 0)
                for i, (dst, row) in enumerate(((mix_w, 1), (mix_a, 4))):
                    s = mu[:, row, :].unsqueeze(2).to_broadcast([P, NB, P])
                    nc.gpsimd.tensor_tensor(dst[:, :, :], dT[:, :, :], s, ALU.mult).then_inc(mixwa_mid, 1)
                    pool.wait_ge(mixwa_mid, t * 2 + (i + 1))
                    nc.gpsimd.tensor_tensor(dst[:, :, :], dst[:, :, :], xT[:, :, :], ALU.add).then_inc(mixwa_ready, 1)

            def unit(t, h):
                u = t * 2 + h
                pool.wait_ge(tw_ready, u + 1)
                nc.gpsimd.tensor_tensor(tw[:, :], tw[:, :], one[:, :].to_broadcast([P, HALF]), ALU.add).then_inc(sg_ready, 1)
                if h == 1 and not is_sample(t, T):
                    mix_wa(t + 1)
                pool.wait_ge(x1_ready, u + 1)
                wait(pool, rk_ready, u)
                wait(pool, kh_ready, u)
                nc.gpsimd.tensor_tensor(kp[:, :], sq[:, :], ks[h][:, :], ALU.add).then_inc(kp_ready, 1)
                pool.wait_ge(rk_ready, u + 1)
                nc.gpsimd.tensor_tensor(rk[:, :], rk[:, :], par[:, 2, h * HALF:(h + 1) * HALF], ALU.mult).then_inc(rkr_ready, 1)

            build_masks(nc, m, pool, mask_order)
            nc.gpsimd.memset(mask_mark[:, :], 0.0).then_inc(masks_ready, 1)
            pool.wait_ge(mu_ready, 1)
            mix_wa(0)
            pool.wait_ge(ready0, 6)
            pool.wait_ge(w_loaded, 16 * 7)
            tiles(pool, T, lambda t, par_: (unit(t, 0), unit(t, 1)))

        @block.vector
        def _(dve):
            def make_dx(t):
                dve.wait_ge(x_loaded, loads_of(t))
                nc.vector.tensor_tensor(dx[:, :], dx[:, :], x[:, :], ALU.subtract).then_inc(dx_ready, 1)

            def mix_rk(t, par_):
                dve.wait_ge(in_taken, t * 4 + 4)
                wait(dve, r_filled, t * 2 - 2)
                for dst, row, ready in ((mix_k[par_], 2, mixk_ready), (mix_r[par_], 0, mixr_ready)):
                    for j in range(NB):
                        last = nc.vector.scalar_tensor_tensor(out=dst[:, j, :], in0=dT[:, j, :], scalar=mu[:, row, j:j + 1],
                                                              in1=xT[:, j, :], op0=ALU.mult, op1=ALU.add)
                    last.then_inc(ready, 1)

            def heads(ap):
                return ap.rearrange("p (h n) -> p h n", n=HD)

            def unit(t, par_, h):
                u = t * 2 + h
                cols = slice(h * HALF, (h + 1) * HALF)
                sample = is_sample(t, T)
                if h == 0 and not sample:
                    make_dx(t + 1)
                dve.wait_ge(ks_ready, u + 1)
                wait(dve, bb_ready, u)
                nc.vector.tensor_tensor(kku[:, :], ks[h][:, :], par[:, 0, cols], ALU.mult).then_inc(kku_ready, 1)
                wait(dve, kp_ready, u)
                dve.wait_ge(kku_ready, u + 1)
                nc.vector.tensor_tensor(sq[:, :], kku[:, :], kku[:, :], ALU.mult).then_inc(sq_ready, 1)
                dve.wait_ge(sq_ready, u + 1)
                wait(dve, clip_ready, u)
                nc.vector.tensor_reduce(ss[:, :], heads(sq[:, :]), X, ALU.add).then_inc(ss_ready, 1)
                if h == 1 and not sample:
                    mix_rk(t + 1, 1 - par_)
                dve.wait_ge(ta_ready, u + 1)
                wait(dve, x1_ready, u)
                nc.vector.scalar_tensor_tensor(out=am[:, :], in0=ta[h][:, :], scalar=1.0, in1=par[:, 1, cols],
                                               op0=ALU.subtract, op1=ALU.mult).then_inc(am_ready, 1)
                dve.wait_ge(am_ready, u + 1)
                dve.wait_ge(ss_ready, u + 1)
                nc.vector.scalar_tensor_tensor(out=sq[:, :], in0=am[:, :], scalar=0.5, in1=ks[h][:, :],
                                               op0=ALU.mult, op1=ALU.mult).then_inc(x1_ready, 1)
                dve.wait_ge(norm_ready, u + 1)
                wait(dve, kkn_ready, u)
                nc.vector.tensor_scalar(rn[:, :], ss[:, :], 1e-12, None, ALU.max).then_inc(clip_ready, 1)
                dve.wait_ge(clip_ready, u + 1)
                nc.vector.reciprocal(rn[:, :], rn[:, :]).then_inc(rn_ready, 1)
                dve.wait_ge(rn_ready, u + 1)
                wait(dve, at_ready, u)
                nc.vector.tensor_tensor(heads(kkn[:, :]), heads(kku[:, :]),
                                        rn[:, :].unsqueeze(2).to_broadcast([P, HH, HD]), ALU.mult).then_inc(kkn_ready, 1)
                dve.wait_ge(kkn_ready, u + 1)
                nc.vector.scalar_tensor_tensor(out=kku[:, :], in0=ta[h][:, :], scalar=1.0, in1=kkn[:, :],
                                               op0=ALU.add, op1=ALU.mult).then_inc(bb_ready, 1)
                dve.wait_ge(bb_ready, u + 1)
                dve.wait_ge(em_ready, u + 1)
                wait(dve, out_filled, (u - 1) * 4)
                wait(dve, tok_stored[h], t * 64)
                nc.vector.scalar_tensor_tensor(out=bh[h][:, :], in0=kku[:, :], scalar=0.5, in1=em[h][:, :],
                                               op0=ALU.mult, op1=ALU.mult).then_inc(bh_ready, 1)
                dve.wait_ge(kp_ready, u + 1)
                nc.vector.tensor_tensor(kh[h][:, :], kp[:, :], em[h][:, :], ALU.mult).then_inc(kh_ready, 1)
                dve.wait_ge(r_filled, u + 1)
                nc.vector.tensor_tensor(rt[h][:, :], pr[:, :], ep[h][:, :], ALU.mult).then_inc(rt_ready, 1)
                wait(dve, bonus_ready, u)
                nc.vector.tensor_tensor(rk[:, :], pr[:, :], kp[:, :], ALU.mult).then_inc(rk_ready, 1)
                dve.wait_ge(ee_ready, u + 1)
                nc.vector.tensor_tensor(at[h][:, :], kkn[:, :], ee[h][:, :], ALU.mult).then_inc(at_ready, 1)
                dve.wait_ge(rkr_ready, u + 1)
                nc.vector.tensor_reduce(bonus[h][:, :], heads(rk[:, :]), X, ALU.add).then_inc(bonus_ready, 1)

            nc.vector.memset(dx[0:1, :], 0.0).then_inc(ready0, 1)
            nc.vector.memset(one[:, :], 1.0).then_inc(ready0, 1)
            nc.vector.memset(hid_w[RANK:RANK + 1, :], 1.0).then_inc(ready0, 1)
            nc.vector.memset(hid_a[RANK:RANK + 1, :], 1.0).then_inc(ready0, 1)
            for h in range(2):
                nc.vector.memset(dec[h][:, :, :], 1.0).then_inc(ready0, 1)

            make_dx(0)
            dve.wait_ge(mu_ready, 1)
            mix_rk(0, 0)
            dve.wait_ge(w_loaded, 16 * 7)
            tiles(dve, T, lambda t, par_: (unit(t, par_, 0), unit(t, par_, 1)))


FP22 = mybir.dt.float32r
BF16 = mybir.dt.bfloat16


def gemm_of_parts(nc, out, x, w, cols):
    (high, low, rough), (w_high, w_low) = x, w
    n = w_high.shape[1]
    for j in range(n):
        nc.tensor.matmul(out, high[:, j, :], w_high[:, j, cols], start=(j == 0), stop=False)
        nc.tensor.matmul(out, low[:, j, :], w_high[:, j, cols], start=False, stop=False)
        last = nc.tensor.matmul(out, rough[:, j, :], w_low[:, j, cols], start=False, stop=(j == n - 1))
    return last


class WeightCuts:

    PIECES = HB

    def __init__(self, nc, sem, parts, room):
        self.nc, self.parts, self.room = nc, parts, room
        self.loaded = [sem(f"piece_loaded{i}") for i in range(len(room))]
        self.high_ready, self.low_ready = sem("cut_high"), sem("cut_low")

    def pieces(self, i):
        src, high, low, cols = self.parts[i]
        for k in range(self.PIECES):
            n, at = i * self.PIECES + k, slice(2 * k, 2 * k + 2)
            room = self.room[n % len(self.room)][:, :].rearrange("p (j c) -> p j c", j=2)
            yield n, src[:, at, cols], high[:, at, cols], low[:, at, cols], room

    def load(self, sp, i):
        for n, src, _, _, room in self.pieces(i):
            wait(sp, self.low_ready, n - len(self.room) + 1)
            sp.dma_start(room, src).then_inc(self.loaded[n % len(self.room)], 16)

    def take_high(self, act, i):
        for n, _, high, _, room in self.pieces(i):
            act.wait_ge(self.loaded[n % len(self.room)], 16 * (n // len(self.room) + 1))
            self.nc.scalar.copy(high, room).then_inc(self.high_ready, 1)

    def take_low(self, dve, i):
        for n, _, high, low, room in self.pieces(i):
            dve.wait_ge(self.high_ready, n + 1)
            self.nc.vector.tensor_tensor(low, room, high.bitcast(F32), ALU.subtract).then_inc(self.low_ready, 1)

    def wait_for(self, eng, i):
        eng.wait_ge(self.low_ready, (i + 1) * self.PIECES)


def phase_a2(nc, m, io, T):
    with ExitStack() as ctx:
        def sb(name, shape, dtype=F32):
            return ctx.enter_context(nc.sbuf_tensor("a2_" + name, shape, dtype))

        sems = []

        def sem(name):
            sems.append(ctx.enter_context(nc.semaphore("a2_" + name)))
            return sems[-1]

        wv, wg = sb("wv", [P, NB, D], FP22), sb("wg", [P, NB, D], FP22)
        wv_low, wg_low = sb("wv_low", [P, NB, D], BF16), sb("wg_low", [P, NB, D], BF16)
        par = sb("par", [P, 2, D])
        mu_rows, mu = sb("mu_rows", [6 * NB, P]), sb("mu", [P, 6, NB])
        x = [sb(f"x{i}", [P, D]) for i in range(2)]
        dx = [sb(f"dx{i}", [P, D]) for i in range(2)]
        xT, dT = sb("xT", [P, NB, P]), sb("dT", [P, NB, P])
        whole = [sb(f"whole_{n}", [P, NB, P]) for n in ("v", "g")]
        mix_v, mix_g = ([(sb(f"{n}_high{i}", [P, NB, P], FP22), sb(f"{n}_low{i}", [P, NB, P], FP22), sb(f"{n}_rough{i}", [P, NB, P], BF16))
                         for i in range(2)] for n in ("mix_v", "mix_g"))
        bonus = [sb(f"bonus{i}", [P, NH]) for i in range(2)]
        v, g, gmul, gadd = (sb(n, [P, D]) for n in ("v", "g", "gmul", "gadd"))

        bank = lambda name: ctx.enter_context(nc.psum_tensor("a2_" + name, [P, 512], F32))
        pv, pg, pin = [bank("pv0"), bank("pv1")], [bank("pg0"), bank("pg1")], [bank("pin0"), bank("pin1")]

        mu_loaded, par_loaded = sem("mu_loaded"), sem("par_loaded")
        x_loaded = [sem(f"x_loaded{i}") for i in range(2)]
        bonus_loaded = [sem(f"bonus_loaded{i}") for i in range(2)]
        zero_row, mask_order = sem("zero_row"), sem("mask_order")
        mu_filled, mu_ready, dx_ready = sem("mu_filled"), sem("mu_ready"), sem("dx_ready")
        in_filled, in_taken = sem("in_filled"), sem("in_taken")
        mix_ready, high_ready, low_ready, rough_ready = (sem(n) for n in ("mix_ready", "mix_high", "mix_low", "mix_rough"))
        v_filled, g_filled = sem("v_filled"), sem("g_filled")
        v_ready, g_ready = sem("v_ready"), sem("g_ready")
        gmul_ready, gadd_ready, bv_ready, sum_ready = (sem(n) for n in ("gmul_ready", "gadd_ready", "bv_ready", "sum_ready"))
        v_stored, gmul_stored, gadd_stored = sem("v_stored"), sem("gmul_stored"), sem("gadd_stored")

        halves = [slice(h * HALF, (h + 1) * HALF) for h in range(2)]
        blocks = lambda w: w.rearrange("(j p) n -> p j n", p=P)
        cuts = WeightCuts(nc, sem, [(blocks(io["a_w_in"][0, i]), w, w_low, halves[h]) for h in range(2)
                                    for i, w, w_low in ((2, wv, wv_low), (3, wg, wg_low))], (gmul, gadd, v, g))

        ctx.callback(clear_semaphores, nc, sems)
        block = ctx.enter_context(nc.Block())

        def loads_of(t, par_):
            return of_parity(t, par_, 32) + (16 * SAMPLE_LOADS if is_sample(t, T) else 32)

        @block.sync
        def _(sp):
            sp.dma_start(mu_rows[:, :], io["a_mu"][0].rearrange("m (j p) -> (m j) p", p=P)).then_inc(mu_loaded, 16)

            def load_x(t, par_):
                wait(sp, in_filled, (t - 1) * 4)
                src = io["x_sample"].rearrange("b i d -> (b i) d") if is_sample(t, T) else io["x_prompt"][0][rows(t), :]
                sp.dma_start(x[par_][:, :], src).then_inc(x_loaded[par_], 16)
                if isinstance(t, int) and t == 0:
                    sp.wait_ge(zero_row, 1)
                load_previous_rows(nc, sp, t, is_sample(t, T), io["x_prompt"][0], io["x_sample"],
                                   io["state_a_shift"], dx[par_], x_loaded[par_])
                wait(sp, gadd_ready, (t - 1) * 2)
                sp.dma_start(bonus[par_][:, :], io["bonus"][rows(t), :]).then_inc(bonus_loaded[par_], 16)

            load_x(0, 0)
            cuts.load(sp, 0)
            load_x(1, 1)
            for i in range(1, 4):
                cuts.load(sp, i)
            for i, name in enumerate(("a_gn_g", "a_gn_b")):
                sp.dma_start(par[:, i, :], io[name].to_broadcast([P, D])).then_inc(par_loaded, 16)

            def step(t, par_):
                if not is_sample(t, T) and not (isinstance(t, int) and t == T - 1):
                    load_x(t + 2, par_)
                for h in range(2):
                    cols = slice(h * HALF, (h + 1) * HALF)
                    sp.wait_ge(v_ready, t * 2 + (h + 1))
                    sp.dma_start(io["tok_v"][rows(t), cols], v[:, cols]).then_inc(v_stored, 16)
                    sp.wait_ge(gmul_ready, t * 2 + (h + 1))
                    sp.dma_start(io["gate_mul"][rows(t), cols], gmul[:, cols]).then_inc(gmul_stored, 16)
                    sp.wait_ge(gadd_ready, t * 2 + (h + 1))
                    sp.dma_start(io["gate_add"][rows(t), cols], gadd[:, cols]).then_inc(gadd_stored, 16)

            tiles(sp, T, step)
            for stored in (v_stored, gmul_stored, gadd_stored):
                sp.wait_ge(stored, 32 * (T + 1))

        @block.tensor
        def _(pe):
            pe.wait_ge(mu_loaded, 16)
            nc.tensor.transpose(pin[0][:, 0:6 * NB], mu_rows[:, :], m["ident"][0:6 * NB, 0:6 * NB]).then_inc(mu_filled, 1)
            pe.wait_ge(mu_ready, 1)

            def turn_in(t, par_, grp):
                if grp == 0:
                    pe.wait_ge(x_loaded[par_], loads_of(t, par_))
                if grp == 1:
                    pe.wait_ge(dx_ready, t + 1)
                wait(pe, in_taken, t * 4 + grp - 1)
                src = x[par_] if grp % 2 == 0 else dx[par_]
                for i in range(HB):
                    j = (grp // 2) * HB + i
                    last = nc.tensor.transpose(pin[grp % 2][:, i * P:(i + 1) * P], src[:, j * P:(j + 1) * P], m["ident"])
                last.then_inc(in_filled, 1)

            def wait_for_mix(t, i):
                pe.wait_ge(low_ready, t * 2 + (i + 1))
                pe.wait_ge(rough_ready, t * 2 + (i + 1))

            def step(t, par_):
                for h in range(2):
                    cols = slice(h * HALF, (h + 1) * HALF)
                    if isinstance(t, int) and t == 0:
                        cuts.wait_for(pe, 2 * h)
                    wait_for_mix(t, 0)
                    wait(pe, v_ready, t * 2 - (1 - h))
                    gemm_of_parts(nc, pv[h][:, :], mix_v[par_], (wv, wv_low), cols).then_inc(v_filled, 1)
                    if not is_sample(t, T) and h == 0:
                        turn_in(t + 1, 1 - par_, 0)
                        turn_in(t + 1, 1 - par_, 1)
                    if isinstance(t, int) and t == 0:
                        cuts.wait_for(pe, 2 * h + 1)
                    wait_for_mix(t, 1)
                    wait(pe, g_ready, t * 2 - (1 - h))
                    gemm_of_parts(nc, pg[h][:, :], mix_g[par_], (wg, wg_low), cols).then_inc(g_filled, 1)
                    if not is_sample(t, T) and h == 0:
                        turn_in(t + 1, 1 - par_, 2)
                        turn_in(t + 1, 1 - par_, 3)

            for grp in range(4):
                turn_in(0, 0, grp)
            tiles(pe, T, step)

        @block.scalar
        def _(act):
            act.wait_ge(mu_filled, 1)
            nc.scalar.copy(mu[:, :, :].rearrange("p m j -> p (m j)"), pin[0][:, 0:6 * NB]).then_inc(mu_ready, 1)

            def take_in(t, grp):
                act.wait_ge(in_filled, t * 4 + (grp + 1))
                if grp == 0:
                    wait(act, mix_ready, t * 2)
                dst = xT if grp % 2 == 0 else dT
                half = slice((grp // 2) * HB, (grp // 2 + 1) * HB)
                nc.scalar.copy(dst[:, half, :].rearrange("p j t -> p (j t)"), pin[grp % 2][:, :]).then_inc(in_taken, 1)

            def high_and_rough(t, par_):
                for i, mix in enumerate((mix_v, mix_g)):
                    act.wait_ge(mix_ready, t * 2 + (i + 1))
                    nc.scalar.copy(mix[par_][0][:, :, :], whole[i][:, :, :]).then_inc(high_ready, 1)
                    act.wait_ge(high_ready, t * 2 + (i + 1))
                    nc.scalar.copy(mix[par_][2][:, :, :], mix[par_][0][:, :, :].bitcast(F32)).then_inc(rough_ready, 1)

            def step(t, par_):
                for h in range(2):
                    cols = slice(h * HALF, (h + 1) * HALF)
                    act.wait_ge(v_filled, t * 2 + (h + 1))
                    wait(act, v_stored, t * 32)
                    wait(act, bv_ready, t * 2)
                    nc.scalar.copy(v[:, cols], pv[h][:, :]).then_inc(v_ready, 1)
                    if not is_sample(t, T) and h == 0:
                        take_in(t + 1, 0)
                        take_in(t + 1, 1)
                    if not is_sample(t, T) and h == 1:
                        high_and_rough(t + 1, 1 - par_)
                    act.wait_ge(g_filled, t * 2 + (h + 1))
                    wait(act, gadd_ready, t * 2)
                    nc.scalar.activation(g[:, cols], pg[h][:, :], ACT.Silu).then_inc(g_ready, 1)
                    if not is_sample(t, T) and h == 0:
                        take_in(t + 1, 2)
                        take_in(t + 1, 3)

            for grp in range(4):
                take_in(0, grp)
            cuts.take_high(act, 0)
            high_and_rough(0, 0)
            for i in range(1, 4):
                cuts.take_high(act, i)
            cuts.wait_for(act, 3)
            tiles(act, T, step)

        @block.gpsimd
        def _(pool):
            build_level_masks(nc, m, pool, mask_order)

            def step(t, par_):
                for i, mix in enumerate((mix_v, mix_g)):
                    high, low, _ = mix[par_]
                    pool.wait_ge(high_ready, t * 2 + (i + 1))
                    nc.gpsimd.tensor_tensor(low[:, :, :], whole[i][:, :, :], high[:, :, :].bitcast(F32), ALU.subtract).then_inc(low_ready, 1)

            tiles(pool, T, step)

        @block.vector
        def _(dve):
            nc.vector.memset(dx[0][0:1, :], 0.0).then_inc(zero_row, 1)

            def make_dx(t, par_):
                dve.wait_ge(x_loaded[par_], loads_of(t, par_))
                nc.vector.tensor_tensor(dx[par_][:, :], dx[par_][:, :], x[par_][:, :], ALU.subtract).then_inc(dx_ready, 1)

            def mixes(t, par_):
                dve.wait_ge(in_taken, t * 4 + 4)
                wait(dve, g_filled, t * 2 - 2)
                for i, row in enumerate((3, 5)):
                    wait(dve, low_ready, t * 2 - (1 - i))
                    for j in range(NB):
                        last = nc.vector.scalar_tensor_tensor(out=whole[i][:, j, :], in0=dT[:, j, :], scalar=mu[:, row, j:j + 1],
                                                              in1=xT[:, j, :], op0=ALU.mult, op1=ALU.add)
                    last.then_inc(mix_ready, 1)

            def step(t, par_):
                if not is_sample(t, T):
                    make_dx(t + 1, 1 - par_)
                for h in range(2):
                    if h == 1 and not is_sample(t, T):
                        mixes(t + 1, 1 - par_)
                    n = t * 2 + (h + 1)
                    cols = slice(h * HALF, (h + 1) * HALF)
                    dve.wait_ge(v_ready, n)
                    dve.wait_ge(bonus_loaded[par_], of_parity(t, par_, 16) + 16)
                    wait(dve, gadd_stored, t * 32)
                    b = bonus[par_][:, h * HH:(h + 1) * HH].unsqueeze(2).to_broadcast([P, HH, HD])
                    nc.vector.tensor_tensor(gadd[:, cols].rearrange("p (h n) -> p h n", n=HD),
                                            v[:, cols].rearrange("p (h n) -> p h n", n=HD), b, ALU.mult).then_inc(bv_ready, 1)
                    dve.wait_ge(bv_ready, n)
                    nc.vector.tensor_tensor(gadd[:, cols], gadd[:, cols], par[:, 1, cols], ALU.add).then_inc(sum_ready, 1)
                    dve.wait_ge(g_ready, n)
                    wait(dve, gmul_stored, t * 32)
                    nc.vector.tensor_tensor(gmul[:, cols], g[:, cols], par[:, 0, cols], ALU.mult).then_inc(gmul_ready, 1)
                    dve.wait_ge(sum_ready, n)
                    nc.vector.tensor_tensor(gadd[:, cols], gadd[:, cols], g[:, cols], ALU.mult).then_inc(gadd_ready, 1)

            make_dx(0, 0)
            dve.wait_ge(mu_ready, 1)
            cuts.take_low(dve, 0)
            mixes(0, 0)
            for i in range(1, 4):
                cuts.take_low(dve, i)
            cuts.wait_for(dve, 3)
            dve.wait_ge(par_loaded, 32)
            tiles(dve, T, step)


SCORE_USES = NH + 4
RAWS = 4
STAGES = 7
CHAIN_PLAN = [[("x", j) for j in range(4, NB)], [None] * 4 + [("sa", j) for j in range(NB)],
              [None] * 3 + [("o", j) for j in range(3)], [("o", j) for j in range(3, NB)],
              [None] * 4 + [("p", j) for j in range(NB)], [], []]


def phase_a3(nc, m, io, T, sample=False):
    with ExitStack() as ctx:
        pre = "s3_" if sample else "a3_"
        bufs = 1 if sample else 2

        def sb(name, shape, dtype=F32):
            return ctx.enter_context(nc.sbuf_tensor(pre + name, shape, dtype))

        sems = []

        def sem(name):
            sems.append(ctx.enter_context(nc.semaphore(pre + name)))
            return sems[-1]

        K_, R_, B_, A_ = range(4)
        fac = [sb(f"fac{i}", [P, 4, NB, P]) for i in range(bufs)]
        dec = [sb(f"dec{i}", [P, NB, DEC]) for i in range(bufs)]
        sc = [sb(f"sc{i}", [P, NH, 4, P]) for i in range(bufs)]
        quad = sb("quad", [P, 4, P])
        na = sb("na", [P, NH, P], F16)
        tu = sb("tu", [P, NH, 2, P], F16)
        mp = sb("mp", [P, NH, P], F16)
        ufin = sb("ufin", [P, NH, P])
        tok = sb("tok", [P, 3, D])
        gates = sb("gates", [P, 2, D])
        xs, sa, o, tmp = (sb(n, [P, D]) for n in ("xs", "sa", "o", "tmp"))
        f, s1, s2 = sb("f", [P, NB]), sb("s1", [P, NH]), sb("s2", [P, NH])
        if sample:
            st = sb("st", [P, NB, DEC, P])
            seq_cols = sb("seq_cols", [P, DEC, P])
            raws = [sb(f"raw{i}", [P, DEC, HD]) for i in range(RAWS)]
            raw_bds = [sb(f"raw_bd{i}", [P, DEC, P]) for i in range(2)]
            raw = raws[0]
            wide = sb("wide", [P, 2, DEC, P])
        else:
            st = sb("st", [P, NB, P])
            raw = sb("raw", [P, NB, HD])

        bank = lambda name: ctx.enter_context(nc.psum_tensor(pre + name, [P, 512], F32))
        psc, pm, ptu, pch = ([bank(f"{n}{i}") for i in range(2)] for n in ("psc", "pm", "ptu", "pch"))

        fac_loaded = [sem(f"fac_loaded{i}") for i in range(bufs)]
        tok_loaded, gates_loaded = sem("tok_loaded"), sem("gates_loaded")
        setup = sem("setup")
        sc_filled, sc_taken = sem("sc_filled"), sem("sc_taken")
        nega_ready, t1_ready, na_ready = sem("nega_ready"), sem("t1_ready"), sem("na_ready")
        m_filled, m_ready = sem("m_filled"), sem("m_ready")
        tu_filled, tu_taken = sem("tu_filled"), sem("tu_taken")
        x_filled, x_ready = sem("x_filled"), sem("x_ready")
        sa_filled, sa_ready = sem("sa_filled"), sem("sa_ready")
        o_filled, o_ready = sem("o_filled"), sem("o_ready")
        p_filled, state_sum, state_ready, f_ready = sem("p_filled"), sem("state_sum"), sem("state_ready"), sem("f_ready")
        sum_ready, mean_ready, d_ready, sq_ready = (sem(n + "_ready") for n in ("sum", "mean", "d", "sq"))
        sqsum_ready, var_ready, std_ready, rstd_ready = (sem(n + "_ready") for n in ("sqsum", "var", "std", "rstd"))
        dn_ready, ymul_ready, y_ready, y_stored = sem("dn_ready"), sem("ymul_ready"), sem("y_ready"), sem("y_stored")
        out_filled, out_ready, state_stored = sem("out_filled"), sem("out_ready"), sem("state_stored")
        if sample:
            raw_loaded = [sem(f"raw_loaded{i}") for i in range(RAWS)]
            bd_ready = [sem(f"bd_ready{i}") for i in range(2)]
            bd_filled, bd_taken, bd_zero = sem("bd_filled"), sem("bd_taken"), sem("bd_zero")
            wide_ready, wide_v_ready, wide_used = sem("wide_ready"), sem("wide_v_ready"), sem("wide_used")

        levels = (2, 4, 8) if sample else (2, 4, 8, 16, 32, 64)
        M_USES = 4 * len(levels) + 4
        TU_USES = 8 * len(levels) + 4
        tile0 = T if sample else 0
        steps = 1 if sample else T

        ctx.callback(clear_semaphores, nc, sems)
        block = ctx.enter_context(nc.Block())

        def over(eng, step):
            if sample:
                step(0, 0)
                step(1, 0)
            else:
                tiles(eng, T, step)

        def has_tile(t):
            return not (isinstance(t, int) and t == steps)

        def has_chain(t):
            return not (isinstance(t, int) and t == 0)

        def fac_loads(t, par_):
            return of_parity(t, par_, 32) + 32

        @block.sync
        def _(sp):
            def load_factors(t, par_):
                sp.dma_start(fac[par_][:, :, :, :], io["factors"][rows(t + tile0), :, :, :]).then_inc(fac_loaded[par_], 16)
                sp.dma_start(dec[par_][:, :, :], io["dec"][rows(t + tile0), :, :]).then_inc(fac_loaded[par_], 16)

            def load_tok(t):
                for i, name in enumerate(("tok_b", "tok_k", "tok_v")):
                    sp.dma_start(tok[:, i, :], io[name][rows(t + tile0), :]).then_inc(tok_loaded, 16)

            def load_gates(t):
                for i, name in enumerate(("gate_mul", "gate_add")):
                    sp.dma_start(gates[:, i, :], io[name][rows(t + tile0), :]).then_inc(gates_loaded, 16)

            load_factors(0, 0)
            load_tok(0)
            load_gates(0)
            if sample:
                for j in range(NB):
                    for e in range(2):
                        wait(sp, bd_ready[e], j - RAWS + 1)
                    for b in range(DEC):
                        src = io["state_a_wkv"][0, b, 2 * j:2 * j + 2, :, :].rearrange("e v k -> (e v) k")
                        sp.dma_start(raws[j % RAWS][:, b, :], src).then_inc(raw_loaded[j % RAWS], 16)
            else:
                load_factors(1, 1)

            def step(t, par_):
                if has_chain(t):
                    if has_tile(t) and not (isinstance(t, int) and t == steps - 1):
                        sp.wait_ge(o_filled, t)
                        sp.wait_ge(f_ready, t)
                        load_factors(t + 1, 1 - par_)
                    if has_tile(t):
                        sp.wait_ge(p_filled, t)
                        load_tok(t)
                    sp.wait_ge(y_ready, t)
                    sp.dma_start(io["mixed"][rows(t + (tile0 - 1)), :], tmp[:, :]).then_inc(y_stored, 16)
                    if has_tile(t):
                        load_gates(t)

            over(sp, step)
            if sample:
                for j in range(NB):
                    sp.wait_ge(out_ready, 2 * j + 2)
                    for b in range(DEC):
                        dst = io["sample_wkv"][0, b, 2 * j:2 * j + 2, :, :].rearrange("e v k -> (e v) k")
                        sp.dma_start(dst, raw[:, b, :]).then_inc(state_stored, 16)
                sp.wait_ge(state_stored, 16 * DEC * NB)
            else:
                sp.wait_ge(out_ready, 4)
                dst = io["prompt_wkv"][0, 0].rearrange("(j e) v k -> (e v) j k", e=2)
                sp.dma_start(dst, raw[:, :, :]).then_inc(state_stored, 16)
                sp.wait_ge(state_stored, 16)
            sp.wait_ge(y_stored, 16 * steps)

        @block.tensor
        def _(pe):
            def head(ap, h):
                return ap[64 * (h % 2):64 * (h % 2) + 64, h // 2, :]

            def scores(t, par_):
                fb = fac[par_]
                pe.wait_ge(fac_loaded[par_], fac_loads(t, par_))
                for h in range(NH):
                    wait(pe, sc_taken, t * SCORE_USES + (h - 1))
                    out = psc[h % 2]
                    a, r, b, k = (head(fb[:, i, :, :], h) for i in (A_, R_, B_, K_))
                    nc.tensor.matmul(out[:, 0:P], a, b, start=True, stop=True)
                    nc.tensor.matmul(out[:, P:2 * P], b, r, start=True, stop=True)
                    nc.tensor.matmul(out[:, 2 * P:3 * P], k, a, start=True, stop=True)
                    nc.tensor.matmul(out[:, 3 * P:4 * P], k, r, start=True, stop=True).then_inc(sc_filled, 1)

            def turn(t, par_):
                for b in range(4):
                    pe.wait_ge(nega_ready, t * 4 + (b + 1))
                    pe.wait_ge(sc_taken, t * SCORE_USES + (NH + b - 1))
                    for i in range(4):
                        last = nc.tensor.transpose(psc[b % 2][:, i * P:(i + 1) * P], sc[par_][:, 4 * b + i, 0, :], m["ident"])
                    last.then_inc(sc_filled, 1)

            def level(t, par_, l, fill):
                for b in range(4):
                    if l == 0:
                        pe.wait_ge(t1_ready, t * 4 + (b + 1))
                        pe.wait_ge(na_ready, t * 4 + (b + 1))
                        pe.wait_ge(sc_taken, t * SCORE_USES + (NH + b + 1))
                    else:
                        pe.wait_ge(tu_taken, t * TU_USES + (8 * (l - 1) + 2 * b + 2))
                    wait(pe, m_ready, t * M_USES + (4 * l + b - 1))
                    for i in range(4):
                        h = 4 * b + i
                        last = nc.tensor.matmul(pm[b % 2][:, i * P:(i + 1) * P], na[:, h, :], tu[:, h, 1, :],
                                                start=True, stop=True)
                    last.then_inc(m_filled, 1)
                    fill(b, 12)
                for q in range(8):
                    pe.wait_ge(m_ready, t * M_USES + (4 * l + q // 2 + 1))
                    wait(pe, tu_taken, t * TU_USES + (8 * l + q - 1))
                    out = ptu[q % 2]
                    for i in range(2):
                        h = 2 * q + i
                        nc.tensor.matmul(out[:, 2 * i * P:(2 * i + 1) * P], mp[:, h, :], tu[:, h, 0, :],
                                         start=True, stop=True)
                        last = nc.tensor.matmul(out[:, (2 * i + 1) * P:(2 * i + 2) * P], tu[:, h, 0, :], mp[:, h, :],
                                                start=True, stop=True)
                    last.then_inc(tu_filled, 1)
                    fill(4 + q, 12)

            def correct(t, par_):
                n = len(levels)
                for b in range(4):
                    pe.wait_ge(tu_taken, t * TU_USES + (8 * (n - 1) + 2 * b + 2))
                    pe.wait_ge(m_ready, t * M_USES + (4 * n + b - 1))
                    for i in range(4):
                        h = 4 * b + i
                        last = nc.tensor.matmul(pm[b % 2][:, i * P:(i + 1) * P], sc[par_][:, h, 0, :], ufin[:, h, :],
                                                start=True, stop=True)
                    last.then_inc(m_filled, 1)
                for b in range(4):
                    pe.wait_ge(m_ready, t * M_USES + (4 * n + b + 1))
                    pe.wait_ge(tu_taken, t * TU_USES + (8 * n + b - 1))
                    for i in range(4):
                        h = 4 * b + i
                        last = nc.tensor.matmul(ptu[b % 2][:, i * P:(i + 1) * P], tu[:, h, 0, :], mp[:, h, :],
                                                start=True, stop=True)
                    last.then_inc(tu_filled, 1)

            def pair_cols(j):
                return slice((j % 4) * P, (j % 4 + 1) * P)

            def from_state(c, c_par, which, j, slot):
                out = pch[j // 4][:, pair_cols(j)]
                if not sample:
                    nc.tensor.matmul(out, fac[c_par][:, which, j, :], st[:, j, :], start=True, stop=False)
                    return
                pe.wait_ge(wide_ready, slot + 1)
                for b in range(DEC):
                    nc.tensor.matmul(out, wide[:, slot % 2, b, :], st[:, j, b, :], start=(b == 0), stop=False)

            def add_heads(j, parts, stop=True):
                n = [(h, *p) for h in (2 * j, 2 * j + 1) for p in parts]
                for i, (h, lhsT, rhs) in enumerate(n):
                    cols = slice((h % 8) * HD, (h % 8 + 1) * HD)
                    last = nc.tensor.matmul(pch[j // 4][:, cols], lhsT(h), rhs[:, h * HD:(h + 1) * HD],
                                            start=False, stop=(i == len(n) - 1))
                return last

            def chain(t, par_, part, j):
                c_par = 0 if sample else 1 - par_
                first, final = j == 0, j == NB - 1
                if part == "x":
                    if first:
                        pe.wait_ge(tok_loaded, t * 48)
                        if sample:
                            pe.wait_ge(bd_taken, 2 * NB)
                        else:
                            wait(pe, state_ready, t - 1)
                    from_state(t - 1, c_par, A_, j, j)
                    last = add_heads(j, [(lambda h: sc[c_par][:, h, 2, :], tok[:, 2, :])])
                    last.then_inc(x_filled, 1)
                if part == "sa":
                    if first:
                        pe.wait_ge(x_ready, t * 2)
                        pe.wait_ge(tu_taken, t * TU_USES)
                    for h in (2 * j, 2 * j + 1):
                        last = nc.tensor.matmul(pch[h // 8][:, (h % 8) * HD:(h % 8 + 1) * HD], ufin[:, h, :],
                                                xs[:, h * HD:(h + 1) * HD], start=True, stop=True)
                    if final:
                        last.then_inc(sa_filled, 1)
                if part == "o":
                    if first:
                        pe.wait_ge(sa_ready, t * 2)
                    from_state(t - 1, c_par, R_, j, NB + j)
                    last = add_heads(j, [(lambda h: sc[c_par][:, h, 1, :], sa), (lambda h: sc[c_par][:, h, 3, :], tok[:, 2, :])])
                    if sample:
                        last.then_inc(wide_used, 1)
                    elif final:
                        last.then_inc(o_filled, 1)
                if part == "p":
                    if first:
                        pe.wait_ge(o_ready, t * 2)
                    cols = slice(j * P, (j + 1) * P)
                    if not sample:
                        out = pch[j // 4][:, pair_cols(j)]
                        nc.tensor.matmul(out, tok[:, 0, cols], sa[:, cols], start=True, stop=False)
                        last = nc.tensor.matmul(out, tok[:, 1, cols], tok[:, 2, cols], start=False, stop=True)
                        if final:
                            last.then_inc(p_filled, 1)
                        return
                    pe.wait_ge(wide_ready, 2 * NB + j + 1)
                    pe.wait_ge(wide_v_ready, j + 1)
                    wait(pe, state_sum, 4 * j)
                    for q in range(2):
                        for i in range(2):
                            last = nc.tensor.matmul(pch[q][:, :], tok[:, i, cols], wide[:, i, 4 * q:4 * q + 4, :],
                                                    start=(i == 0), stop=(i == 1))
                    last.then_inc(p_filled, 1)
                    if j > 0:
                        turn_states(j - 1)
                    if final:
                        turn_states(j)

            def turn_states(j):
                pe.wait_ge(state_ready, j + 1)
                wait(pe, out_ready, 2 * j)
                for b in range(DEC):
                    last = nc.tensor.transpose(psc[b // 4][:, (b % 4) * P:(b % 4 + 1) * P], st[:, j, b, :], m["ident"])
                last.then_inc(out_filled, 1)

            def step(t, par_):
                def chain_parts(units):
                    for unit in units:
                        if unit and has_chain(t):
                            chain(t, par_, *unit)

                if has_tile(t):
                    scores(t, par_)
                    turn(t, par_)
                chain_parts([("x", j) for j in range(4)])
                for l, units in enumerate(CHAIN_PLAN):
                    if has_tile(t) and l < len(levels):
                        share = lambda k, n: chain_parts(units[len(units) * k // n:len(units) * (k + 1) // n])
                        level(t, par_, l, share)
                    else:
                        chain_parts(units)
                    if has_tile(t) and l == STAGES - 1:
                        correct(t, par_)

            if not sample:
                pe.wait_ge(setup, 5)
            if sample:
                for j in range(NB):
                    for e in range(2):
                        pe.wait_ge(bd_ready[e], j + 1)
                    wait(pe, bd_taken, 2 * j)
                    for b in range(DEC):
                        last = nc.tensor.transpose(pch[b // 4][:, (b % 4) * P:(b % 4 + 1) * P], raw_bds[j % 2][:, b, :], m["ident"])
                    last.then_inc(bd_filled, 1)
            over(pe, step)
            if not sample:
                pe.wait_ge(state_ready, T)
                pe.wait_ge(sc_taken, T * SCORE_USES)
                for j in range(NB):
                    last = nc.tensor.transpose(psc[j // 4][:, pair_cols(j)], st[:, j, :], m["ident"])
                last.then_inc(out_filled, 1)

        @block.scalar
        def _(act):
            def take_tu(t, l):
                for q in range(8):
                    act.wait_ge(tu_filled, t * TU_USES + (8 * l + q + 1))
                    if l == len(levels) - 1:
                        src = ptu[q % 2][:, :].rearrange("p (h i c) -> p h i c", h=2, i=2)
                        nc.scalar.copy(tu[:, 2 * q:2 * q + 2, 0, :], src[:, :, 0, :])
                        nc.scalar.copy(ufin[:, 2 * q:2 * q + 2, :], src[:, :, 1, :]).then_inc(tu_taken, 1)
                        continue
                    dst = tu[:, 2 * q:2 * q + 2, :, :].rearrange("p h i c -> p (h i c)")
                    nc.scalar.copy(dst, ptu[q % 2][:, :]).then_inc(tu_taken, 1)

            def take(dst, ready, scale=1.0):
                for i in range(2):
                    nc.scalar.mul(dst[:, i * HALF:(i + 1) * HALF], pch[i][:, :], scale).then_inc(ready, 1)

            def chain(t, part):
                if part == "x":
                    act.wait_ge(x_filled, t * NB)
                    wait(act, sqsum_ready, t - 1)
                    take(xs, x_ready)
                if part == "sa":
                    act.wait_ge(sa_filled, t)
                    take(sa, sa_ready, -1.0)
                if part == "o":
                    if sample:
                        act.wait_ge(wide_used, NB)
                    else:
                        act.wait_ge(o_filled, t)
                    wait(act, d_ready, t - 1)
                    take(o, o_ready)
                if part == "square":
                    act.wait_ge(d_ready, t)
                    nc.scalar.square(xs[:, :], tmp[:, :]).then_inc(sq_ready, 1)
                if part == "root":
                    act.wait_ge(var_ready, t)
                    nc.scalar.activation(s2[:, :], s2[:, :], ACT.Sqrt).then_inc(std_ready, 1)

            def step(t, par_):
                parts = ["x", "sa", None, "o", None, "square", "root"] if has_chain(t) else [None] * STAGES
                for l in range(STAGES):
                    if has_tile(t) and l < len(levels):
                        take_tu(t, l)
                    if parts[l]:
                        chain(t, parts[l])

            if sample:
                for j in range(NB):
                    act.wait_ge(bd_filled, j + 1)
                    for q in range(2):
                        nc.scalar.copy(st[:, j, 4 * q:4 * q + 4, :].rearrange("p b c -> p (b c)"), pch[q][:, :]).then_inc(bd_taken, 1)
            over(act, step)

        @block.gpsimd
        def _(pool):
            signs = ["s_neg_lower", "s_incl", "s_strict", "s_incl"] if sample else ["neg_lower", "incl", "strict", "incl"]
            for i, name in enumerate(signs):
                nc.gpsimd.tensor_copy(quad[:, i, :], m[name]).then_inc(setup, 1)
                pool.wait_ge(setup, i + 1)
            if sample:
                nc.gpsimd.memset(seq_cols[:, :, :], 1.0).then_inc(setup, 1)
                pool.wait_ge(setup, 5)
                nc.gpsimd.affine_select(out=seq_cols[:, :, :], in_=seq_cols[:, :, :], compare_op=ALU.is_ge, fill=0.0, base=0,
                                        pattern=[[-DSEQ, DEC], [1, P]], channel_multiplier=0).then_inc(setup, 1)
                pool.wait_ge(setup, 6)
                nc.gpsimd.affine_select(out=seq_cols[:, :, :], in_=seq_cols[:, :, :], compare_op=ALU.is_ge, fill=0.0, base=DSEQ - 1,
                                        pattern=[[DSEQ, DEC], [-1, P]], channel_multiplier=0).then_inc(setup, 1)
                pool.wait_ge(setup, 7)

            def negated_a(t, par_):
                for b in range(4):
                    heads = slice(4 * b, 4 * b + 4)
                    pool.wait_ge(sc_taken, t * SCORE_USES + (4 * b + 4))
                    a = sc[par_][:, heads, 0, :]
                    nc.gpsimd.tensor_tensor(a, a, m["ident"].unsqueeze(1).to_broadcast([P, 4, P]), ALU.subtract).then_inc(nega_ready, 1)
                    pool.wait_ge(nega_ready, t * 4 + (b + 1))
                    nc.gpsimd.tensor_tensor(tu[:, heads, 0, :], a, m["lev1T"].unsqueeze(1).to_broadcast([P, 4, P]),
                                            ALU.mult).then_inc(t1_ready, 1)
                    nc.gpsimd.tensor_copy(na[:, heads, :], a).then_inc(na_ready, 1)

            def per_head(col):
                return col.unsqueeze(2).to_broadcast([P, NH, HD])

            def by_head(ap):
                return ap.rearrange("p (h n) -> p h n", n=HD)

            def step(t, par_):
                if has_tile(t):
                    negated_a(t, par_)
                if not has_chain(t):
                    return
                if sample:
                    pool.wait_ge(fac_loaded[0], 32)
                    for j in range(NB):
                        spread_after_x(j)
                    for j in range(NB):
                        spread_after_o(j)
                pool.wait_ge(mean_ready, t)
                wait(pool, y_stored, (t - 1) * 16)
                nc.gpsimd.tensor_tensor(by_head(tmp[:, :]), by_head(o[:, :]), per_head(s1[:, :]), ALU.subtract).then_inc(d_ready, 1)
                pool.wait_ge(rstd_ready, t)
                nc.gpsimd.tensor_tensor(by_head(tmp[:, :]), by_head(tmp[:, :]), per_head(s2[:, :]), ALU.mult).then_inc(dn_ready, 1)
                pool.wait_ge(dn_ready, t)
                pool.wait_ge(gates_loaded, t * 32)
                nc.gpsimd.tensor_tensor(tmp[:, :], tmp[:, :], gates[:, 0, :], ALU.mult).then_inc(ymul_ready, 1)
                pool.wait_ge(ymul_ready, t)
                nc.gpsimd.tensor_tensor(tmp[:, :], tmp[:, :], gates[:, 1, :], ALU.add).then_inc(y_ready, 1)
                if sample:
                    for j in range(NB):
                        cols = slice(j * P, (j + 1) * P)
                        wait(pool, p_filled, j)
                        nc.gpsimd.tensor_tensor(wide[:, 0, :, :], sa[:, cols].unsqueeze(1).to_broadcast([P, DEC, P]),
                                                m.seq_rows[:, :].unsqueeze(2).to_broadcast([P, DEC, P]), ALU.mult).then_inc(wide_ready, 1)
                        pool.wait_ge(wide_ready, 2 * NB + j + 1)

            def spread_after_x(j):
                if j >= 2:
                    pool.wait_ge(x_filled, j - 1)
                nc.gpsimd.tensor_tensor(wide[:, j % 2, :, :], fac[0][:, A_, j, :].unsqueeze(1).to_broadcast([P, DEC, P]),
                                        seq_cols[:, :, :], ALU.mult).then_inc(wide_ready, 1)

            def spread_after_o(j):
                pool.wait_ge(wide_ready, NB + j)
                if j < 2:
                    pool.wait_ge(x_filled, NB - 1 + j)
                else:
                    pool.wait_ge(wide_used, j - 1)
                nc.gpsimd.tensor_tensor(wide[:, j % 2, :, :], fac[0][:, R_, j, :].unsqueeze(1).to_broadcast([P, DEC, P]),
                                        seq_cols[:, :, :], ALU.mult).then_inc(wide_ready, 1)

            over(pool, step)

        @block.vector
        def _(dve):
            def take_scores(t, par_):
                for h in range(NH):
                    dve.wait_ge(sc_filled, t * SCORE_USES + (h + 1))
                    nc.vector.tensor_tensor(sc[par_][:, h, :, :], psc[h % 2][:, :].rearrange("p (i c) -> p i c", i=4),
                                            quad[:, :, :], ALU.mult).then_inc(sc_taken, 1)

            def take_turned(t):
                for b in range(4):
                    dve.wait_ge(sc_filled, t * SCORE_USES + (NH + b + 1))
                    nc.vector.tensor_tensor(tu[:, 4 * b:4 * b + 4, 1, :], psc[b % 2][:, :].rearrange("p (i c) -> p i c", i=4),
                                            m["lev1"].unsqueeze(1).to_broadcast([P, 4, P]), ALU.mult).then_inc(sc_taken, 1)

            def take_m(t, l):
                for b in range(4):
                    dve.wait_ge(m_filled, t * M_USES + (4 * l + b + 1))
                    nc.vector.tensor_tensor(mp[:, 4 * b:4 * b + 4, :], pm[b % 2][:, :].rearrange("p (i c) -> p i c", i=4),
                                            m[f"lev{levels[l]}"].unsqueeze(1).to_broadcast([P, 4, P]), ALU.mult).then_inc(m_ready, 1)

            def take_residual(t):
                for b in range(4):
                    dve.wait_ge(m_filled, t * M_USES + (4 * len(levels) + b + 1))
                    nc.vector.tensor_tensor(mp[:, 4 * b:4 * b + 4, :], pm[b % 2][:, :].rearrange("p (i c) -> p i c", i=4),
                                            m["ident"].unsqueeze(1).to_broadcast([P, 4, P]), ALU.add).then_inc(m_ready, 1)

            def take_corrected(t):
                for b in range(4):
                    dve.wait_ge(tu_filled, t * TU_USES + (8 * len(levels) + b + 1))
                    nc.vector.tensor_tensor(ufin[:, 4 * b:4 * b + 4, :], ptu[b % 2][:, :].rearrange("p (i c) -> p i c", i=4),
                                            ufin[:, 4 * b:4 * b + 4, :], ALU.add).then_inc(tu_taken, 1)

            def chain(t, par_, part):
                c_par = 0 if sample else 1 - par_
                if part == "mean":
                    dve.wait_ge(o_ready, t * 2)
                    wait(dve, d_ready, t - 1)
                    nc.vector.tensor_reduce(s1[:, :], o[:, :].rearrange("p (h n) -> p h n", n=HD), X, ALU.add).then_inc(sum_ready, 1)
                    dve.wait_ge(sum_ready, t)
                    nc.vector.tensor_scalar(s1[:, :], s1[:, :], 1.0 / HD, None, ALU.mult).then_inc(mean_ready, 1)
                if part == "state" and not sample:
                    dve.wait_ge(p_filled, t)
                    for q in range(2):
                        for e in range(2):
                            s = st[64 * e:64 * e + 64, 4 * q:4 * q + 4, 64 * e:64 * e + 64]
                            d = pch[q][64 * e:64 * e + 64, :].rearrange("p (j c) -> p j c", j=4)[:, :, 64 * e:64 * e + 64]
                            nc.vector.tensor_tensor(s, d, s, ALU.add).then_inc(state_sum, 1)
                    dve.wait_ge(state_sum, t * 4)
                    dve.wait_ge(f_ready, t)
                    for e in range(2):
                        s = st[64 * e:64 * e + 64, :, 64 * e:64 * e + 64]
                        last = nc.vector.tensor_tensor(s, s, f[64 * e:64 * e + 64, :].unsqueeze(2).to_broadcast([64, NB, 64]), ALU.mult)
                    last.then_inc(state_ready, 1)
                if part == "var":
                    dve.wait_ge(sq_ready, t)
                    wait(dve, dn_ready, t - 1)
                    nc.vector.tensor_reduce(s2[:, :], xs[:, :].rearrange("p (h n) -> p h n", n=HD), X, ALU.add).then_inc(sqsum_ready, 1)
                    dve.wait_ge(sqsum_ready, t)
                    nc.vector.tensor_scalar(s2[:, :], s2[:, :], 1.0 / HD, GN_EPS, ALU.mult, ALU.add).then_inc(var_ready, 1)
                if part == "rstd":
                    dve.wait_ge(std_ready, t)
                    nc.vector.reciprocal(s2[:, :], s2[:, :]).then_inc(rstd_ready, 1)

            def decay_factor(t, par_):
                if has_tile(t):
                    dve.wait_ge(fac_loaded[par_], fac_loads(t, par_))
                    nc.vector.tensor_tensor(f[:, :], dec[1 - par_][:, :, 1], dec[par_][:, :, 0], ALU.mult).then_inc(f_ready, 1)
                else:
                    nc.vector.tensor_copy(f[:, :], dec[1 - par_][:, :, 1]).then_inc(f_ready, 1)

            def step(t, par_):
                if has_tile(t):
                    take_scores(t, par_)
                    take_turned(t)
                if has_chain(t) and not sample:
                    decay_factor(t, par_)
                parts = [None, None, None, None, "mean", "state", "rstd"] if has_chain(t) else [None] * STAGES
                for l in range(STAGES):
                    if has_tile(t) and l < len(levels):
                        take_m(t, l)
                    if l == STAGES - 1:
                        if has_tile(t):
                            take_residual(t)
                        if has_chain(t):
                            chain(t, par_, "var")
                        if has_tile(t):
                            take_corrected(t)
                    if parts[l]:
                        chain(t, par_, parts[l])

            if sample:
                for i in range(2):
                    nc.vector.memset(raw_bds[i][:, :, :], 0.0).then_inc(bd_zero, 1)
                dve.wait_ge(bd_zero, 2)
                for j in range(NB):
                    dve.wait_ge(raw_loaded[j % RAWS], 16 * DEC * (j // RAWS + 1))
                    wait(dve, bd_filled, j - 1)
                    nc.vector.tensor_copy(raw_bds[j % 2][0:64, :, 0:64], raws[j % RAWS][0:64, :, :]).then_inc(bd_ready[0], 1)
                    nc.vector.tensor_copy(raw_bds[j % 2][64:P, :, 64:P], raws[j % RAWS][64:P, :, :]).then_inc(bd_ready[1], 1)
            dve.wait_ge(setup, 4)
            if sample:
                dve.wait_ge(bd_taken, 2 * NB)
            else:
                nc.vector.memset(st[:, :, :], 0.0).then_inc(setup, 1)
                dve.wait_ge(setup, 5)
            over(dve, step)
            def take_states(j):
                dve.wait_ge(out_filled, j + 1)
                wait(dve, state_stored, 16 * DEC * j)
                for e in range(2):
                    for q in range(2):
                        d = psc[q][64 * e:64 * e + 64, :].rearrange("p (b c) -> p b c", b=4)[:, :, 64 * e:64 * e + 64]
                        last = nc.vector.tensor_copy(raw[64 * e:64 * e + 64, 4 * q:4 * q + 4, :], d)
                    last.then_inc(out_ready, 1)

            def spread_v(j):
                nc.vector.tensor_tensor(wide[:, 1, :, :], tok[:, 2, j * P:(j + 1) * P].unsqueeze(1).to_broadcast([P, DEC, P]),
                                        m.seq_rows[:, :].unsqueeze(2).to_broadcast([P, DEC, P]), ALU.mult).then_inc(wide_v_ready, 1)

            if sample:
                dve.wait_ge(wide_used, NB)
                spread_v(0)
                for j in range(NB):
                    dve.wait_ge(p_filled, j + 1)
                    if j + 1 < NB:
                        spread_v(j + 1)
                    for q in range(2):
                        for e in range(2):
                            s = st[64 * e:64 * e + 64, j, 4 * q:4 * q + 4, 64 * e:64 * e + 64]
                            d = pch[q][64 * e:64 * e + 64, :].rearrange("p (b c) -> p b c", b=4)[:, :, 64 * e:64 * e + 64]
                            nc.vector.tensor_tensor(s, d, s, ALU.add).then_inc(state_sum, 1)
                    dve.wait_ge(state_sum, 4 * (j + 1))
                    for e in range(2):
                        s = st[64 * e:64 * e + 64, j, :, 64 * e:64 * e + 64]
                        last = nc.vector.tensor_tensor(s, s, dec[0][64 * e:64 * e + 64, j, :].unsqueeze(2).to_broadcast([64, DEC, 64]), ALU.mult)
                    last.then_inc(state_ready, 1)
                    if j > 0:
                        take_states(j - 1)
                take_states(NB - 1)
            else:
                dve.wait_ge(out_filled, 1)
                for q in range(2):
                    for e in range(2):
                        d = psc[q][64 * e:64 * e + 64, :].rearrange("p (j c) -> p j c", j=4)[:, :, 64 * e:64 * e + 64]
                        nc.vector.tensor_copy(raw[64 * e:64 * e + 64, 4 * q:4 * q + 4, :], d).then_inc(out_ready, 1)


def phase_a3_sample(nc, m, io, T):
    phase_a3(nc, m, io, T, sample=True)


class Uses:

    def __init__(self, order, full=2):
        self.order, self.full = order, full
        self.n = len(order(full))
        assert self.n % 2 == 0

    def before(self, t, what):
        if isinstance(t, int):
            return sum(len(self.order(i)) for i in range(t)) + self.order(t).index(what)
        start = sum(len(self.order(i)) for i in range(self.full))
        return t * self.n + (start - self.full * self.n + self.order(self.full).index(what))

    def bank(self, t, what):
        i = t if isinstance(t, int) else self.full
        return self.before(i, what) % 2


def iterations(eng, T, step):
    tiles(eng, T, step)
    step(T + 1, 1)
    step(T + 2, 0)


class Norm:

    def __init__(self, nc, sb, sem, name, gain, bias):
        self.nc, self.gain, self.bias = nc, gain, bias
        self.stats, self.mv, self.rstd = sb(name + "_stats", [P, 2, 6]), sb(name + "_mv", [P, 2]), sb(name + "_rstd", [P, 1])
        self.pause = sb(name + "_pause", [P, 1])
        self.stats_ready, self.mv_ready, self.var_ready = sem(name + "_stats"), sem(name + "_mv"), sem(name + "_var")
        self.std_ready, self.rstd_ready = sem(name + "_std"), sem(name + "_rstd")
        self.scaled_ready, self.gained_ready, self.done_ready = sem(name + "_scaled"), sem(name + "_gained"), sem(name + "_done")

    def statistics(self, dve, buf, n):
        nc = self.nc
        for h in range(2):
            nc.vector.bn_stats(self.stats[:, h, :], buf[:, h * HALF:(h + 1) * HALF]).then_inc(self.stats_ready, 1)
        dve.wait_ge(self.stats_ready, n * 2 + 2)
        nc.vector.memset(self.pause[:, :], 0.0)
        nc.vector.bn_aggr(self.mv[:, :], self.stats[:, :, :]).then_inc(self.mv_ready, 1)
        dve.wait_ge(self.mv_ready, n + 1)
        nc.vector.tensor_scalar(self.rstd[:, :], self.mv[:, 1:2], LN_EPS, None, ALU.add).then_inc(self.var_ready, 1)

    def root(self, act, n):
        act.wait_ge(self.var_ready, n + 1)
        self.nc.scalar.activation(self.rstd[:, :], self.rstd[:, :], ACT.Sqrt).then_inc(self.std_ready, 1)

    def scale(self, dve, dst, src, n):
        nc = self.nc
        dve.wait_ge(self.std_ready, n + 1)
        nc.vector.reciprocal(self.rstd[:, :], self.rstd[:, :]).then_inc(self.rstd_ready, 1)
        dve.wait_ge(self.rstd_ready, n + 1)
        nc.vector.tensor_scalar(dst, src, self.mv[:, 0:1], self.rstd[:, 0:1], ALU.subtract, ALU.mult).then_inc(self.scaled_ready, 1)

    def apply(self, pool, buf, n):
        nc = self.nc
        pool.wait_ge(self.scaled_ready, n + 1)
        nc.gpsimd.tensor_tensor(buf, buf, self.gain, ALU.mult).then_inc(self.gained_ready, 1)
        pool.wait_ge(self.gained_ready, n + 1)
        nc.gpsimd.tensor_tensor(buf, buf, self.bias, ALU.add).then_inc(self.done_ready, 1)


def phase_out(nc, m, io, T, layer):
    shared = layer == 0
    source = io["mixed" if shared else "gated"]
    w_out_src = io["a_w_out" if shared else "b_w_out"][0]
    with ExitStack() as ctx:
        def sb(name, shape, dtype=F32):
            return ctx.enter_context(nc.sbuf_tensor(f"out{layer}_" + name, shape, dtype))

        sems = []

        def sem(name):
            sems.append(ctx.enter_context(nc.semaphore(f"out{layer}_" + name)))
            return sems[-1]

        w_out = sb("w_out", [P, NB, D], FP22)
        w_out_low = sb("w_out_low", [P, NB, D], BF16)
        gate_cut = not shared
        w_gate = sb("w_gate", [P, NB, D], FP22 if gate_cut else F32)
        if gate_cut:
            w_gate_low = sb("w_gate_low", [P, NB, D], BF16)
        if shared:
            w_kv, cT, kv = sb("w_kv", [P, NB, HALF]), sb("cT", [P, NB, P]), sb("kv", [P, HALF])
        w_proj = sb("w_proj", [P, PLE // P, D])
        par = sb("par", [P, 4, D])
        x, y, z = ([sb(f"{n}{i}", [P, D]) for i in range(2)] for n in ("x", "y", "z"))
        p = [sb(f"p{i}", [P, PLE]) for i in range(2)]
        cut = lambda name: (sb(name + "_high", [P, NB, P], FP22), sb(name + "_low", [P, NB, P], FP22), sb(name + "_rough", [P, NB, P], BF16))
        yT = cut("yT")
        zT = cut("zT") if gate_cut else sb("zT", [P, NB, P])
        pT = sb("pT", [P, PLE // P, P])
        sig, c = sb("sig", [P, D]), sb("c", [P, D])

        bank = lambda name: ctx.enter_context(nc.psum_tensor(f"out{layer}_" + name, [P, 512], F32))
        pout, pgate, pturn = ([bank(f"{n}{i}") for i in range(2)] for n in ("pout", "pgate", "pturn"))
        pproj, pkv = bank("pproj"), bank("pkv")

        gate_w_loaded = [sem(f"gate_w_loaded{i}") for i in range(2)]
        w_loaded = sem("w_loaded")
        y_high, y_rough, z_high, z_rough = (sem(n) for n in ("y_high", "y_rough", "z_high", "z_rough"))
        y_loaded = [sem(f"y_loaded{i}") for i in range(2)]
        xp_loaded = [sem(f"xp_loaded{i}") for i in range(2)]
        turn_filled, turn_taken = sem("turn_filled"), sem("turn_taken")
        out_filled, z_ready = sem("out_filled"), sem("z_ready")
        gate_filled, sig_ready, proj_filled, u_ready, x1_ready = (
            sem(n) for n in ("gate_filled", "sig_ready", "proj_filled", "u_ready", "x1_ready"))
        kv_filled, kv_ready, kv_stored = sem("kv_filled"), sem("kv_ready"), sem("kv_stored")
        x1_stored = [sem(f"x1_stored{i}") for i in range(2)]
        norm = Norm(nc, sb, sem, "ln", par[:, 0, :], par[:, 1, :])
        kv_norm = Norm(nc, sb, sem, "kvln", par[:, 2, :], par[:, 3, :])

        def has(t):
            return not isinstance(t, int) or 0 <= t <= T

        def has_kv(t):
            return shared and has(t)

        def order(t):
            return ((["z0", "z1", "p0", "p1"] if has(t - 1) else []) + (["c0", "c1"] if has_kv(t - 2) else [])
                    + (["y0", "y1"] if has(t + 1) else []))

        turns = Uses(order)
        FIRST = 2

        def turned(t, what):
            return turns.before(t, what) + (FIRST + 1)

        halves = [slice(h * HALF, (h + 1) * HALF) for h in range(2)]
        blocks = lambda w: w.rearrange("(j p) n -> p j n", p=P)
        cuts = WeightCuts(nc, sem, [(blocks(w_out_src), w_out, w_out_low, halves[h]) for h in range(2)]
                          + ([(blocks(io["ple_w_gate"][layer]), w_gate, w_gate_low, halves[h]) for h in range(2)] if gate_cut else []),
                          (sig, c, z[1]))

        ctx.callback(clear_semaphores, nc, sems)
        block = ctx.enter_context(nc.Block())

        @block.sync
        def _(sp):
            def load_y(t, par_):
                sp.dma_start(y[par_][:, :], source[rows(t), :]).then_inc(y_loaded[par_], 16)

            def load_xp(t, par_):
                sample = is_sample(t, T)
                src = (io["x1"][rows(t), :] if not shared else io["x_sample"].rearrange("b i d -> (b i) d") if sample
                       else io["x_prompt"][0][rows(t), :])
                sp.dma_start(x[par_][:, :], src).then_inc(xp_loaded[par_], 16)
                src = io["p_sample"][layer].rearrange("b i d -> (b i) d") if sample else io["p_prompt"][layer, 0][rows(t), :]
                sp.dma_start(p[par_][:, :], src).then_inc(xp_loaded[par_], 16)

            load_y(0, 0)
            for h in range(2):
                cuts.load(sp, h)
            load_xp(0, 0)
            load_y(1, 1)
            load_xp(1, 1)
            for i, v in enumerate((io["ln_g"][layer:layer + 1, :], io["ln_b"][layer:layer + 1, :], io["kv_ln_g"].unsqueeze(0), io["kv_ln_b"].unsqueeze(0))):
                sp.dma_start(par[:, i, :], v.to_broadcast([P, D])).then_inc(w_loaded, 16)
            for h in range(2):
                if gate_cut:
                    cuts.load(sp, 2 + h)
                    continue
                sp.dma_start(w_gate[:, :, halves[h]], blocks(io["ple_w_gate"][layer])[:, :, halves[h]]).then_inc(gate_w_loaded[h], 16)
            sp.dma_start(w_proj[:, :, :], blocks(io["ple_w_proj"][layer])).then_inc(w_loaded, 16)
            if shared:
                sp.dma_start(w_kv[:, :, :], blocks(io["w_kv"])).then_inc(w_loaded, 16)

            def step(t, par_):
                if has(t + 2):
                    wait(sp, turn_filled, FIRST if isinstance(t, int) and t == 0 else turned(t - 1, "y1"))
                    load_y(t + 2, par_)
                if has(t - 1) and not (isinstance(t, int) and t == 0):
                    if has(t + 1):
                        sp.wait_ge(turn_filled, turned(t, "p1"))
                        load_xp(t + 1, 1 - par_)
                    sp.wait_ge(x1_ready, t)
                    dst = (io["x1"][rows(t - 1), :] if shared else io["y_sample"].rearrange("b i d -> (b i) d")
                           if is_sample(t - 1, T) else io["y_prompt"][0][rows(t - 1), :])
                    sp.dma_start(dst, z[1 - par_][:, :]).then_inc(x1_stored[1 - par_], 16)
                if has_kv(t - 2):
                    sp.wait_ge(kv_ready, t - 1)
                    sp.dma_start(io["kv"][rows(t - 2), :], kv[:, :]).then_inc(kv_stored, 16)
                    if isinstance(t, int) and t in (T + 1, T + 2):
                        for i, name in enumerate(("prompt_k", "prompt_v") if t == T + 1 else ("sample_k", "sample_v")):
                            dst = io[name].rearrange("a b h d -> (a b) (h d)")
                            sp.dma_start(dst, kv[:, i * 256:(i + 1) * 256]).then_inc(kv_stored, 16)

            iterations(sp, T, step)
            if shared:
                sp.wait_ge(kv_stored, 16 * (T + 1) + 64)
            sp.wait_ge(x1_stored[0], 16 * (T // 2 + 1))
            sp.wait_ge(x1_stored[1], 16 * (T // 2))

        @block.tensor
        def _(pe):
            def turn(src, n, i, value):
                wait(pe, turn_taken, value - 2)
                for k in range(n):
                    j = i * n + k
                    last = nc.tensor.transpose(pturn[i][:, k * P:(k + 1) * P], src[:, j * P:(j + 1) * P], m["ident"])
                last.then_inc(turn_filled, 1)

            def step(t, par_):
                second = isinstance(t, int) and t == 1

                def turn_z():
                    pe.wait_ge(norm.done_ready, t)
                    for i in range(2):
                        turn(z[1 - par_], HB, i, turned(t, f"z{i}"))

                if has(t - 1) and not second:
                    turn_z()
                for h in range(2):
                    if has(t):
                        if isinstance(t, int) and t == 0:
                            cuts.wait_for(pe, h)
                        pe.wait_ge(turn_taken, FIRST if isinstance(t, int) and t == 0 else turned(t - 1, "y1"))
                        pe.wait_ge(y_rough, t + 1)
                        wait(pe, z_ready, t * 2 - (1 - h))
                        gemm_of_parts(nc, pout[h][:, :], yT, (w_out, w_out_low), halves[h]).then_inc(out_filled, 1)
                if second:
                    turn_z()
                if has(t - 1):
                    pe.wait_ge(xp_loaded[1 - par_], of_parity(t - 1, 1 - par_, 32) + 32)
                    for i in range(2):
                        turn(p[1 - par_], 1, i, turned(t, f"p{i}"))
                for h in range(2):
                    cols = slice(h * HALF, (h + 1) * HALF)
                    if isinstance(t, int) and t == 1:
                        if gate_cut:
                            cuts.wait_for(pe, 2 + h)
                        else:
                            pe.wait_ge(gate_w_loaded[h], 16)
                        pe.wait_ge(w_loaded, 16 * (6 if shared else 5))
                    if has(t - 1):
                        pe.wait_ge(turn_taken, turned(t, "z1"))
                        wait(pe, sig_ready, t * 2 - (3 - h))
                        if gate_cut:
                            pe.wait_ge(z_rough, t)
                            last = gemm_of_parts(nc, pgate[h][:, :], zT, (w_gate, w_gate_low), cols)
                        else:
                            last = gemm(nc, pgate[h][:, :], zT, w_gate, cols)
                        last.then_inc(gate_filled, 1)
                        pe.wait_ge(turn_taken, turned(t, "p1"))
                        wait(pe, u_ready, t * 2 - (2 - h))
                        gemm(nc, pproj[:, :], pT, w_proj, cols).then_inc(proj_filled, 1)
                    if has_kv(t - 2) and h == 0:
                        pe.wait_ge(kv_norm.done_ready, t - 1)
                        for i in range(2):
                            turn(c, HB, i, turned(t, f"c{i}"))
                    if has(t + 1) and h == 0:
                        pe.wait_ge(y_loaded[1 - par_], of_parity(t + 1, 1 - par_, 16) + 16)
                        for i in range(2):
                            turn(y[1 - par_], HB, i, turned(t, f"y{i}"))
                if has_kv(t - 2):
                    pe.wait_ge(turn_taken, turned(t, "c1"))
                    wait(pe, kv_ready, t - 2)
                    gemm(nc, pkv[:, :], cT, w_kv, slice(0, HALF)).then_inc(kv_filled, 1)

            pe.wait_ge(y_loaded[0], 16)
            for i in range(2):
                turn(y[0], HB, i, i + 1)
            iterations(pe, T, step)

        @block.scalar
        def _(act):
            def take(dst, i, n, value):
                act.wait_ge(turn_filled, value)
                wait(act, turn_taken, value - 1)
                nc.scalar.copy(dst[:, i * n:(i + 1) * n, :].rearrange("p j t -> p (j t)"), pturn[i][:, 0:n * P]).then_inc(turn_taken, 1)

            def take_high(parts, i, value, ready):
                act.wait_ge(turn_filled, value)
                nc.scalar.copy(parts[0][:, i * HB:(i + 1) * HB, :].rearrange("p j t -> p (j t)"), pturn[i][:, :]).then_inc(ready, 1)

            def rough(parts, high, ready, n):
                act.wait_ge(high, n * 2)
                nc.scalar.copy(parts[2][:, :, :], parts[0][:, :, :].bitcast(F32)).then_inc(ready, 1)

            def step(t, par_):
                if has(t - 1):
                    for i in range(2):
                        if gate_cut:
                            take_high(zT, i, turned(t, f"z{i}"), z_high)
                        else:
                            take(zT, i, HB, turned(t, f"z{i}"))
                    if gate_cut:
                        rough(zT, z_high, z_rough, t)
                if has(t):
                    norm.root(act, t)
                if has(t - 1):
                    for i in range(2):
                        take(pT, i, 1, turned(t, f"p{i}"))
                for h in range(2):
                    if has(t - 1):
                        act.wait_ge(gate_filled, t * 2 - (1 - h))
                        wait(act, x1_ready, t - 1)
                        nc.scalar.activation(sig[:, h * HALF:(h + 1) * HALF], pgate[h][:, :], ACT.Sigmoid).then_inc(sig_ready, 1)
                    if has_kv(t - 2) and h == 0:
                        for i in range(2):
                            take(cT, i, HB, turned(t, f"c{i}"))
                    if has(t + 1) and h == 0:
                        for i in range(2):
                            take_high(yT, i, turned(t, f"y{i}"), y_high)
                        rough(yT, y_high, y_rough, t + 2)
                if isinstance(t, int) and t == 0 and gate_cut:
                    for i in (2, 3):
                        cuts.take_high(act, i)
                if has_kv(t - 1):
                    kv_norm.root(act, t - 1)
                if has_kv(t - 2):
                    act.wait_ge(kv_filled, t - 1)
                    wait(act, kv_stored, t * 16 - 32 + (32 if is_sample(t - 2, T) else 0))
                    nc.scalar.copy(kv[:, :], pkv[:, :]).then_inc(kv_ready, 1)

            for i in range(2):
                take_high(yT, i, i + 1, y_high)
            rough(yT, y_high, y_rough, 1)
            for h in range(2):
                cuts.take_high(act, h)
            iterations(act, T, step)

        @block.gpsimd
        def _(pool):
            pool.wait_ge(w_loaded, 16 * (6 if shared else 5))

            def step(t, par_):
                if has(t):
                    norm.apply(pool, z[par_][:, :], t)
                if has_kv(t - 1):
                    kv_norm.apply(pool, c[:, :], t - 1)

            iterations(pool, T, step)

        @block.vector
        def _(dve):
            def take_low(parts, value, high, n):
                for i in range(2):
                    dst = parts[1][:, i * HB:(i + 1) * HB, :].rearrange("p j t -> p (j t)")
                    taken = parts[0][:, i * HB:(i + 1) * HB, :].rearrange("p j t -> p (j t)").bitcast(F32)
                    dve.wait_ge(high, n * 2 - (1 - i))
                    wait(dve, turn_taken, value + (i - 2))
                    nc.vector.tensor_tensor(dst, pturn[i][:, :], taken, ALU.subtract).then_inc(turn_taken, 1)

            def step(t, par_):
                if has(t - 1) and gate_cut:
                    take_low(zT, turned(t, "z1"), z_high, t)
                if has(t):
                    dve.wait_ge(xp_loaded[par_], of_parity(t, par_, 32) + 32)
                    wait(dve, x1_stored[par_], of_parity(t, par_, 16))
                    if shared:
                        wait(dve, kv_norm.scaled_ready, t - 1)
                    for h in range(2):
                        cols = slice(h * HALF, (h + 1) * HALF)
                        dve.wait_ge(out_filled, t * 2 + (h + 1))
                        nc.vector.scalar_tensor_tensor(out=z[par_][:, cols], in0=x[par_][:, cols], scalar=ALPHA,
                                                       in1=pout[h][:, :], op0=ALU.mult, op1=ALU.add).then_inc(z_ready, 1)
                    dve.wait_ge(z_ready, t * 2 + 2)
                    norm.statistics(dve, z[par_], t)
                    norm.scale(dve, z[par_][:, :], z[par_][:, :], t)
                if has(t - 1):
                    for h in range(2):
                        cols = slice(h * HALF, (h + 1) * HALF)
                        dve.wait_ge(proj_filled, t * 2 - (1 - h))
                        dve.wait_ge(sig_ready, t * 2 - (1 - h))
                        nc.vector.tensor_tensor(sig[:, cols], sig[:, cols], pproj[:, :], ALU.mult).then_inc(u_ready, 1)
                        if h == 0 and has(t + 1):
                            take_low(yT, turned(t, "y1"), y_high, t + 2)
                elif has(t + 1):
                    take_low(yT, turned(t, "y1"), y_high, t + 2)
                if isinstance(t, int) and t == 0 and gate_cut:
                    for i in (2, 3):
                        cuts.take_low(dve, i)
                    cuts.wait_for(dve, 3)
                if has(t - 1):
                    dve.wait_ge(u_ready, t * 2)
                    zb = z[1 - par_]
                    nc.vector.tensor_tensor(zb[:, :], zb[:, :], sig[:, :], ALU.add).then_inc(x1_ready, 1)
                if has_kv(t - 1):
                    dve.wait_ge(x1_ready, t)
                    kv_norm.statistics(dve, zb, t - 1)
                    wait(dve, turn_filled, turned(t, "c1") if has_kv(t - 2) else 0)
                    kv_norm.scale(dve, c[:, :], zb[:, :], t - 1)

            take_low(yT, FIRST, y_high, 1)
            for h in range(2):
                cuts.take_low(dve, h)
            iterations(dve, T, step)


def phase_out_a(nc, m, io, T):
    phase_out(nc, m, io, T, 0)


def phase_out_b(nc, m, io, T):
    phase_out(nc, m, io, T, 1)


PAIRS = NH // 2
KEYS = P + DSEQ



def head_of(i, c):
    return i // 2 * 4 + c * 2 + i % 2


SLOPES = [2.0 ** (-8.0 * (h + 1) / NH) for h in range(NH)]


def attention_constants():
    import numpy as np
    q, k = np.arange(P)[:, None], np.arange(2 * P)[None, :] - P
    age = q // 64 - k // 64
    near = np.where((age >= 0) & (age <= 2), -np.abs(q - k), -1e30).astype(np.float32)
    row = np.arange(P)
    head = (row // DSEQ * 2)[:, None, None] + np.arange(2)[None, :, None]
    dist = np.abs((row % DSEQ)[:, None, None] + P - np.arange(KEYS)[None, None, :])
    bias = (-np.array(SLOPES)[head] * dist).astype(np.float32)
    return {"near": near, "sample_bias": np.ascontiguousarray(bias)}


def phase_b(nc, m, io, T):
    with ExitStack() as ctx:
        def sb(name, shape):
            return ctx.enter_context(nc.sbuf_tensor("b_" + name, shape, F32))

        sems = []

        def sem(name):
            sems.append(ctx.enter_context(nc.semaphore("b_" + name)))
            return sems[-1]

        twice = lambda name, shape: [sb(f"{name}{i}", shape) for i in range(2)]
        w = sb("w", [P, NB, 2 * D])
        near, sample_bias = sb("near", [P, 2 * P]), sb("sample_bias", [P, 2, KEYS])
        sink, neg_sink = twice("sink", [P, 4, 2, 2]), twice("neg_sink", [P, 4, 2, 2])
        x, xT = sb("x", [P, D]), sb("xT", [P, NB, P])
        kd = sb("kd", [P, 4, 2, HD])
        kT, v = twice("kT", [P, 4, P]), twice("v", [P, 4 * HD])
        qT, gate, y = twice("qT", [P, NB, P]), twice("gate", [P, D]), twice("y", [P, D])
        th = sb("th", [P, HALF])
        s, pT = twice("s", [P, 2, 2 * P]), twice("pT", [P, 4, P])
        mx, nm, den = sb("mx", [P, 2]), sb("nm", [P, 4, 2, 2]), sb("den", [P, 4, 2, 2])
        sunk, rden = sb("sunk", [P, 4, 2, 2]), sb("rden", [P, 4, 2, 2])
        each = lambda name, shape: [sb(f"{name}{i}", shape) for i in range(DEC)]
        kd_c, kd_n = each("kd_c", [P, 4, 2, HD]), each("kd_n", [DSEQ, 4, 2, HD])
        v_c, v_n, kT_s = each("v_c", [P, 4 * HD]), each("v_n", [DSEQ, 4 * HD]), each("kT_s", [P, 4, KEYS])

        bank = lambda name: ctx.enter_context(nc.psum_tensor("b_" + name, [P, 512], F32))
        ps, pturn, po = ([bank(f"{n}{i}") for i in range(2)] for n in ("ps", "pturn", "po"))
        pq, pg = bank("pq"), bank("pg")

        w_loaded, const_loaded, x_loaded, k_loaded, v_loaded = (
            sem(n + "_loaded") for n in ("w", "const", "x", "k", "v"))
        request_loaded = [sem(f"request_loaded{i}") for i in range(DEC)]
        neg_ready = sem("neg_ready")
        turn_filled, turn_taken = sem("turn_filled"), sem("turn_taken")
        q_filled, q_ready, gate_filled, th_ready, gate_ready = (
            sem(n) for n in ("q_filled", "q_ready", "gate_filled", "th_ready", "gate_ready"))
        s_filled, s_ready, mx_ready, nm_ready, e_ready, pv_filled = (
            sem(n) for n in ("s_filled", "s_ready", "mx_ready", "nm_ready", "e_ready", "pv_filled"))
        sum_ready, sunk_ready, den_ready, rden_ready, o_ready, y_ready = (
            sem(n) for n in ("sum_ready", "sunk_ready", "den_ready", "rden_ready", "o_ready", "y_ready"))
        attended_stored, attended_loaded = sem("attended_stored"), sem("attended_loaded")
        y_stored = [sem(f"y_stored{i}") for i in range(2)]

        def prompt(t):
            return not isinstance(t, int) or 0 <= t < T

        def order(t):
            if not isinstance(t, int) or t < T:
                return ([f"p{i}" for i in range(PAIRS)] + (["k0", "k1"] if prompt(t + 1) else [])
                        + (["x0", "x1"] if prompt(t + 1) else []))
            names = []
            for i in range(DEC + 3):
                names += [f"kc{i}", f"kn{i}"] if i < DEC else []
                names += [f"pc{i - 3}", f"pn{i - 3}"] if i >= 3 else []
            return names

        def flat(a):
            return a[:, :, :, :].rearrange("p g c h -> p (g c h)")

        def lined(q):
            return q[:, :, :].rearrange("p j t -> p (j t)")

        turns = Uses(order)
        FIRST = 6

        def turned(t, what):
            if isinstance(t, int) and t < 0:
                return {"x1": FIRST, "k1": 4}[what]
            return turns.before(t, what) + (FIRST + 1)

        ctx.callback(clear_semaphores, nc, sems)
        block = ctx.enter_context(nc.Block())

        @block.sync
        def _(sp):
            def load_x(t):
                sp.dma_start(x[:, :], io["x1"][rows(t), :]).then_inc(x_loaded, 16)

            def load_keys(dst, src, loaded):
                for c in range(2):
                    sp.dma_start(dst[:, :, c, :], src.rearrange("n (g d) -> n g d", d=HD)).then_inc(loaded, 16)

            def load_v(t, par_):
                sp.dma_start(v[par_][:, :], io["kv"][rows(t), 4 * HD:8 * HD]).then_inc(v_loaded, 16)

            load_x(0)
            wv = io["b_w_in"][0].rearrange("(j p) n -> p j n", p=P)
            for i in range(2):
                cols = slice(i * HALF, (i + 1) * HALF)
                sp.dma_start(w[:, :, cols], wv[:, :, cols]).then_inc(w_loaded, 16)
            load_keys(kd, io["kv"][rows(0), 0:4 * HD], k_loaded)
            load_v(0, 0)
            sp.dma_start(w[:, :, D:2 * D], wv[:, :, D:2 * D]).then_inc(w_loaded, 16)
            sp.dma_start(near[:, :], io["near"]).then_inc(const_loaded, 16)
            sp.dma_start(sample_bias[:, :, :], io["sample_bias"]).then_inc(const_loaded, 16)
            sp.dma_start(flat(sink[0]), io["b_sinks"].to_broadcast([P, NH])).then_inc(const_loaded, 16)
            for r in range(PAIRS):
                sp.dma_start(flat(sink[1])[r * DSEQ:(r + 1) * DSEQ, :].rearrange("t (b c) -> t b c", c=2),
                             io["b_sinks"][:, 2 * r:2 * r + 2].unsqueeze(1).to_broadcast([DSEQ, DEC, 2])).then_inc(const_loaded, 16)
            sp.wait_ge(turn_filled, 2)
            load_x(1)

            def load_request(b):
                new = slice(T * P + b * DSEQ, T * P + (b + 1) * DSEQ)
                load_keys(kd_c[b], io["cache_k"][b].rearrange("n g d -> n (g d)"), request_loaded[b])
                load_keys(kd_n[b], io["kv"][new, 0:4 * HD], request_loaded[b])
                sp.dma_start(v_c[b][:, :], io["cache_v"][b].rearrange("n g d -> n (g d)")).then_inc(request_loaded[b], 16)
                sp.dma_start(v_n[b][:, :], io["kv"][new, 4 * HD:8 * HD]).then_inc(request_loaded[b], 16)

            for b in range(DEC):
                load_request(b)

            def step(t, par_):
                if is_sample(t, T):
                    sp.wait_ge(o_ready, t * 2 + 2)
                    att = io["attended"].rearrange("(b t) (r c) -> r t b c", t=DSEQ, c=P)
                    for r in range(PAIRS):
                        sp.dma_start(att[r], y[par_][r * DSEQ:(r + 1) * DSEQ, :].rearrange("t (b c) -> t b c", c=P)).then_inc(attended_stored, 16)
                    sp.wait_ge(attended_stored, 16 * PAIRS)
                    sp.dma_start(x[:, :], io["attended"]).then_inc(attended_loaded, 16)
                else:
                    if prompt(t + 1):
                        wait(sp, turn_filled, turned(t - 1, "k1"))
                        load_keys(kd, io["kv"][rows(t + 1), 0:4 * HD], k_loaded)
                        wait(sp, turn_filled, turned(t - 1, "x1"))
                        load_x(t + 2)
                        sp.wait_ge(pv_filled, t * PAIRS + PAIRS)
                        load_v(t + 1, 1 - par_)
                sp.wait_ge(y_ready, t * 2 + 2)
                sp.dma_start(io["gated"][rows(t), :], y[par_][:, :]).then_inc(y_stored[par_], 16)

            tiles(sp, T, step)
            sp.wait_ge(y_stored[0], 16 * (T // 2 + 1))
            sp.wait_ge(y_stored[1], 16 * (T // 2))

        @block.tensor
        def _(pe):
            def turn(i, pieces, value):
                wait(pe, turn_taken, value - 2)
                for src, n, col in pieces:
                    last = nc.tensor.transpose(pturn[i][0:src.shape[1], col:col + n], src, m["ident"][0:n, 0:n])
                last.then_inc(turn_filled, 1)

            def turn_x(t, value):
                pe.wait_ge(x_loaded, t * 16 + 16)
                for i in range(2):
                    turn(i, [(x[:, (i * HB + j) * P:(i * HB + j + 1) * P], P, j * P) for j in range(HB)], value + (i - 1))

            def keys(kd_, g):
                return kd_[:, g, :, :].rearrange("n c d -> n (c d)")

            def turn_k(t, value):
                pe.wait_ge(k_loaded, t * 32 + 32)
                for i in range(2):
                    turn(i, [(keys(kd, 2 * i + g), P, g * P) for g in range(2)], value + (i - 1))

            def q_block(t, i):
                if i % HB == 0:
                    wait(pe, q_ready, t * 2 + i // HB)
                out = pq[:, i % HB * P:(i % HB + 1) * P]
                for j in range(NB):
                    last = nc.tensor.matmul(out, w[:, j, i * P:(i + 1) * P], xT[:, j, :], start=(j == 0), stop=(j == NB - 1))
                if i % HB == HB - 1:
                    last.then_inc(q_filled, 1)

            def gate_piece(t, i):
                h, first = i // HB, i % HB * 2
                if first == 0:
                    wait(pe, gate_ready, t * 2 + h)
                for j in (first, first + 1):
                    last = nc.tensor.matmul(pg[:, :], xT[:, j, :], w[:, j, D + h * HALF:D + (h + 1) * HALF],
                                            start=(j == 0), stop=(j == NB - 1))
                if j == NB - 1:
                    last.then_inc(gate_filled, 1)

            def scores(t, par_, i):
                wait(pe, s_ready, t * 2 * PAIRS + (i * 2 - 2))
                if i == 0:
                    pe.wait_ge(q_ready, t * 2 + 2)
                    pe.wait_ge(turn_taken, turned(t - 1, "k1"))
                half = slice(i % 2 * HD, (i % 2 + 1) * HD)
                for c in range(2):
                    for ring, at in ((1 - par_, 0), (par_, P)):
                        if at == 0 and isinstance(t, int) and t == 0:
                            continue
                        last = nc.tensor.matmul(ps[i % 2][:, c * 2 * P + at:c * 2 * P + at + P], qT[par_][half, i // 2 * 2 + c, :],
                                                kT[ring][half, i // 2, :], start=True, stop=True)
                last.then_inc(s_filled, 1)

            def weighted(t, par_, i):
                if i == 0:
                    pe.wait_ge(v_loaded, t * 16 + 16)
                if i % HB == 0:
                    wait(pe, o_ready, t * 2 + (i // HB - 1))
                pe.wait_ge(turn_taken, turned(t, f"p{i}"))
                first = isinstance(t, int) and t == 0
                for c in range(2):
                    col = head_of(i, c) % HH * HD
                    for k, ring in enumerate((1 - par_, par_)):
                        if k == 0 and first:
                            continue
                        last = nc.tensor.matmul(po[i // HB][:, col:col + HD], pT[i % 2][:, c * 2 + k, :],
                                                v[ring][:, i // 2 * HD:(i // 2 + 1) * HD], start=(k == 0 or first), stop=(k == 1))
                last.then_inc(pv_filled, 1)

            def prompt_step(t, par_):
                for i in range(PAIRS + 2):
                    if i < PAIRS:
                        scores(t, par_, i)
                    if 1 <= i <= PAIRS:
                        n = i - 1
                        pe.wait_ge(e_ready, t * 2 * PAIRS + (n * 2 + 2))
                        first = isinstance(t, int) and t == 0
                        turn(turns.bank(t, f"p{n}"), [(s[n % 2][:, c, k * P:(k + 1) * P], P, (c * 2 + k) * P)
                                                     for c in range(2) for k in range(1 if first else 0, 2)], turned(t, f"p{n}"))
                    if i < PAIRS:
                        if i == 0:
                            pe.wait_ge(turn_taken, turned(t - 1, "x1"))
                        q_block(t + 1, i)
                    if 2 <= i < PAIRS + 1:
                        weighted(t, par_, i - 2)
                    if i < PAIRS:
                        gate_piece(t + 1, i)
                    if prompt(t + 1):
                        if i == PAIRS:
                            turn_k(t + 1, turned(t, "k1"))
                        if i == PAIRS + 1:
                            turn_x(t + 2, turned(t, "x1"))
                weighted(t, par_, PAIRS - 1)

            def sample_step(t, par_):
                for i in range(DEC + 4):
                    if i < DEC:
                        pe.wait_ge(request_loaded[i], 96)
                        turn(turns.bank(t, f"kc{i}"), [(keys(kd_c[i], g), P, g * P) for g in range(4)], turned(t, f"kc{i}"))
                        turn(turns.bank(t, f"kn{i}"), [(keys(kd_n[i], g), DSEQ, g * DSEQ) for g in range(4)], turned(t, f"kn{i}"))
                    u = i - 2
                    if 0 <= u < PAIRS:
                        half, requests = slice(u % 2 * HD, (u % 2 + 1) * HD), (u // 2 * 2, u // 2 * 2 + 1)
                        pe.wait_ge(s_ready, t * 2 * PAIRS + u * 2 - 2)
                        if u == 0:
                            pe.wait_ge(q_ready, t * 2 + 2)
                        pe.wait_ge(turn_taken, turned(t, f"kn{requests[1]}"))
                        for c, b in enumerate(requests):
                            for g in range(4):
                                last = nc.tensor.matmul(ps[u % 2][g * 32:(g + 1) * 32, c * KEYS:(c + 1) * KEYS],
                                                        lined(qT[par_])[half, (4 * b + g) * 32:(4 * b + g + 1) * 32],
                                                        kT_s[b][half, g, :], start=True, stop=True)
                        last.then_inc(s_filled, 1)
                    u = i - 3
                    if 0 <= u < PAIRS:
                        pe.wait_ge(e_ready, t * 2 * PAIRS + u * 2 + 2)
                        e = lined(s[u % 2])
                        turn(turns.bank(t, f"pc{u}"), [(e[:, c * KEYS:c * KEYS + P], P, c * P) for c in range(2)], turned(t, f"pc{u}"))
                        turn(turns.bank(t, f"pn{u}"), [(e[:, c * KEYS + P:(c + 1) * KEYS], P, c * P) for c in range(2)], turned(t, f"pn{u}"))
                    u = i - 4
                    if 0 <= u < PAIRS:
                        if u % HB == 0:
                            pe.wait_ge(o_ready, t * 2 + u // HB - 1)
                        pe.wait_ge(turn_taken, turned(t, f"pn{u}"))
                        for c in range(2):
                            b, col = u // 2 * 2 + c, head_of(u, c) % HH * HD
                            for g in range(4):
                                mine, of_g = slice(g * 32, (g + 1) * 32), slice(g * HD, (g + 1) * HD)
                                out = po[u // HB][mine, col:col + HD]
                                nc.tensor.matmul(out, pT[u % 2][:, c, mine], v_c[b][:, of_g], start=True, stop=False)
                                last = nc.tensor.matmul(out, pT[u % 2][0:DSEQ, 2 + c, mine], v_n[b][:, of_g], start=False, stop=True)
                        last.then_inc(pv_filled, 1)

            turn_x(0, 2)
            turn_k(0, 4)
            pe.wait_ge(turn_taken, 2)
            pe.wait_ge(w_loaded, 16 * 2)
            for i in range(NB):
                q_block(0, i)
            pe.wait_ge(w_loaded, 16 * 3)
            for i in range(NB):
                gate_piece(0, i)
            turn_x(1, FIRST)
            tiles(pe, T, lambda t, par_: sample_step(t, par_) if is_sample(t, T) else prompt_step(t, par_))

        @block.scalar
        def _(act):
            def take(i, pieces, value):
                act.wait_ge(turn_filled, value)
                for dst, src in pieces:
                    last = nc.scalar.copy(dst, src)
                last.then_inc(turn_taken, 1)

            def take_x(value):
                for i in range(2):
                    take(i, [(xT[:, i * HB:(i + 1) * HB, :].rearrange("p j t -> p (j t)"), pturn[i][:, :])], value + (i - 1))

            def take_k(par_, value):
                for i in range(2):
                    take(i, [(kT[par_][:, 2 * i:2 * i + 2, :].rearrange("p g t -> p (g t)"), pturn[i][:, 0:2 * P])], value + (i - 1))

            def take_q(t, par_, h):
                act.wait_ge(q_filled, t * 2 + (h + 1))
                dst, src = qT[par_][:, h * HB:(h + 1) * HB, :], pq[:, :].rearrange("p (j t) -> p j t", t=P)
                if is_sample(t, T):
                    dst = lined(qT[par_]).rearrange("p (b j t) -> p j b t", b=DEC, t=DSEQ)[:, h * HB:(h + 1) * HB]
                    src = src.rearrange("p j (b t) -> p j b t", t=DSEQ)
                nc.scalar.activation(dst, src, ACT.Copy,
                                     scale=HD ** -0.5).then_inc(q_ready, 1)

            def gate_tanh(t, h):
                act.wait_ge(gate_filled, t * 2 + (h + 1))
                wait(act, gate_ready, t * 2 + h)
                nc.scalar.activation(th[:, :], pg[:, :], ACT.Tanh, scale=0.5).then_inc(th_ready, 1)

            def exps(t, i, keys):
                act.wait_ge(nm_ready, t * PAIRS + (i + 1))
                for c in range(2):
                    nc.scalar.activation(keys[c], keys[c], ACT.Exp, bias=flat(nm)[:, head_of(i, c):head_of(i, c) + 1],
                                         accum_out=flat(den)[:, head_of(i, c):head_of(i, c) + 1]).then_inc(e_ready, 1)

            def exp_sinks(t):
                act.wait_ge(sum_ready, t + 1)
                nc.scalar.activation(flat(sunk), flat(sunk), ACT.Exp).then_inc(sunk_ready, 1)

            def prompt_step(t, par_):
                first = isinstance(t, int) and t == 0
                for i in range(PAIRS + 1):
                    if i in (HB, PAIRS):
                        gate_tanh(t + 1, i // HB - 1)
                    if i >= 1:
                        n = i - 1
                        if n >= 2:
                            act.wait_ge(pv_filled, t * PAIRS + (n - 1))
                        else:
                            wait(act, pv_filled, t * PAIRS + (n - 1) if not first else 0)
                        b = turns.bank(t, f"p{n}")
                        pieces = ([(pT[n % 2][:, c * 2 + 1, :], pturn[b][:, (c * 2 + 1) * P:(c * 2 + 2) * P]) for c in range(2)] if first
                                  else [(pT[n % 2][:, :, :].rearrange("p k t -> p (k t)"), pturn[b][:, :])])
                        take(b, pieces, turned(t, f"p{n}"))
                    if i < PAIRS:
                        exps(t, i, [s[i % 2][:, c, P if first else 0:] for c in range(2)])
                    if i in (HB - 1, PAIRS - 1):
                        take_q(t + 1, 1 - par_, i // HB)
                exp_sinks(t)
                if prompt(t + 1):
                    take_k(1 - par_, turned(t, "k1"))
                    take_x(turned(t, "x1"))

            def sample_step(t, par_):
                for i in range(DEC + 3):
                    if i < DEC:
                        b, k = turns.bank(t, f"kc{i}"), kT_s[i]
                        take(b, [(k[:, :, 0:P], pturn[b][:, :].rearrange("p (g n) -> p g n", n=P))], turned(t, f"kc{i}"))
                        b = turns.bank(t, f"kn{i}")
                        take(b, [(k[:, :, P:KEYS], pturn[b][:, 0:4 * DSEQ].rearrange("p (g n) -> p g n", n=DSEQ))], turned(t, f"kn{i}"))
                    n = i - 3
                    if n >= 0:
                        b = turns.bank(t, f"pc{n}")
                        act.wait_ge(pv_filled, t * PAIRS + n - 1)
                        take(b, [(pT[n % 2][:, 0:2, :].rearrange("p c t -> p (c t)"), pturn[b][:, 0:2 * P])], turned(t, f"pc{n}"))
                        b = turns.bank(t, f"pn{n}")
                        take(b, [(pT[n % 2][0:DSEQ, 2:4, :].rearrange("p c t -> p (c t)"), pturn[b][0:DSEQ, 0:2 * P])], turned(t, f"pn{n}"))
                    n = i - 2
                    if 0 <= n < PAIRS:
                        exps(t, n, [lined(s[n % 2])[:, c * KEYS:(c + 1) * KEYS] for c in range(2)])
                exp_sinks(t)

            take_x(2)
            take_k(0, 4)
            for h in range(2):
                take_q(0, 0, h)
            for h in range(2):
                gate_tanh(0, h)
            take_x(FIRST)
            tiles(act, T, lambda t, par_: sample_step(t, par_) if is_sample(t, T) else prompt_step(t, par_))

        @block.vector
        def _(dve):
            def make_gate(t, par_, h):
                dve.wait_ge(th_ready, t * 2 + (h + 1))
                wait(dve, y_ready, t * 2 - 2 if not isinstance(t, int) or t > 1 else 0)
                nc.vector.scalar_tensor_tensor(out=gate[par_][:, h * HALF:(h + 1) * HALF], in0=th[:, :], scalar=1.0,
                                               in1=pg[:, :], op0=ALU.add, op1=ALU.mult).then_inc(gate_ready, 1)

            def maximum(t, i, keys, kind):
                dve.wait_ge(s_ready, t * 2 * PAIRS + (i * 2 + 2))
                wait(dve, nm_ready, t * PAIRS + i)
                nc.vector.tensor_reduce(mx[:, :], keys, X, ALU.max).then_inc(mx_ready, 1)
                dve.wait_ge(mx_ready, t * PAIRS + (i + 1))
                nc.vector.scalar_tensor_tensor(out=nm[:, i // 2, :, i % 2], in0=mx[:, :], scalar=-1.0, in1=neg_sink[kind][:, i // 2, :, i % 2],
                                               op0=ALU.mult, op1=ALU.min).then_inc(nm_ready, 1)

            def finish(t, par_, kind):
                dve.wait_ge(e_ready, t * 2 * PAIRS + 2 * PAIRS)
                nc.vector.tensor_tensor(flat(sunk), flat(nm), flat(sink[kind]), ALU.add).then_inc(sum_ready, 1)
                dve.wait_ge(sunk_ready, t + 1)
                nc.vector.tensor_tensor(flat(den), flat(den), flat(sunk), ALU.add).then_inc(den_ready, 1)
                dve.wait_ge(den_ready, t + 1)
                nc.vector.reciprocal(flat(rden), flat(den)).then_inc(rden_ready, 1)
                dve.wait_ge(rden_ready, t + 1)
                wait(dve, y_stored[par_], of_parity(t, par_, 16))
                for h in range(2):
                    dve.wait_ge(pv_filled, t * PAIRS + (h + 1) * HB)
                    scale = flat(rden)[:, h * HH:(h + 1) * HH].unsqueeze(2).to_broadcast([P, HH, HD])
                    nc.vector.tensor_tensor(y[par_][:, h * HALF:(h + 1) * HALF].rearrange("p (i d) -> p i d", d=HD),
                                            po[h][:, :].rearrange("p (i d) -> p i d", d=HD), scale, ALU.mult).then_inc(o_ready, 1)
                if kind == 1:
                    dve.wait_ge(attended_loaded, 16)
                for h in range(2):
                    cols = slice(h * HALF, (h + 1) * HALF)
                    dve.wait_ge(o_ready, t * 2 + (h + 1))
                    nc.vector.scalar_tensor_tensor(out=y[par_][:, cols], in0=(x if kind == 1 else y[par_])[:, cols], scalar=0.5,
                                                   in1=gate[par_][:, cols], op0=ALU.mult, op1=ALU.mult).then_inc(y_ready, 1)

            def prompt_step(t, par_):
                first = isinstance(t, int) and t == 0
                lo = P if first else 0
                for i in range(PAIRS):
                    n_turned = turned(t, f"p{i - 2}") if i >= 2 else (0 if first else turned(t - 1, f"p{PAIRS - 2 + i}"))
                    dve.wait_ge(s_filled, t * PAIRS + (i + 1))
                    wait(dve, turn_filled, n_turned)
                    for c in range(2):
                        nc.vector.scalar_tensor_tensor(out=s[i % 2][:, c, lo:], in0=near[:, lo:], scalar=SLOPES[head_of(i, c)],
                                                       in1=ps[i % 2][:, c * 2 * P + lo:(c + 1) * 2 * P], op0=ALU.mult,
                                                       op1=ALU.add).then_inc(s_ready, 1)
                    maximum(t, i, s[i % 2][:, :, lo:], 0)
                    if i == HB:
                        make_gate(t + 1, 1 - par_, 0)
                make_gate(t + 1, 1 - par_, 1)
                finish(t, par_, 0)

            def sample_step(t, par_):
                for b in range(DEC):
                    dve.wait_ge(s_filled, t * PAIRS + b + 1)
                    dve.wait_ge(turn_filled, turned(t, f"pn{b - 2}") if b >= 2 else turned(t - 1, f"p{PAIRS - 2 + b}"))
                    both = lambda a: a[:, 0:2 * KEYS].rearrange("p (c k) -> p c k", k=KEYS)
                    nc.vector.tensor_tensor(both(lined(s[b % 2])), both(ps[b % 2]),
                                            sample_bias[:, b % 2, :].unsqueeze(1).to_broadcast([P, 2, KEYS]), ALU.add).then_inc(s_ready, 2)
                    maximum(t, b, both(lined(s[b % 2])), 1)
                finish(t, par_, 1)

            dve.wait_ge(const_loaded, 16 * (3 + PAIRS))
            for kind in range(2):
                nc.vector.tensor_scalar(flat(neg_sink[kind]), flat(sink[kind]), -1.0, 0.0, ALU.mult, ALU.add).then_inc(neg_ready, 1)
            dve.wait_ge(neg_ready, 2)
            for h in range(2):
                make_gate(0, 0, h)
            tiles(dve, T, lambda t, par_: sample_step(t, par_) if is_sample(t, T) else prompt_step(t, par_))


INS = ["x_prompt", "x_sample", "p_prompt", "p_sample", "state_a_shift", "state_a_wkv", "cache_k", "cache_v",
       "a_mu", "a_w_in", "a_w0", "a_w_w1", "a_w_w2", "a_a0", "a_w_a1", "a_w_a2", "a_k_k", "a_k_a", "a_r_k",
       "a_gn_g", "a_gn_b", "a_w_out", "kv_ln_g", "kv_ln_b", "w_kv", "b_w_in", "b_sinks", "b_w_out",
       "ln_g", "ln_b", "ple_w_proj", "ple_w_gate"]


def outputs_of(seq):
    return [("y_prompt", (1, seq, D)), ("y_sample", (DEC, DSEQ, D)), ("prompt_shift", (1, 1, D)),
            ("prompt_wkv", (1, 1, NH, HD, HD)), ("prompt_k", (1, P, 4, HD)), ("prompt_v", (1, P, 4, HD)),
            ("sample_shift", (1, DEC, D)), ("sample_wkv", (1, DEC, NH, HD, HD)),
            ("sample_k", (DEC, DSEQ, 4, HD)), ("sample_v", (DEC, DSEQ, 4, HD))]


def scratch_of(n_rows):
    return [("factors", (n_rows, 4, NB, P)),
            ("tok_b", (n_rows, D)), ("tok_k", (n_rows, D)), ("tok_v", (n_rows, D)),
            ("gate_mul", (n_rows, D)), ("gate_add", (n_rows, D)), ("bonus", (n_rows, NH)),
            ("dec", (n_rows, NB, DEC)), ("mixed", (n_rows, D)), ("x1", (n_rows, D)),
            ("kv", (n_rows, 2 * 4 * HD)), ("attended", (P, D)), ("gated", (n_rows, D))]


def build(nc, io, seq, phases):
    T = seq // P
    with ExitStack() as ctx:
        m = Masks(nc, ctx)
        for phase in phases:
            phase(nc, m, io, T)


PHASES = [phase_a1, phase_a2, phase_a3, phase_a3_sample, phase_out_a, phase_b, phase_out_b]


def kernel(**inputs):
    import numpy as _np
    import concourse.bacc as _bacc
    from concourse.bass_utils import run_bass_kernel_spmd as _run

    nc = _bacc.Bacc("TRN2", target_bir_lowering=False, num_devices=1)
    arrays, io = {}, {}
    for name in INS:
        a = _np.ascontiguousarray(inputs[name])
        arrays["in_" + name] = a
        io[name] = nc.dram_tensor("in_" + name, a.shape, mybir.dt.from_np(a.dtype), kind="ExternalInput").ap()
    for name, a in attention_constants().items():
        arrays["in_" + name] = a
        io[name] = nc.dram_tensor("in_" + name, a.shape, F32, kind="ExternalInput").ap()
    seq = inputs["x_prompt"].shape[1]
    outs = outputs_of(seq)
    for name, shape in outs:
        io[name] = nc.dram_tensor("out_" + name, shape, F32, kind="ExternalOutput").ap()
    for name, shape in scratch_of(seq + P):
        io[name] = nc.dram_tensor(name, shape, F32).ap()
    build(nc, io, seq, PHASES)
    r = _run(nc, [arrays], core_ids=[0])
    return tuple(r.results[0]["out_" + name] for name, _ in outs)
```
